# Optimizing a Trainium2 kernel written in Bass

```python
import jax, jax.numpy as jnp
from jax import lax
import numpy as np

D_MODEL = 1024
BATCH = 1
SEQ = 256
DEPTH = 2

GRID_W = 64
HEAD_DIM = 64
A_HEADS = 8
A_KV_HEADS = 2
B_HEADS = 8
B_KV_HEADS = 2
C_HEADS = D_MODEL // HEAD_DIM
Q_BLOCK = 128
WINDOW = 128
NA_KH = 8
NA_KW = 16
MEM_TOKENS = 256
MEM_HEADS = 4
MEM_HEAD_DIM = D_MODEL // MEM_HEADS
D_FF = 256 * ((8 * D_MODEL // 3 + 255) // 256)
ROPE_THETA = 10000.0
LN_EPS = 1e-5
RMS_EPS = 1e-6
ALPHA = (2.0 * DEPTH) ** 0.25
BETA = (8.0 * DEPTH) ** -0.25
N_EVEN = (DEPTH + 1) // 2
N_ODD = DEPTH // 2

A_Q = A_HEADS * HEAD_DIM
A_KV = A_KV_HEADS * HEAD_DIM
B_Q = B_HEADS * HEAD_DIM
B_KV = B_KV_HEADS * HEAD_DIM
AB_IN = A_Q + 2 * A_KV + B_Q + 2 * B_KV
AB_OUT = (A_HEADS + B_HEADS) * HEAD_DIM
AB_SPLITS = [A_Q, A_Q + A_KV, A_Q + 2 * A_KV, A_Q + 2 * A_KV + B_Q, A_Q + 2 * A_KV + B_Q + B_KV]
C_WIDTH = C_HEADS * HEAD_DIM


def layer_norm(x, g, b):
    xf = x.astype(jnp.float32)
    mu = xf.mean(-1, keepdims=True)
    var = jnp.square(xf - mu).mean(-1, keepdims=True)
    return ((xf - mu) * lax.rsqrt(var + LN_EPS) * g.astype(jnp.float32) + b.astype(jnp.float32)).astype(x.dtype)

def rms_norm(x, g):
    xf = x.astype(jnp.float32)
    return (xf * lax.rsqrt(jnp.mean(xf * xf, -1, keepdims=True) + RMS_EPS) * g.astype(jnp.float32)).astype(x.dtype)

def swiglu(x, w_gate, w_up, w_down):
    return (jax.nn.silu(x @ w_gate) * (x @ w_up)) @ w_down

def rope_angles(pos, dim):
    inv = ROPE_THETA ** (-jnp.arange(0, dim, 2, dtype=jnp.float32) / dim)
    return pos[:, None] * inv[None, :]

def apply_rope(x, ang):
    half = x.shape[-1] // 2
    cos = jnp.cos(ang)[None, :, None, :].astype(x.dtype)
    sin = jnp.sin(ang)[None, :, None, :].astype(x.dtype)
    x1, x2 = x[..., :half], x[..., half:]
    return jnp.concatenate([x1 * cos - x2 * sin, x2 * cos + x1 * sin], axis=-1)

def global_gqa(q, k, v):
    B, S, H, d = q.shape
    Hkv = k.shape[2]
    G = H // Hkv
    nb = S // Q_BLOCK
    scale = d ** -0.5
    qb = q.reshape(B, nb, Q_BLOCK, Hkv, G, d).transpose(1, 0, 2, 3, 4, 5)

    def one_block(q_blk):
        s = jnp.einsum('bqkgd,bskd->bkgqs', q_blk, k).astype(jnp.float32) * scale
        p = jax.nn.softmax(s, axis=-1).astype(v.dtype)
        return jnp.einsum('bkgqs,bskd->bqkgd', p, v)

    o = lax.map(one_block, qb)
    return o.transpose(1, 0, 2, 3, 4, 5).reshape(B, S, H * d)

def window_gqa_sink(q, k, v, sink):
    B, S, H, d = q.shape
    Hkv = k.shape[2]
    G = H // Hkv
    nb = S // Q_BLOCK
    scale = d ** -0.5
    qb = q.reshape(B, nb, Q_BLOCK, Hkv, G, d)
    pad = ((0, 0), (Q_BLOCK, Q_BLOCK), (0, 0), (0, 0))
    kp = jnp.pad(k, pad).reshape(B, nb + 2, Q_BLOCK, Hkv, d)
    vp = jnp.pad(v, pad).reshape(B, nb + 2, Q_BLOCK, Hkv, d)
    k_band = jnp.concatenate([kp[:, :-2], kp[:, 1:-1], kp[:, 2:]], axis=2)
    v_band = jnp.concatenate([vp[:, :-2], vp[:, 1:-1], vp[:, 2:]], axis=2)
    blk = jnp.arange(nb)[:, None] * Q_BLOCK
    qi = blk + jnp.arange(Q_BLOCK)[None, :]
    kj = blk - Q_BLOCK + jnp.arange(3 * Q_BLOCK)[None, :]
    rel = kj[:, None, :] - qi[:, :, None]
    valid = (jnp.abs(rel) <= WINDOW) & (kj[:, None, :] >= 0) & (kj[:, None, :] < S)
    s = jnp.einsum('bnqkgd,bnskd->bnkgqs', qb, k_band).astype(jnp.float32) * scale
    s = jnp.where(valid[None, :, None, None], s, -jnp.inf)
    sink_l = sink.astype(jnp.float32).reshape(Hkv, G)[None, None, :, :, None, None]
    m = jnp.maximum(s.max(-1, keepdims=True), sink_l)
    p = jnp.exp(s - m)
    p = (p / (p.sum(-1, keepdims=True) + jnp.exp(sink_l - m))).astype(v.dtype)
    o = jnp.einsum('bnkgqs,bnskd->bnqkgd', p, v_band)
    return o.reshape(B, S, H * d)

def mixer_ab(h, w_in, w_out, q_gain, k_gain, sink, ang_2d, ang_1d):
    B, S, _ = h.shape
    qa, ka, va, qb, kb, vb = jnp.split(h @ w_in, AB_SPLITS, axis=-1)
    qa = qa.reshape(B, S, A_HEADS, HEAD_DIM)
    ka = ka.reshape(B, S, A_KV_HEADS, HEAD_DIM)
    va = va.reshape(B, S, A_KV_HEADS, HEAD_DIM)
    qa = apply_rope(rms_norm(qa, q_gain), ang_2d)
    ka = apply_rope(rms_norm(ka, k_gain), ang_2d)
    out_a = global_gqa(qa, ka, va)
    qb = apply_rope(qb.reshape(B, S, B_HEADS, HEAD_DIM), ang_1d)
    kb = apply_rope(kb.reshape(B, S, B_KV_HEADS, HEAD_DIM), ang_1d)
    vb = vb.reshape(B, S, B_KV_HEADS, HEAD_DIM)
    out_b = window_gqa_sink(qb, kb, vb, sink)
    return jnp.concatenate([out_a, out_b], axis=-1) @ w_out

def mixer_c(h, w_in, w_out, rpb):
    B, S, _ = h.shape
    rows = S // GRID_W
    kh = min(NA_KH, rows)
    kw = NA_KW
    scale = HEAD_DIM ** -0.5
    q, k, v = jnp.split(h @ w_in, 3, axis=-1)
    qg = q.reshape(B, rows, GRID_W, C_HEADS, HEAD_DIM)
    kg = k.reshape(B, rows, GRID_W, C_HEADS, HEAD_DIM)
    vg = v.reshape(B, rows, GRID_W, C_HEADS, HEAD_DIM)
    col = jnp.arange(GRID_W)
    col_start = jnp.clip(col - kw // 2, 0, GRID_W - kw)
    col_idx = col_start[:, None] + jnp.arange(kw)[None, :]
    dc = col_idx - col[:, None]

    def row_block(r):
        rs = jnp.clip(r - kh // 2, 0, rows - kh)
        k_rows = lax.dynamic_slice_in_dim(kg, rs, kh, axis=1)
        v_rows = lax.dynamic_slice_in_dim(vg, rs, kh, axis=1)
        k_nb = jnp.take(k_rows, col_idx, axis=2)
        v_nb = jnp.take(v_rows, col_idx, axis=2)
        q_r = lax.dynamic_index_in_dim(qg, r, axis=1, keepdims=False)
        dr = rs + jnp.arange(kh) - r
        bias = rpb[:, dr[None, :, None] + NA_KH - 1, dc[:, None, :] + NA_KW - 1]
        s = jnp.einsum('bwhd,bawjhd->bhwaj', q_r, k_nb).astype(jnp.float32) * scale
        s = s + bias.astype(jnp.float32)[None]
        p = jax.nn.softmax(s.reshape(B, C_HEADS, GRID_W, kh * kw), axis=-1)
        p = p.reshape(B, C_HEADS, GRID_W, kh, kw).astype(v.dtype)
        return jnp.einsum('bhwaj,bawjhd->bwhd', p, v_nb)

    o = lax.map(row_block, jnp.arange(rows))
    o = o.transpose(1, 0, 2, 3, 4).reshape(B, S, C_WIDTH)
    return o @ w_out

def memory_attn(h, mem, w_q, w_kv, w_o):
    B, S, _ = h.shape
    M = mem.shape[1]
    q = (h @ w_q).reshape(B, S, MEM_HEADS, MEM_HEAD_DIM)
    k, v = jnp.split(mem @ w_kv, 2, axis=-1)
    k = k.reshape(B, M, MEM_HEADS, MEM_HEAD_DIM)
    v = v.reshape(B, M, MEM_HEADS, MEM_HEAD_DIM)
    s = jnp.einsum('bshd,bmhd->bhsm', q, k).astype(jnp.float32) * (MEM_HEAD_DIM ** -0.5)
    p = jax.nn.softmax(s, axis=-1).astype(v.dtype)
    o = jnp.einsum('bhsm,bmhd->bshd', p, v).reshape(B, S, D_MODEL)
    return o @ w_o

def first_inputs(seed: int = 0) -> dict:
    key = jax.random.key(seed)
    ks = jax.random.split(key, 20)
    nrm = jax.random.normal
    f32 = jnp.float32
    d_sc = D_MODEL ** -0.5
    return {
        "x": nrm(ks[0], (BATCH, SEQ, D_MODEL), f32),
        "mem": nrm(ks[1], (BATCH, MEM_TOKENS, D_MODEL), f32),
        "ln_g": 1.0 + 0.02 * nrm(ks[2], (DEPTH, 4, D_MODEL), f32),
        "ln_b": 0.02 * nrm(ks[3], (DEPTH, 4, D_MODEL), f32),
        "ffn_w_gate": nrm(ks[4], (DEPTH, 2, D_MODEL, D_FF), f32) * d_sc,
        "ffn_w_up": nrm(ks[5], (DEPTH, 2, D_MODEL, D_FF), f32) * d_sc,
        "ffn_w_down": nrm(ks[6], (DEPTH, 2, D_FF, D_MODEL), f32) * (D_FF ** -0.5) * BETA,
        "ab_w_in": nrm(ks[7], (N_EVEN, D_MODEL, AB_IN), f32) * d_sc,
        "ab_w_out": nrm(ks[8], (N_EVEN, AB_OUT, D_MODEL), f32) * (AB_OUT ** -0.5) * BETA,
        "ab_q_gain": 1.0 + 0.02 * nrm(ks[9], (N_EVEN, HEAD_DIM), f32),
        "ab_k_gain": 1.0 + 0.02 * nrm(ks[10], (N_EVEN, HEAD_DIM), f32),
        "ab_sink": 0.5 * nrm(ks[11], (N_EVEN, B_HEADS), f32),
        "c_w_in": nrm(ks[12], (N_ODD, D_MODEL, 3 * C_WIDTH), f32) * d_sc,
        "c_w_out": nrm(ks[13], (N_ODD, C_WIDTH, D_MODEL), f32) * (C_WIDTH ** -0.5) * BETA,
        "c_rpb": 0.1 * nrm(ks[14], (N_ODD, C_HEADS, 2 * NA_KH - 1, 2 * NA_KW - 1), f32),
        "mem_w_q": nrm(ks[15], (DEPTH, D_MODEL, D_MODEL), f32) * d_sc,
        "mem_w_kv": nrm(ks[16], (DEPTH, D_MODEL, 2 * D_MODEL), f32) * d_sc,
        "mem_w_o": nrm(ks[17], (DEPTH, D_MODEL, D_MODEL), f32) * d_sc * BETA,
    }

def first_block(x, mem, ln_g, ln_b, ffn_w_gate, ffn_w_up, ffn_w_down,
              ab_w_in, ab_w_out, ab_q_gain, ab_k_gain, ab_sink,
              c_w_in, c_w_out, c_rpb, mem_w_q, mem_w_kv, mem_w_o):
    S = x.shape[1]
    t = jnp.arange(S)
    row = (t // GRID_W).astype(jnp.float32)
    colp = (t % GRID_W).astype(jnp.float32)
    ang_2d = jnp.concatenate([rope_angles(row, HEAD_DIM // 2), rope_angles(colp, HEAD_DIM // 2)], axis=-1)
    ang_1d = rope_angles(t.astype(jnp.float32), HEAD_DIM)
    for i in range(DEPTH):
        j = i // 2
        y = swiglu(x, ffn_w_gate[i, 0], ffn_w_up[i, 0], ffn_w_down[i, 0])
        x = layer_norm(ALPHA * x + 0.5 * y, ln_g[i, 0], ln_b[i, 0])
        if i % 2 == 0:
            y = mixer_ab(x, ab_w_in[j], ab_w_out[j], ab_q_gain[j], ab_k_gain[j], ab_sink[j], ang_2d, ang_1d)
        else:
            y = mixer_c(x, c_w_in[j], c_w_out[j], c_rpb[j])
        x = layer_norm(ALPHA * x + y, ln_g[i, 1], ln_b[i, 1])
        y = memory_attn(x, mem, mem_w_q[i], mem_w_kv[i], mem_w_o[i])
        x = layer_norm(ALPHA * x + y, ln_g[i, 2], ln_b[i, 2])
        y = swiglu(x, ffn_w_gate[i, 1], ffn_w_up[i, 1], ffn_w_down[i, 1])
        x = layer_norm(ALPHA * x + 0.5 * y, ln_g[i, 3], ln_b[i, 3])
    return x


DN_HEAD_DIM = 128
DN_HEADS = D_MODEL // (2 * DN_HEAD_DIM)
DN_WIDTH = DN_HEADS * DN_HEAD_DIM
DN_CONV = 5
DN_CHUNK = 64
HG_EXPAND = 128
HG_HEAD_DIM = 128
HG_HEADS = D_MODEL // (2 * HG_HEAD_DIM)
HG_KEY_WIDTH = HG_HEADS * HG_EXPAND
HG_VAL_WIDTH = HG_HEADS * HG_HEAD_DIM
HG_CHUNK = 32
D_FF_2 = 2816
FFN_CONV = 3
EPS = 1e-6

IN_SIZES = (3 * DN_WIDTH, DN_WIDTH, 2 * DN_HEADS, 2 * DN_HEADS,
            HG_KEY_WIDTH, HG_KEY_WIDTH, HG_KEY_WIDTH, HG_VAL_WIDTH, HG_VAL_WIDTH,
            D_MODEL, D_MODEL)
IN_COLS = 4 * DN_WIDTH + 4 * DN_HEADS + 3 * HG_KEY_WIDTH + 2 * HG_VAL_WIDTH + 2 * D_MODEL


def _split(x, sizes):
    idx = np.cumsum(np.array(sizes))[:-1].tolist()
    return jnp.split(x, idx, axis=-1)

def _rmsnorm(x, w):
    xf = x.astype(jnp.float32)
    y = xf * lax.rsqrt(jnp.mean(xf * xf, axis=-1, keepdims=True) + EPS)
    return (y * w.astype(jnp.float32)).astype(x.dtype)

def _gated_rmsnorm(o, z, w):
    y = o * lax.rsqrt(jnp.mean(o * o, axis=-1, keepdims=True) + EPS)
    return y * w.astype(jnp.float32) * jax.nn.silu(z)

def _l2norm(x):
    return x * lax.rsqrt(jnp.sum(x * x, axis=-1, keepdims=True) + EPS)

def _dwconv(x, w):
    return lax.conv_general_dilated(x, w[:, None, :].astype(x.dtype), window_strides=(1,),
                                    padding='SAME', dimension_numbers=('NWC', 'WIO', 'NWC'),
                                    feature_group_count=x.shape[-1])

def _to_heads(x, n):
    b, s, _ = x.shape
    return x.reshape(b, s, n, -1).transpose(0, 2, 1, 3)

def _gated_delta_rule(q, k, v, beta, g):
    b, h, s, dk = q.shape
    dv = v.shape[-1]
    c = DN_CHUNK
    n = s // c
    q = q.reshape(b, h, n, c, dk)
    k = k.reshape(b, h, n, c, dk)
    v = v.reshape(b, h, n, c, dv)
    beta = beta.reshape(b, h, n, c)
    gc = jnp.cumsum(g.reshape(b, h, n, c), axis=-1)
    incl = jnp.tril(jnp.ones((c, c), dtype=bool))
    strict = jnp.tril(jnp.ones((c, c), dtype=bool), k=-1)
    decay = jnp.exp(jnp.where(incl, gc[..., :, None] - gc[..., None, :], -jnp.inf))
    kb = k * beta[..., None]
    a = jnp.where(strict, jnp.einsum('bhntd,bhnsd->bhnts', kb, k) * decay, 0.0)
    eye = jnp.eye(c, dtype=q.dtype)
    t_inv = lax.linalg.triangular_solve(a + eye, jnp.broadcast_to(eye, a.shape),
                                        left_side=True, lower=True, unit_diagonal=True)
    u = jnp.einsum('bhnts,bhnsv->bhntv', t_inv, v * beta[..., None])
    w = jnp.einsum('bhnts,bhnsd->bhntd', t_inv, kb * jnp.exp(gc)[..., None])
    qk = jnp.einsum('bhntd,bhnsd->bhnts', q, k) * decay
    qg = q * jnp.exp(gc)[..., None]
    kd = k * jnp.exp(gc[..., -1:] - gc)[..., None]
    gl = jnp.exp(gc[..., -1])
    xs = (jnp.moveaxis(u, 2, 0), jnp.moveaxis(w, 2, 0), jnp.moveaxis(qk, 2, 0),
          jnp.moveaxis(qg, 2, 0), jnp.moveaxis(kd, 2, 0), jnp.moveaxis(gl, 2, 0))

    def step(state, inp):
        u_n, w_n, qk_n, qg_n, kd_n, gl_n = inp
        v_new = u_n - jnp.einsum('bhtd,bhdv->bhtv', w_n, state)
        o = jnp.einsum('bhtd,bhdv->bhtv', qg_n, state) + jnp.einsum('bhts,bhsv->bhtv', qk_n, v_new)
        state = state * gl_n[..., None, None] + jnp.einsum('bhsd,bhsv->bhdv', kd_n, v_new)
        return state, o

    state0 = jnp.zeros((b, h, dk, dv), dtype=q.dtype)
    _, o = lax.scan(step, state0, xs)
    return jnp.moveaxis(o, 0, 2).reshape(b, h, s, dv)

def _hgrn2_scan(q, k, i, logf):
    b, h, s, dk = q.shape
    dv = i.shape[-1]
    c = HG_CHUNK
    n = s // c
    q = jnp.moveaxis(q.reshape(b, h, n, c, dk), 2, 0)
    k = jnp.moveaxis(k.reshape(b, h, n, c, dk), 2, 0)
    i = jnp.moveaxis(i.reshape(b, h, n, c, dv), 2, 0)
    bc = jnp.moveaxis(jnp.cumsum(logf.reshape(b, h, n, c, dk), axis=-2), 2, 0)
    incl = jnp.tril(jnp.ones((c, c), dtype=bool))[:, :, None]

    def step(state, inp):
        q_n, k_n, i_n, b_n = inp
        dec = jnp.exp(jnp.where(incl, b_n[:, :, :, None, :] - b_n[:, :, None, :, :], -jnp.inf))
        att = jnp.einsum('bhtd,bhsd,bhtsd->bhts', q_n, k_n, dec)
        o = (jnp.einsum('bhtd,bhdv->bhtv', q_n * jnp.exp(b_n), state)
             + jnp.einsum('bhts,bhsv->bhtv', att, i_n))
        last = b_n[:, :, -1:, :]
        state = (state * jnp.exp(last[:, :, 0, :])[..., None]
                 + jnp.einsum('bhsd,bhsv->bhdv', k_n * jnp.exp(last - b_n), i_n))
        return state, o

    state0 = jnp.zeros((b, h, dk, dv), dtype=q.dtype)
    _, o = lax.scan(step, state0, (q, k, i, bc))
    return jnp.moveaxis(o, 0, 2).reshape(b, h, s, dv)

def _flip(t):
    return jnp.flip(t, axis=2)

def _mixer(h, w_in, dn_conv, dn_a_log, dn_dt_bias, dn_norm, lb, hg_norm, w_branch_dn, w_branch_hg, w_out):
    b, s, _ = h.shape
    f32 = jnp.float32
    p = h @ w_in
    (qkv, z, beta_r, a_r, hq, hf_fwd, hf_bwd, hi, hgate, gate_dn, gate_hg) = _split(p, IN_SIZES)

    qkv = jax.nn.silu(_dwconv(qkv, dn_conv)).astype(f32)
    q, k, v = _split(qkv, (DN_WIDTH, DN_WIDTH, DN_WIDTH))
    q = _l2norm(_to_heads(q, DN_HEADS)) * (DN_HEAD_DIM ** -0.5)
    k = _l2norm(_to_heads(k, DN_HEADS))
    v = _to_heads(v, DN_HEADS)
    beta = jax.nn.sigmoid(beta_r.astype(f32)).reshape(b, s, 2, DN_HEADS).transpose(2, 0, 3, 1)
    g = (-jnp.exp(dn_a_log.astype(f32))
         * jax.nn.softplus(a_r.astype(f32).reshape(b, s, 2, DN_HEADS) + dn_dt_bias.astype(f32)))
    g = g.transpose(2, 0, 3, 1)
    o_f = _gated_delta_rule(q, k, v, beta[0], g[0])
    o_b = _flip(_gated_delta_rule(_flip(q), _flip(k), _flip(v), _flip(beta[1]), _flip(g[1])))
    o_dn = (o_f + o_b).transpose(0, 2, 1, 3)
    o_dn = _gated_rmsnorm(o_dn, z.astype(f32).reshape(b, s, DN_HEADS, DN_HEAD_DIM), dn_norm)
    o_dn = o_dn.reshape(b, s, DN_WIDTH).astype(h.dtype)

    lb = lb.astype(f32)
    qh = _to_heads(jax.nn.silu(hq.astype(f32)), HG_HEADS) * (HG_EXPAND ** -0.5)
    ih = _to_heads(hi.astype(f32), HG_HEADS)
    outs = []
    for d, fr in enumerate((hf_fwd, hf_bwd)):
        fr = fr.astype(f32)
        logf = jax.nn.log_sigmoid(fr) + jnp.log1p(lb[d] * jnp.exp(-fr))
        kk = (1.0 - lb[d]) * jax.nn.sigmoid(-fr)
        outs.append((_to_heads(kk, HG_HEADS), _to_heads(logf, HG_HEADS)))
    o_hf = _hgrn2_scan(qh, outs[0][0], ih, outs[0][1])
    o_hb = _flip(_hgrn2_scan(_flip(qh), _flip(outs[1][0]), _flip(ih), _flip(outs[1][1])))
    o_hg = (o_hf + o_hb).transpose(0, 2, 1, 3)
    o_hg = _gated_rmsnorm(o_hg, hgate.astype(f32).reshape(b, s, HG_HEADS, HG_HEAD_DIM), hg_norm)
    o_hg = o_hg.reshape(b, s, HG_VAL_WIDTH).astype(h.dtype)

    merged = (jax.nn.sigmoid(gate_dn) * (o_dn @ w_branch_dn)
              + jax.nn.sigmoid(gate_hg) * (o_hg @ w_branch_hg))
    return merged @ w_out

def _conv_ffn(h, w_up, ffn_conv, ffn_conv_bias, w_down):
    gate, up = _split(h @ w_up, (D_FF_2, D_FF_2))
    gate = _dwconv(gate, ffn_conv) + ffn_conv_bias
    return (jax.nn.silu(gate) * up) @ w_down

def _log(v):
    return float(np.log(v))

def second_inputs(seed: int = 0) -> dict:
    key = jax.random.key(seed)
    ks = jax.random.split(key, 20)
    f32 = jnp.float32
    nrm = lambda k, shape, scale: jax.random.normal(k, shape, f32) * scale
    dt = jnp.exp(jax.random.uniform(ks[5], (DEPTH, 2, DN_HEADS), f32)
                 * (_log(0.1) - _log(0.001)) + _log(0.001))
    return {
        'x': nrm(ks[0], (BATCH, SEQ, D_MODEL), 1.0),
        'mix_norm': 1.0 + nrm(ks[1], (DEPTH, D_MODEL), 0.02),
        'w_in': nrm(ks[2], (DEPTH, D_MODEL, IN_COLS), D_MODEL ** -0.5),
        'dn_conv': nrm(ks[3], (DEPTH, DN_CONV, 3 * DN_WIDTH), DN_CONV ** -0.5),
        'dn_a_log': jnp.log(jax.random.uniform(ks[4], (DEPTH, 2, DN_HEADS), f32, 1.0, 16.0)),
        'dn_dt_bias': dt + jnp.log(-jnp.expm1(-dt)),
        'dn_norm': 1.0 + nrm(ks[6], (DEPTH, DN_HEAD_DIM), 0.02),
        'hg_lb_logits': nrm(ks[7], (DEPTH, 2, HG_KEY_WIDTH), 1.0),
        'hg_norm': 1.0 + nrm(ks[8], (DEPTH, HG_HEAD_DIM), 0.02),
        'w_branch_dn': nrm(ks[9], (DEPTH, DN_WIDTH, D_MODEL), DN_WIDTH ** -0.5),
        'w_branch_hg': nrm(ks[10], (DEPTH, HG_VAL_WIDTH, D_MODEL), HG_VAL_WIDTH ** -0.5),
        'w_out': nrm(ks[11], (DEPTH, D_MODEL, D_MODEL), D_MODEL ** -0.5),
        'ffn_norm': 1.0 + nrm(ks[12], (DEPTH, D_MODEL), 0.02),
        'w_up': nrm(ks[13], (DEPTH, D_MODEL, 2 * D_FF_2), D_MODEL ** -0.5),
        'ffn_conv': nrm(ks[14], (DEPTH, FFN_CONV, D_FF_2), FFN_CONV ** -0.5),
        'ffn_conv_bias': nrm(ks[15], (DEPTH, D_FF_2), 0.02),
        'w_down': nrm(ks[16], (DEPTH, D_FF_2, D_MODEL), D_FF_2 ** -0.5),
        'final_norm': 1.0 + nrm(ks[17], (D_MODEL,), 0.02),
    }

def second_block(x, mix_norm, w_in, dn_conv, dn_a_log, dn_dt_bias, dn_norm, hg_lb_logits, hg_norm,
              w_branch_dn, w_branch_hg, w_out, ffn_norm, w_up, ffn_conv, ffn_conv_bias, w_down, final_norm):
    sm = jax.nn.softmax(hg_lb_logits.astype(jnp.float32), axis=0)
    lb_all = jnp.clip(jnp.cumsum(sm, axis=0) - sm[0:1], 0.0, 1.0)
    for l in range(DEPTH):
        h = _rmsnorm(x, mix_norm[l])
        x = x + _mixer(h, w_in[l], dn_conv[l], dn_a_log[l], dn_dt_bias[l], dn_norm[l], lb_all[l],
                       hg_norm[l], w_branch_dn[l], w_branch_hg[l], w_out[l])
        h = _rmsnorm(x, ffn_norm[l])
        x = x + _conv_ffn(h, w_up[l], ffn_conv[l], ffn_conv_bias[l], w_down[l])
    return _rmsnorm(x, final_norm)


def setup_inputs(seed=0):
    out = dict(first_inputs(seed))
    for name, value in second_inputs(seed + 1).items():
        if name != "x":
            out[name + "_2"] = value
    return out


def reference(
    x, mem, ln_g, ln_b, ffn_w_gate, ffn_w_up, ffn_w_down, ab_w_in, ab_w_out, ab_q_gain,
    ab_k_gain, ab_sink, c_w_in, c_w_out, c_rpb, mem_w_q, mem_w_kv, mem_w_o, mix_norm_2, w_in_2,
    dn_conv_2, dn_a_log_2, dn_dt_bias_2, dn_norm_2, hg_lb_logits_2, hg_norm_2, w_branch_dn_2,
    w_branch_hg_2, w_out_2, ffn_norm_2, w_up_2, ffn_conv_2, ffn_conv_bias_2, w_down_2,
    final_norm_2,
):
    x = first_block(
        x, mem, ln_g, ln_b, ffn_w_gate, ffn_w_up, ffn_w_down, ab_w_in, ab_w_out, ab_q_gain,
        ab_k_gain, ab_sink, c_w_in, c_w_out, c_rpb, mem_w_q, mem_w_kv, mem_w_o,
    )
    return second_block(
        x, mix_norm_2, w_in_2, dn_conv_2, dn_a_log_2, dn_dt_bias_2, dn_norm_2, hg_lb_logits_2,
        hg_norm_2, w_branch_dn_2, w_branch_hg_2, w_out_2, ffn_norm_2, w_up_2, ffn_conv_2,
        ffn_conv_bias_2, w_down_2, final_norm_2,
    )


_drawn_inputs = setup_inputs


def setup_inputs(seed=0):
    import zlib

    import numpy as np

    out = dict(_drawn_inputs(seed))
    spreads = {}
    factors = {'ab_q_gain': 8.0,
     'ab_k_gain': 8.0,
     'ab_sink': 23.63,
     'c_rpb': 6.111,
     'mix_norm_2': 2.766,
     'dn_norm_2': 5.925,
     'hg_lb_logits_2': 8.199,
     'hg_norm_2': 6.176,
     'ffn_norm_2': 7.505,
     'ffn_conv_bias_2': 11.401,
     'final_norm_2': 22.927}
    for name, (base, spread) in spreads.items():
        noise = np.random.default_rng([zlib.crc32(name.encode()), seed]).standard_normal(out[name].shape)
        drawn = base * np.exp(spread * noise) if base else spread * noise
        out[name] = __import__('jax').numpy.asarray(drawn.astype(out[name].dtype))
    for name, factor in factors.items():
        out[name] = (out[name] * factor).astype(out[name].dtype)
    return out
```

```python
from contextlib import ExitStack

import numpy as np

import concourse.bass as bass
from concourse import mybir

F32 = mybir.dt.float32
F32R = mybir.dt.float32r
U8 = mybir.dt.uint8
ALU = mybir.AluOpType
ACT = mybir.ActivationFunctionType
AX_X = mybir.AxisListType.X

P = 128
S = 256
D = 1024
KT = D // P
TT = S // P
FF = 2816
FT = FF // P
UW = 2048
RING = 3
NB = 4
HD = 64
DEPTH = 2
ALPHA = (2.0 * DEPTH) ** 0.25
LN_EPS = 1e-5
EPS = 1e-6
NEG = -1.0e30
GRID = 64
NA_KH, NA_KW = 8, 16
WINDOW = 128
NHEADS = 16
FU = 33
DN_H = 4
LEVELS = 7



class Plan:

    def __init__(self):
        self.unit = {}
        self.tile = {}
        self.units = 0
        self.tiles = 0
        self.freed = []
        self.splits = 0
        self.ready = []
        self.plain = 0
        self.stages()

    def from_units(self, name, n, per=1):
        self.unit[name] = self.units
        self.tile[name] = self.tiles
        for i in range(n):
            self.units += 1
            self.freed.append(("unit_used", self.units))
            for _ in range(per):
                self.ready.append(("unit_used", self.units))
                self.tiles += 1

    def from_chip(self, name, n):
        self.tile[name] = self.tiles
        for _ in range(n):
            self.plain += 1
            self.ready.append(("tile_ready", self.plain))
            self.tiles += 1

    def to_acc(self, name, n):
        self.unit[name] = self.units
        for _ in range(n):
            self.units += 1
            self.freed.append(("unit_used", self.units))

    def ffn(self, name):
        self.unit[name] = self.units
        self.tile[name] = self.tiles
        order = "GG" + "GGD" * (FT // 2 - 1) + "D"
        for c in order:
            self.units += 1
            self.splits += 1
            self.freed.append(("w_lo", self.splits))
            if c == "G":
                self.ready.append(("unit_used", self.units))
                self.tiles += 1

    def attention(self, name, groups, per):
        for g in range(groups + 3):
            if g < groups:
                self.from_chip((name, "S", g), per)
            if 2 <= g < groups + 2:
                self.from_chip((name, "T", g - 2), per)
            if g >= 3:
                self.from_chip((name, "O", g - 3), 1)

    def stages(self):
        self.from_chip("x", 4)
        self.from_chip("mem", 4)
        for i in range(DEPTH):
            self.ffn(("ffn", 2 * i))
            self.from_chip(("ln", 4 * i), 4)
            if i == 0:
                self.from_units("ab_in", 6)
                self.from_units(("kv", 0), 8)
                self.from_chip("ab_T", 6)
                self.attention(("att", 0), 8, 2)
            else:
                self.from_units("c_in", 12)
                self.from_units(("kv", 1), 8)
                self.attention(("att", 2), 8, 2)
            self.to_acc(("out", 2 * i), 4)
            self.from_chip(("ln", 4 * i + 1), 4)
            self.from_units(("mq", i), 4)
            self.attention(("att", 2 * i + 1), 4, 1)
            self.to_acc(("out", 2 * i + 1), 4)
            self.from_chip(("ln", 4 * i + 2), 4)
            self.ffn(("ffn", 2 * i + 1))
            self.from_chip(("ln", 4 * i + 3), 4)

        for l in range(DEPTH):
            self.from_chip(("rms", 2 * l), 4)
            self.from_units(("hq", l), 2)
            self.from_units(("hf", l), 4)
            self.from_units(("hi", l), 2)
            self.from_units(("hz", l), 2)
            self.from_units(("qkv", l), 6)
            self.from_chip(("ba", l), 1)
            self.from_units(("z", l), 2)
            for i in range(LEVELS + 2):
                if i < 8:
                    self.from_units(("gate", l, i), 1)
                self.from_chip(("level", l, i), 2)
            self.from_chip(("hg_o", l), 2)
            self.from_chip(("l2", l), 4)
            self.from_chip(("hg_T", l), 2)
            self.from_chip(("kv_T", l), 4)
            self.from_chip(("gcum", l), 1)
            self.from_chip(("gcB", l), 4)
            self.from_chip(("G", l), 2)
            self.from_chip(("QK", l), 2)
            self.from_chip(("A0", l), 4)
            for v in range(1, LEVELS):
                self.from_chip(("Y", l, v), 4)
                self.from_chip(("Z", l, v), 8 if v < LEVELS - 1 else 4)
            for name in ("vnA", "S", "kS", "vnB", "qS", "dn_o", "dn_T"):
                self.from_chip((name, l), 2)
            self.from_units(("branch_dn", l), 2, per=2)
            self.from_units(("branch_hg", l), 2, per=2)
            self.to_acc(("out", 4 + l), 4)
            self.from_chip(("rms", 2 * l + 1), 4)
            self.ffn(("ffn", 4 + l))



def scores_per_attention(a):
    return 16 if a % 2 == 0 else 4


def first_score(a):
    return sum(scores_per_attention(b) for b in range(a))



def pack_columns(w):
    c = w.shape[1] // 256
    return w.reshape(KT, P, c, 256).transpose(2, 1, 0, 3).reshape(c, P, UW)


def pack_rows(w):
    n = w.shape[0] // 256
    return w.reshape(n, 2, P, D).transpose(0, 2, 1, 3).reshape(n, P, UW)


def pack_ffn(gate, up, down):
    g = gate.reshape(KT, P, FT, P).transpose(2, 1, 0, 3)
    u = up.reshape(KT, P, FT, P).transpose(2, 1, 0, 3)
    gu = np.concatenate([g, u], axis=3).reshape(FT, P, UW)
    d = pack_rows(down)
    out = [gu[0:2]]
    for j in range(FT // 2 - 1):
        out += [gu[2 * j + 2:2 * j + 4], d[j:j + 1]]
    out.append(d[FT // 2 - 1:])
    return out


def pack_branch(w):
    return w.reshape(4, P, 2, 512).transpose(2, 1, 0, 3).reshape(2, P, UW)


def weight_stream(a):
    out = []
    for i in range(DEPTH):
        out += pack_ffn(a["ffn_w_gate"][i, 0], a["ffn_w_up"][i, 0], a["ffn_w_down"][i, 0])
        out.append(pack_columns((a["ab_w_in"] if i == 0 else a["c_w_in"])[0]))
        out.append(pack_columns(a["mem_w_kv"][i]))
        out.append(pack_rows((a["ab_w_out"] if i == 0 else a["c_w_out"])[0]))
        out.append(pack_columns(a["mem_w_q"][i]))
        out.append(pack_rows(a["mem_w_o"][i]))
        out += pack_ffn(a["ffn_w_gate"][i, 1], a["ffn_w_up"][i, 1], a["ffn_w_down"][i, 1])

    for l in range(DEPTH):
        w = a["w_in_2"][l]
        out.append(pack_columns(w[:, 2064:4624]))
        out.append(pack_columns(w[:, 0:2048]))
        out.append(pack_columns(w[:, 4624:6672]))
        out.append(pack_branch(a["w_branch_dn_2"][l]))
        out.append(pack_branch(a["w_branch_hg_2"][l]))
        out.append(pack_rows(a["w_out_2"][l]))
        up = a["w_up_2"][l]
        out += pack_ffn(up[:, :FF], up[:, FF:], a["w_down_2"][l])

    return np.concatenate(out, axis=0)


def columns(v):
    n, w = v.shape
    return v.reshape(n, w // P, P).transpose(2, 0, 1).reshape(P, -1)


def level_mask(l):
    t = np.arange(P)[:, None]
    s = np.arange(P)[None, :]
    return ((t >> (l + 1)) == (s >> (l + 1))) & ((t >> l) % 2 == 1) & ((s >> l) % 2 == 0)


def constants():
    i = np.arange(P)
    out = {"ident": np.eye(P), "ones": np.ones((P, P)),
           "le": (i[:, None] <= i[None, :]) * 1.0, "ge": (i[:, None] >= i[None, :]) * 1.0}
    q = np.arange(S).reshape(TT, P).transpose(1, 0)[:, :, None]
    s = np.arange(S)[None, None, :]
    out["window"] = np.where(np.abs(s - q) <= WINDOW, 0.0, NEG).reshape(P, -1)
    c = (i % GRID)[:, None]
    start = np.clip(c - NA_KW // 2, 0, GRID - NA_KW)
    cc = np.arange(GRID)[None, ::-1]
    out["grid"] = np.where((cc >= start) & (cc < start + NA_KW), 0.0, NEG)
    t = np.arange(S)
    inv2 = 10000.0 ** (-np.arange(0, 32, 2, dtype=np.float32) / 32)
    inv1 = 10000.0 ** (-np.arange(0, 64, 2, dtype=np.float32) / 64)
    f = np.float32
    ang2 = np.concatenate([(t // GRID).astype(f)[:, None] * inv2.astype(f),
                           (t % GRID).astype(f)[:, None] * inv2.astype(f)], axis=1)
    ang1 = t.astype(f)[:, None] * inv1.astype(f)
    rope = np.stack([np.stack([np.cos(x), np.cos(x), -np.sin(x), np.sin(x)], 1) for x in (ang2, ang1)], 1)
    out["rope"] = rope.reshape(TT, P, 2 * 4 * 32).transpose(1, 0, 2).reshape(P, -1)
    return {k: np.ascontiguousarray(v, dtype=np.float32) for k, v in out.items()}


def offsets(parts):
    at, out = 0, {}
    for name, v in parts.items():
        out[name] = (at, v.shape[1])
        at += v.shape[1]
    return out, at


def hg_masks():
    m = [level_mask(l) | level_mask(l).T for l in range(LEVELS)] + [np.eye(P, dtype=bool)]
    m += [level_mask(l) for l in range(LEVELS)] + [level_mask(l).T for l in range(LEVELS)]
    return np.concatenate(m, axis=1).astype(np.float32)


CONSTANTS, CONSTANTS_W = offsets(constants())



class Progress:

    def __init__(self, eng, sem):
        self.eng, self.sem, self.n = eng, sem, 0

    def did(self, ins):
        ins.then_inc(self.sem, 1)
        self.n += 1

    def sync(self):
        self.eng.wait_ge(self.sem, self.n)

    def link(self, ins):
        self.did(ins)
        self.sync()


def build(nc, weights, x_in, mem_in, consts, cols, ln_g_rows, ln_b_rows, gains, sink, rpb, hmask_in, wba_in, head_rows, decay_rows, final_norm,
          out):
    plan = Plan()
    with ExitStack() as ctx:
        def sb(name, shape, dt=F32):
            return ctx.enter_context(nc.sbuf_tensor(name, shape, dt))

        ring = sb("ring", [P, RING, UW])
        x = sb("x", [P, TT, D])
        xT = sb("xT", [P, KT, S])
        xT_hi = sb("xT_hi", [P, KT, S], F32R)
        xT_lo = sb("xT_lo", [P, KT, S], F32R)
        hidden = sb("hidden", [P, 4, S])
        hidden_hi = sb("hidden_hi", [P, 4, S], F32R)
        hidden_lo = sb("hidden_lo", [P, 4, S], F32R)
        silu_gate = sb("silu_gate", [P, 4, S])
        const = sb("const", [P, CONSTANTS_W])
        WORK = 29696
        WORK_AT = nc.sbuf_base
        work = sb("work", [P, WORK])
        col = sb("col", [P, cols.shape[1]])
        bn = sb("bn", [P, 4, 6])
        mv = sb("mv", [P, TT, 2])
        var = sb("var", [P, TT])
        std = sb("std", [P, TT])
        rstd = sb("rstd", [P, TT])
        gain = sb("gain", [P, 2 * HD])
        sink_b = sb("sink_b", [P, 8])
        ssq = sb("ssq", [P, TT, 10])
        srt = sb("srt", [P, TT, 10])
        mx = sb("mx", [P, 16, TT])
        nmx = sb("nmx", [P, 16, TT])
        psum_p = sb("psum_p", [P, 16, TT])
        sink_e = sb("sink_e", [P, 16, TT])
        rec = sb("rec", [P, 16, TT])

        hmask = sb("hmask", [P, (LEVELS + 1) * P], U8)
        levels = sb("levels", [P, 2 * LEVELS * P], mybir.dt.bfloat16)
        wba = sb("wba", [P, DEPTH, KT, 16])
        arow = sb("arow", [P, DEPTH, 2, 8])
        lb = sb("lb", [P, 2, 8])
        omlb = sb("omlb", [P, 2, 8])
        small = sb("small", [P, 14, 16])
        btot_t = sb("btot_t", [P, 4])


        def split_slot(name, at):
            return nc.alloc_sbuf_tensor_at(name, [P, UW], F32R, offset=WORK_AT + 4 * at)

        w_hi = [split_slot(f"w_hi{i}", at) for i, at in enumerate((4096, 8192, 10240))]
        w_lo = [split_slot(f"w_lo{i}", at) for i, at in enumerate((12288, 14336, 16384))]

        def region(at, *shape):
            n = int(np.prod(shape))
            v = work[:, at:at + n]
            if len(shape) == 2:
                v = v.rearrange("p (a b) -> p a b", a=shape[0])
            if len(shape) == 3:
                v = v.rearrange("p (a b c) -> p a b c", a=shape[0], b=shape[1])
            return v

        def table(name):
            a, n = CONSTANTS[name]
            return const[:, a:a + n]

        ident = table("ident")
        xh = region(0, TT, D)
        qT = region(0, 8, S)
        kT = region(2048, 8, S)
        v_tok = region(4096, TT, D)
        memT = region(6144, KT, S)
        mkT = region(8192, KT, S)
        mv_tok = region(10240, TT, D)
        prob = region(12288, 6, TT, S)
        probT = region(15360, 4, TT, S)
        score = region(17408, 4, TT, S)
        oT = region(19456, KT, S)
        g_rows = region(21504, D)
        b_rows = region(22528, D)
        raw = region(23552, TT, 1536)
        roped = region(26624, TT, 2 * 768)
        rtmp = region(12288, 4, 2, 640)
        grid_bias = region(23552, NHEADS, 6, GRID)

        acc = [ctx.enter_context(nc.psum_tensor(f"acc{b}", [P, 512], F32)) for b in range(4)]
        bank = [ctx.enter_context(nc.psum_tensor(f"tile{b}", [P, 512], F32)) for b in range(NB)]

        names = ["const_in", "x_in", "mem_in", "unit_used", "tile_ready", "acc_ready",
                 "act_step", "dve_step", "pool_step", "out_stored",
                 "gate_silu", "bias_ready", "w_hi", "w_lo", "x_hi", "x_lo", "hidden_high", "hidden_split",
                 "ln_var", "ln_std", "ln_xh", "x_updated", "rows_in", "cols_in", "rpb_in",
                 "ab_raw", "ab_sqrt", "ab_ssq", "ab_roped",
                 "score_max", "prob_exp", "prob_norm"]

        names += ["head_in", "gains_in", "masks_in", "lb_arg", "lb_exp", "qkv_conv", "qkv_silu", "conv_done", "conv_step", "final_rows", "final_in",
                  "hg_num", "hg_log", "hg_arg", "hg_exp", "hg_k", "hg_q", "hg_ssq", "hg_std", "hg_out",
                  "l2_sq", "l2_arg", "l2_sqrt", "l2_done",
                  "ba_y", "ba_sp", "g_ready", "gc_arg", "gc_exp", "dec_arg", "dec", "dec_masked",
                  "a_ready", "a_level", "x_first", "vb", "kd", "nbe",
                  "z_ready", "dn_ssq", "dn_std", "dn_out", "gates_ready", "merged_dn", "merged"]
        hq = region(2048, 4, S)
        hk = region(3072, 2, 4, S)
        hF = region(5120, 2, 4, S)
        hE = region(7168, 2, 2, 4 * S)
        hKQ = region(11264, 2, 2, 4 * S)
        hatt = region(15360, TT, 4, S)
        hi = region(17408, TT, 512)
        dec = region(2048, 4, 512)
        amat = region(4096, 4, 512)
        qkd = region(6144, 4, 512)
        xinv = region(8192, 4, 512)
        winv = region(10240, 4, 512)
        yinv = region(12288, 4, 512)
        alev = region(14336, 4, 512)
        kd = region(16384, 2, 512)
        state = region(17408, 2, 512)
        vb, vn, qs, dn_o = dec, yinv, region(8192, 2, 512), region(4096, TT, 512)
        l2s = region(8192, 4, 512)
        l2r = region(12288, 4, 512)
        merged = region(18432, KT, S)
        mtmp = region(12288, KT, S)
        qkvT = region(18432, 12, S)
        v_tk = region(21504, TT, 512)
        k_tk = region(22528, TT, 512)
        gates = region(23552, 16, S)
        zs = region(27648, TT, 512)
        hz = region(28672, TT, 512)
        oT_hg = region(0, 4, S)
        oT_dn = region(1024, 4, S)
        conv = region(18432, 4, S)
        f_rows = region(21504, D)
        (eb, yb, ny, beta, gg, gc, eg, kdf, nbe, bss) = [small[:, i, :] for i in range(2, 12)]
        brs = small[:, 12, :]
        note = small[:, 13, :]
        ba32 = small[:, 0:2, :].rearrange("p a b -> p (a b)")
        btot = btot_t[:, :]

        head_norm = table("window").rearrange("p (l b d) -> p l b d", l=DEPTH, b=2)

        def heads2(v):
            return v.rearrange("p (h s) -> p h s", s=P)

        sems = {n: ctx.enter_context(nc.semaphore(n)) for n in names}
        slot_full = [ctx.enter_context(nc.semaphore(f"slot_full{s}")) for s in range(RING)]
        tile_taken = [ctx.enter_context(nc.semaphore(f"tile_taken{b}")) for b in range(NB)]

        def ready(t):
            name, value = plan.ready[t]
            return sems[name], value

        def taken(t):
            return tile_taken[t % NB], t // NB + 1

        def pair(buf, j):
            return buf[:, 2 * j:2 * j + 2, :].rearrange("p a b -> p (a b)")

        def tile_of_step(m):
            if m < 2:
                return m
            if m == FU - 1 or (m - 2) % 3 == 2:
                return None
            return 2 + 2 * ((m - 2) // 3) + (m - 2) % 3

        def run_steps(eng, do):
            for m in range(2):
                do(m)
            with eng.Fori(0, 4) as lap:
                for m in range(2, 8):
                    do(m, lap)
            for m in range(26, FU):
                do(m, split=m + RING < FU)

        block = ctx.enter_context(nc.Block())

        @block.sync
        def _(sp):
            for s in range(RING):
                sp.dma_start(ring[:, s, :], weights[s]).then_inc(slot_full[s], 16)
            u = RING
            while u < plan.units:
                name, value = plan.freed[u - RING]
                n = 1
                while u + n < plan.units and plan.freed[u + n - RING][0] == name:
                    n += 1

                def load(v, freed, more=0, address=None):
                    s = v % RING
                    sp.wait_ge(sems[name], more * RING + freed)
                    src = weights[v] if address is None else \
                        weights[bass.ds(address, 1)].rearrange("u p n -> p (u n)")
                    sp.dma_start(ring[:, s, :], src).then_inc(slot_full[s], 16)
                laps = n // RING if n >= 2 * RING else 0
                if laps:
                    with sp.Fori(0, laps) as lap:
                        for s in range(RING):
                            load(u + s, value + s, lap, lap * RING + (u + s))
                for k in range(laps * RING, n):
                    load(u + k, value + k)
                u += n
            sp.wait_ge(sems["out_stored"], 16)

        @block.tensor
        def _(pe):
            mm = nc.tensor.matmul

            def open_tile(t, more=0):
                if t >= NB:
                    pe.wait_ge(tile_taken[t % NB], more + t // NB)
                return bank[t % NB]

            def open_unit(u, more=0):
                pe.wait_ge(slot_full[u % RING], more * 16 + 16 * (u // RING + 1))
                return ring[:, u % RING, :]

            def features(u, t, src, more_u=0, more_t=0):
                w = open_unit(u, more_u).rearrange("p (k c) -> p k c", k=KT)
                ps = open_tile(t, more_t)
                for f in range(2):
                    for k in range(KT):
                        i = mm(ps[:, f * S:(f + 1) * S], w[:, k, f * P:(f + 1) * P], src[:, k, :],
                               start=(k == 0), stop=(k == KT - 1))
                i.then_inc(sems["unit_used"], 1)

            THREE = ((0, 0), (0, 1), (1, 0))

            def ffn_features(u, t, first=None, more=0):
                s, n = u % RING, u - FFN_U0[0]
                pe.wait_ge(sems["w_lo"], more * 6 + FFN_U0[1] + n + 1)
                ps = open_tile(t, more)
                w = [v[s][:, :].rearrange("p (k c) -> p k c", k=KT) for v in (w_hi, w_lo)]
                x2 = (xT_hi, xT_lo)
                for f in range(2):
                    for k in range(KT):
                        if first is not None and f == 0 and k % 2 == 0:
                            pe.wait_ge(sems["x_lo"], first + k // 2 + 1)
                        for i, (a, b) in enumerate(THREE):
                            j = mm(ps[:, f * S:(f + 1) * S], w[a][:, k, f * P:(f + 1) * P], x2[b][:, k, :],
                                   start=(k == 0 and i == 0), stop=(k == KT - 1 and i == 2))
                j.then_inc(sems["unit_used"], 1)

            def ffn_to_acc(u, h, first, last, more=0):
                s, n = u % RING, u - FFN_U0[0]
                pe.wait_ge(sems["w_lo"], more * 6 + FFN_U0[1] + n + 1)
                w = [v[s][:, :].rearrange("p (k c) -> p k c", k=2) for v in (w_hi, w_lo)]
                h2 = (hidden_hi, hidden_lo)
                for tt in range(TT):
                    for c in range(2):
                        for k in range(2):
                            for i, (a, b) in enumerate(THREE):
                                j = mm(acc[tt * 2 + c][:, :], h2[b][:, h + k, tt * P:(tt + 1) * P],
                                       w[a][:, k, c * 512:(c + 1) * 512],
                                       start=(first and k == 0 and i == 0), stop=(last and k == 1 and i == 2))
                        if last and tt * 2 + c < 3:
                            j.then_inc(sems["acc_ready"], 1)
                j.then_inc(sems["unit_used"], 1)

            FFN_U0 = [0, 0]

            def tokens(u, t, src):
                w = open_unit(u).rearrange("p (k c) -> p k c", k=KT)
                ps = open_tile(t)
                for tt in range(TT):
                    for k in range(KT):
                        i = mm(ps[:, tt * 256:(tt + 1) * 256], src[:, k, tt * P:(tt + 1) * P],
                               w[:, k, :], start=(k == 0), stop=(k == KT - 1))
                i.then_inc(sems["unit_used"], 1)

            def to_acc(u, src, first, last, more_u=0):
                w = open_unit(u, more_u).rearrange("p (k c) -> p k c", k=2)
                for tt in range(TT):
                    for n in range(2):
                        for k in range(2):
                            i = mm(acc[tt * 2 + n][:, :], src[k][:, tt * P:(tt + 1) * P],
                                   w[:, k, n * 512:(n + 1) * 512],
                                   start=(first and k == 0), stop=(last and k == 1))
                        if last and tt * 2 + n < 3:
                            i.then_inc(sems["acc_ready"], 1)
                i.then_inc(sems["unit_used"], 1)

            def transposes(t0, src):
                for q in range(4):
                    ps = open_tile(t0 + q)
                    for k in range(2):
                        for tt in range(TT):
                            c = (2 * q + k) * P
                            i = nc.tensor.transpose(ps[:, k * S + tt * P:k * S + (tt + 1) * P],
                                                    src[:, tt, c:c + P], ident)
                    i.then_inc(sems["tile_ready"], 1)

            def await_features(t0):
                for q in range(4):
                    pe.wait_ge(*taken(t0 + q))

            def ffn(n):
                u0, t0 = plan.unit[("ffn", n)], plan.tile[("ffn", n)]

                FFN_U0[:] = [u0, FU * n]

                def down(j, u, first, last, more=0):
                    pe.wait_ge(sems["hidden_split"], more * 4 + FT * n + 2 * j + 2)
                    ffn_to_acc(u, 2 * j % 4, first, last, more)

                ffn_features(u0, t0, first=4 * n)
                ffn_features(u0 + 1, t0 + 1)

                def lap(it):
                    for half in range(2):
                        u, t = u0 + 2 + 3 * half, t0 + 2 + 2 * half
                        ffn_features(u, t, more=it)
                        ffn_features(u + 1, t + 1, more=it)
                        down(half, u + 2, isinstance(it, int) and half == 0, False, it)
                lap(0)
                with pe.Fori(1, (FT // 2 - 1) // 2) as it:
                    lap(it)
                down(FT // 2 - 1, u0 + FU - 1, False, True)

            def norm_transposes(key, inst):
                pe.wait_ge(sems["ln_xh"], 2 * (inst + 1))
                transposes(plan.tile[key], xh)
                await_features(plan.tile[key])

            def out_proj(n, src_tiles):
                u0 = plan.unit[("out", n)]
                for j in range(4):
                    to_acc(u0 + j, [oT[:, 2 * j, :], oT[:, 2 * j + 1, :]], j == 0, j == 3)

            def attention(a, groups, per, q_of, k_of, v_of):
                key = ("att", a)
                e0 = first_score(a)
                for g in range(groups + 3):
                    if g < groups:
                        for j in range(per):
                            e = g * per + j
                            ps = open_tile(plan.tile[(key, "S", g)] + j)
                            qs, ks = q_of(e), k_of(e)
                            for tt in range(TT):
                                for m in range(len(qs)):
                                    i = mm(ps[:, tt * S:(tt + 1) * S], qs[m][:, tt * P:(tt + 1) * P],
                                           ks[m], start=(m == 0), stop=(m == len(qs) - 1))
                            i.then_inc(sems["tile_ready"], 1)
                    if 2 <= g < groups + 2:
                        for j in range(per):
                            e = (g - 2) * per + j
                            ps = open_tile(plan.tile[(key, "T", g - 2)] + j)
                            pe.wait_ge(sems["prob_norm"], e0 + e + 1)
                            for st in range(TT):
                                for tt in range(TT):
                                    i = nc.tensor.transpose(
                                        ps[:, st * S + tt * P:st * S + (tt + 1) * P],
                                        prob[:, e % 6, tt, st * P:(st + 1) * P], ident)
                            i.then_inc(sems["tile_ready"], 1)
                    if g >= 3:
                        t = plan.tile[(key, "O", g - 3)]
                        ps = open_tile(t)
                        for j in range(2):
                            e = (g - 3) * per + (j if per == 2 else 0)
                            pe.wait_ge(*taken(plan.tile[(key, "T", g - 3)] + e % per))
                            for st in range(TT):
                                dst = ps[HD * j:HD * (j + 1), 0:S] if per == 2 else ps[:, j * S:(j + 1) * S]
                                i = mm(dst, v_of(e, j)[:, st, :], probT[:, e % 4, st, :],
                                       start=(st == 0), stop=(st == TT - 1))
                        i.then_inc(sems["tile_ready"], 1)
                for g in range(groups):
                    pe.wait_ge(*taken(plan.tile[(key, "O", g)]))

            pe.wait_ge(sems["const_in"], 16)
            pe.wait_ge(sems["x_in"], 16)
            transposes(plan.tile["x"], x)
            pe.wait_ge(sems["mem_in"], 16)
            transposes(plan.tile["mem"], xh)
            await_features(plan.tile["x"])
            for i in range(DEPTH):
                ffn(2 * i)
                norm_transposes(("ln", 4 * i), 4 * i)
                if i == 0:
                    for j in range(6):
                        tokens(plan.unit["ab_in"] + j, plan.tile["ab_in"] + j, xT)
                else:
                    for j in range(8):
                        features(plan.unit["c_in"] + j, plan.tile["c_in"] + j, xT)
                    for j in range(8, 12):
                        tokens(plan.unit["c_in"] + j, plan.tile["c_in"] + j, xT)
                if i == 0:
                    await_features(plan.tile["mem"])
                for j in range(4):
                    features(plan.unit[("kv", i)] + j, plan.tile[("kv", i)] + j, memT)
                for j in range(4, 8):
                    tokens(plan.unit[("kv", i)] + j, plan.tile[("kv", i)] + j, memT)
                if i == 0:
                    t0 = plan.tile["ab_T"]
                    pe.wait_ge(sems["ab_roped"], 2)
                    for q in range(6):
                        ps = open_tile(t0 + q)
                        for b in range(2):
                            for tt in range(TT):
                                if q < 4:
                                    c = (q // 2) * 768 + ((q % 2) * 2 + b) * P
                                else:
                                    c = (q - 4) * 768 + 512 + b * P
                                i2 = nc.tensor.transpose(ps[:, b * S + tt * P:b * S + (tt + 1) * P],
                                                         roped[:, tt, c:c + P], ident)
                        i2.then_inc(sems["tile_ready"], 1)
                    for q in range(6):
                        pe.wait_ge(*taken(t0 + q))
                    attention(0, 8, 2,
                              lambda e: [qT[HD * (e % 2):HD * (e % 2) + HD, e // 2, :]],
                              lambda e: [kT[HD * (e % 2):HD * (e % 2) + HD, e // 4, :]],
                              lambda e, j: raw[:, :, (e // 8) * 768 + 640 + (e // 4 % 2) * HD:
                                               (e // 8) * 768 + 640 + (e // 4 % 2) * HD + HD])
                else:
                    for j in range(12):
                        pe.wait_ge(*taken(plan.tile["c_in"] + j))
                    attention(2, 8, 2,
                              lambda e: [qT[HD * (e % 2):HD * (e % 2) + HD, e // 2, :]],
                              lambda e: [kT[HD * (e % 2):HD * (e % 2) + HD, e // 2, :]],
                              lambda e, j: v_tok[:, :, e * HD:(e + 1) * HD])
                out_proj(2 * i, None)
                norm_transposes(("ln", 4 * i + 1), 4 * i + 1)
                for j in range(4):
                    features(plan.unit[("mq", i)] + j, plan.tile[("mq", i)] + j, xT)
                for j in range(4):
                    pe.wait_ge(*taken(plan.tile[("mq", i)] + j))
                for j in range(8):
                    pe.wait_ge(*taken(plan.tile[("kv", i)] + j))
                attention(2 * i + 1, 4, 1,
                          lambda e: [qT[:, 2 * e + m, :] for m in range(2)],
                          lambda e: [mkT[:, 2 * e + m, :] for m in range(2)],
                          lambda e, j: mv_tok[:, :, (2 * e + j) * P:(2 * e + j + 1) * P])
                out_proj(2 * i + 1, None)
                norm_transposes(("ln", 4 * i + 2), 4 * i + 2)
                ffn(2 * i + 1)
                norm_transposes(("ln", 4 * i + 3), 4 * i + 3)

            def small_tokens(l):
                ps = open_tile(plan.tile[("ba", l)])
                for tt in range(TT):
                    for k in range(KT):
                        i = mm(ps[:, tt * 16:(tt + 1) * 16], xT[:, k, tt * P:(tt + 1) * P], wba[:, l, k, :],
                               start=(k == 0), stop=(k == KT - 1))
                i.then_inc(sems["tile_ready"], 1)

            def per_head(t, lhsT, rhs):
                ps = open_tile(t)
                for h in range(4):
                    i = mm(ps[:, h * P:(h + 1) * P], lhsT(h), rhs(h), start=True, stop=True)
                i.then_inc(sems["tile_ready"], 1)

            def hd(h):
                return slice(h * P, (h + 1) * P)

            def turn4(t, src):
                ps = open_tile(t)
                for b in range(4):
                    i = nc.tensor.transpose(ps[:, b * P:(b + 1) * P], src(b), ident)
                i.then_inc(sems["tile_ready"], 1)

            def mixer2(l):
                U, T = plan.unit, plan.tile
                for j in range(2):
                    features(U[("hq", l)] + j, T[("hq", l)] + j, xT)
                for j in range(4):
                    features(U[("hf", l)] + j, T[("hf", l)] + j, xT)
                for j in range(2):
                    tokens(U[("hi", l)] + j, T[("hi", l)] + j, xT)
                for j in range(2):
                    tokens(U[("hz", l)] + j, T[("hz", l)] + j, xT)
                for j in range(6):
                    features(U[("qkv", l)] + j, T[("qkv", l)] + j, xT)
                small_tokens(l)
                for j in range(2):
                    tokens(U[("z", l)] + j, T[("z", l)] + j, xT)
                for i in range(LEVELS + 2):
                    if i < 8:
                        features(U[("gate", l, i)], T[("gate", l, i)], xT)
                    pe.wait_ge(sems["hg_k"], (LEVELS + 2) * l + i + 1)
                    pe.wait_ge(sems["hg_q"], (LEVELS + 2) * l + i + 1)
                    K, Q = hKQ[:, i % 2, 0], hKQ[:, i % 2, 1]
                    for c in range(2):
                        s, t = (c, c) if i <= LEVELS else (c, 1 - c)
                        per_head(T[("level", l, i)] + c,
                                 lambda h: K[:, h * S + s * P:h * S + (s + 1) * P],
                                 lambda h: Q[:, h * S + t * P:h * S + (t + 1) * P])
                for i in range(LEVELS + 2):
                    for c in range(2):
                        pe.wait_ge(*taken(T[("level", l, i)] + c))
                for tt in range(TT):
                    ps = open_tile(T[("hg_o", l)] + tt)
                    for h in range(4):
                        for st in range(TT):
                            i = mm(ps[:, hd(h)], hatt[:, st, h, tt * P:(tt + 1) * P], hi[:, st, hd(h)],
                                   start=(st == 0), stop=(st == TT - 1))
                    i.then_inc(sems["tile_ready"], 1)
                for j in range(4):
                    pe.wait_ge(sems["l2_sq"], 4 * l + j + 1)
                    ps = open_tile(T[("l2", l)] + j)
                    mm(ps[:, :], table("ones"), l2s[:, j, :], start=True, stop=True).then_inc(sems["tile_ready"], 1)
                pe.wait_ge(sems["hg_out"], l + 1)
                for j in range(2):
                    turn4(T[("hg_T", l)] + j, lambda b: hz[:, b % 2, hd(2 * j + b // 2)])
                pe.wait_ge(sems["l2_done"], l + 1)
                for j in range(4):
                    turn4(T[("kv_T", l)] + j, lambda b: qkvT[:, 4 + 4 * (j // 2) + b, (j % 2) * P:(j % 2 + 1) * P])
                pe.wait_ge(sems["g_ready"], l + 1)
                ps = open_tile(T[("gcum", l)])
                sums = [table("le"), table("ge")]
                for tt in range(TT):
                    for d in range(2):
                        c = tt * 8 + d * 4
                        mm(ps[:, c:c + 4], sums[d], gg[:, c:c + 4], start=True, stop=True)
                i = mm(ps[:, 16:32], table("ones"), gg[:, :], start=True, stop=True)
                i.then_inc(sems["tile_ready"], 1)
                for g in range(4):
                    tt, d = g // 2, g % 2
                    per_head(T[("gcB", l)] + g,
                             lambda h: gg[:, tt * 8 + d * 4 + h:tt * 8 + d * 4 + h + 1].to_broadcast([P, P]),
                             lambda h: sums[d])
                for tt in range(TT):
                    per_head(T[("G", l)] + tt, lambda h: qkvT[:, 4 + h, tt * P:(tt + 1) * P],
                             lambda h: qkvT[:, 4 + h, tt * P:(tt + 1) * P])
                for tt in range(TT):
                    per_head(T[("QK", l)] + tt, lambda h: qkvT[:, 4 + h, tt * P:(tt + 1) * P],
                             lambda h: qkvT[:, h, tt * P:(tt + 1) * P])
                for g in range(4):
                    pe.wait_ge(sems["a_level"], 4 * LEVELS * l + g + 1)
                    turn4(T[("A0", l)] + g, lambda h: alev[:, g, hd(h)])
                for v in range(1, LEVELS):
                    for g in range(4):
                        before = T[("A0", l)] + g if v == 1 else T[("Z", l, v - 1)] + 2 * g
                        pe.wait_ge(*taken(before))
                        pe.wait_ge(sems["a_level"], 4 * LEVELS * l + 4 * v + g + 1)
                        per_head(T[("Y", l, v)] + g, lambda h: alev[:, g, hd(h)], lambda h: winv[:, g, hd(h)])
                    for g in range(4):
                        if v == 1:
                            pe.wait_ge(sems["x_first"], 4 * l + g + 1)
                        else:
                            pe.wait_ge(*taken(T[("Z", l, v - 1)] + 2 * g + 1))
                        pe.wait_ge(*taken(T[("Y", l, v)] + g))
                        z = T[("Z", l, v)] + (2 * g if v < LEVELS - 1 else g)
                        per_head(z, lambda h: xinv[:, g, hd(h)], lambda h: yinv[:, g, hd(h)])
                        if v < LEVELS - 1:
                            per_head(z + 1, lambda h: yinv[:, g, hd(h)], lambda h: xinv[:, g, hd(h)])
                for d in range(2):
                    ga = 3 * d
                    pe.wait_ge(sems["vb"], 4 * l + ga + 1)
                    pe.wait_ge(*taken(T[("Z", l, LEVELS - 1)] + ga))
                    per_head(T[("vnA", l)] + d, lambda h: winv[:, ga, hd(h)], lambda h: vb[:, ga, hd(h)])
                for d in range(2):
                    pe.wait_ge(sems["kd"], 2 * l + d + 1)
                    pe.wait_ge(*taken(T[("vnA", l)] + d))
                    per_head(T[("S", l)] + d, lambda h: kd[:, d, hd(h)], lambda h: vn[:, 3 * d, hd(h)])
                for d in range(2):
                    tb = 1 - d
                    pe.wait_ge(*taken(T[("S", l)] + d))
                    per_head(T[("kS", l)] + d, lambda h: qkvT[:, 4 + h, tb * P:(tb + 1) * P],
                             lambda h: state[:, d, hd(h)])
                for d in range(2):
                    gb = 2 - d
                    pe.wait_ge(*taken(T[("kS", l)] + d))
                    pe.wait_ge(*taken(T[("Z", l, LEVELS - 1)] + gb))
                    per_head(T[("vnB", l)] + d, lambda h: winv[:, gb, hd(h)], lambda h: vb[:, gb, hd(h)])
                for d in range(2):
                    tb = 1 - d
                    per_head(T[("qS", l)] + d, lambda h: qkvT[:, h, tb * P:(tb + 1) * P],
                             lambda h: state[:, d, hd(h)])
                for d in range(2):
                    pe.wait_ge(*taken(T[("vnB", l)] + d))
                for tt in range(TT):
                    pe.wait_ge(*taken(T[("QK", l)] + tt))
                    ps = open_tile(T[("dn_o", l)] + tt)
                    for h in range(4):
                        for d in range(2):
                            i = mm(ps[:, hd(h)], qkd[:, 2 * tt + d, hd(h)], vn[:, 2 * tt + d, hd(h)],
                                   start=(d == 0), stop=(d == 1))
                    i.then_inc(sems["tile_ready"], 1)
                pe.wait_ge(sems["dn_out"], l + 1)
                for j in range(2):
                    turn4(T[("dn_T", l)] + j, lambda b: dn_o[:, b % 2, hd(2 * j + b // 2)])
                for name, src, turned in (("branch_dn", oT_dn, "dn_T"), ("branch_hg", oT_hg, "hg_T")):
                    for j in range(2):
                        pe.wait_ge(*taken(T[(turned, l)] + j))
                    for j in range(2):
                        w = open_unit(U[(name, l)] + j).rearrange("p (k c) -> p k c", k=4)
                        for half in range(2):
                            ps = open_tile(T[(name, l)] + 2 * j + half)
                            for f in range(2):
                                c = (half * 2 + f) * P
                                for k in range(4):
                                    i = mm(ps[:, f * S:(f + 1) * S], w[:, k, c:c + P], src[:, k, :],
                                           start=(k == 0), stop=(k == 3))
                        i.then_inc(sems["unit_used"], 1)
                for j in range(4):
                    pe.wait_ge(sems["merged"], 4 * l + j + 1)
                    to_acc(U[("out", 4 + l)] + j, [merged[:, 2 * j, :], merged[:, 2 * j + 1, :]], j == 0, j == 3)

            pe.wait_ge(sems["head_in"], 16 * 2)
            for l in range(DEPTH):
                norm_transposes(("rms", 2 * l), 8 + 2 * l)
                mixer2(l)
                norm_transposes(("rms", 2 * l + 1), 9 + 2 * l)
                ffn(4 + l)


        @block.scalar
        def _(act):
            A = nc.scalar.activation
            step = Progress(act, sems["act_step"])

            act.dma_start(const[:, :], consts).then_inc(sems["const_in"], 16)
            act.dma_start(x[:, :, :], x_in.rearrange("b (t p) d -> p (b t) d", p=P)).then_inc(sems["x_in"], 16)
            act.dma_start(xh, mem_in.rearrange("b (t p) d -> p (b t) d", p=P)).then_inc(sems["mem_in"], 16)
            act.dma_start(col[:, :], cols).then_inc(sems["cols_in"], 16)
            act.dma_start(gain[:, :], gains.partition_broadcast(P)).then_inc(sems["cols_in"], 16)
            act.dma_start(sink_b[:, :], sink.partition_broadcast(P)).then_inc(sems["cols_in"], 16)

            act.dma_start(region(18432, (3 * LEVELS + 1) * P), hmask_in).then_inc(sems["masks_in"], 16)
            act.dma_start(wba[:, :, :, :], wba_in).then_inc(sems["head_in"], 16)
            act.dma_start(arow[:, :, :, :].rearrange("p a b c -> p (a b c)"),
                          decay_rows.partition_broadcast(P)).then_inc(sems["head_in"], 16)

            def take(t, dst, src=None):
                act.wait_ge(*ready(t))
                ps = bank[t % NB]
                A(dst, ps[:, :] if src is None else src(ps), ACT.Copy).then_inc(tile_taken[t % NB], 1)

            def take_scaled(t, k, scale, bias=None):
                act.wait_ge(*ready(t))
                for j in range(2):
                    i = A(xT[:, k + j, :], bank[t % NB][:, j * S:(j + 1) * S], ACT.Identity,
                          scale=scale[:, k + j:k + j + 1], bias=bias[:, k + j:k + j + 1] if bias is not None else 0.0)
                    if j == 0:
                        step.did(i)
                i.then_inc(tile_taken[t % NB], 1)

            def split_x(n, t0):
                for q in range(4):
                    act.wait_ge(*taken(t0 + q))
                    A(pair(xT_hi, q), pair(xT, q), ACT.Copy).then_inc(sems["x_hi"], 1)

            def split_w(n, m, more=0):
                u = plan.unit[("ffn", n)] + m
                act.wait_ge(slot_full[u % RING], more * 32 + 16 * (u // RING + 1))
                act.wait_ge(sems["unit_used"], more * 6 + u - RING + 1) if u >= RING else None
                A(w_hi[u % RING][:, :], ring[:, u % RING, :], ACT.Copy).then_inc(sems["w_hi"], 1)

            def ffn(n, conv_first=False):
                t0, u0 = plan.tile[("ffn", n)], plan.unit[("ffn", n)]

                def gate(f, more):
                    if conv_first:
                        act.wait_ge(sems["conv_done"], more * 4 + FT * (n - 4) + f + 1)
                        src = conv[:, f % 4, :]
                    else:
                        act.wait_ge(sems["unit_used"], more * 6 + plan.ready[t0 + f][1])
                        src = bank[(t0 + f) % NB][:, 0:S]
                    A(silu_gate[:, f % 4, :], src, ACT.Silu).then_inc(sems["gate_silu"], 1)

                def ffn_step(m, more=0, split=True):
                    f = tile_of_step(m)
                    if f is not None and not conv_first:
                        gate(f, more)
                    if split:
                        split_w(n, m + RING, more)
                    if f is not None and conv_first:
                        gate(f, more)
                run_steps(act, ffn_step)

            def norm(inst, key, has_bias=True):
                act.wait_ge(sems["ln_var"], inst + 1)
                A(std[:, :], var[:, :], ACT.Sqrt).then_inc(sems["ln_std"], 1)
                t0 = plan.tile[key]
                gcol = col[:, inst * KT:(inst + 1) * KT]
                bcol = col[:, (8 + inst) * KT:(9 + inst) * KT] if has_bias else None
                for q in (0, 2):
                    take_scaled(t0 + q, 2 * q, gcol, bcol)

            def attention(a, groups, per, scale, mode, dst):
                key = ("att", a)
                e0 = first_score(a)
                for g in range(groups + 3):
                    if g < groups:
                        for j in range(per):
                            e = g * per + j
                            t = plan.tile[(key, "S", g)] + j
                            act.wait_ge(sems["score_max"], e0 + e + 1)
                            masked = mode(e)
                            src = score[:, e % 4, :, :] if masked else bank[t % NB][:, :].rearrange("p (t s) -> p t s", t=TT)
                            for tt in range(TT):
                                i = A(prob[:, e % 6, tt, :], src[:, tt, :], ACT.Exp,
                                      bias=nmx[:, e, tt:tt + 1], scale=1.0 if masked else scale,
                                      accum_out=psum_p[:, e, tt:tt + 1])
                                if tt == 0:
                                    step.did(i)
                            if not masked:
                                i.then_inc(tile_taken[t % NB], 1)
                            elif masked == "bias":
                                i.then_inc(sems["prob_exp"], 1)
                            else:
                                step.did(i)
                                for tt in range(TT):
                                    i = A(sink_e[:, e, tt:tt + 1], sink_b[:, e - 8:e - 7], ACT.Exp,
                                          bias=nmx[:, e, tt:tt + 1])
                                    if tt == 0:
                                        step.did(i)
                                i.then_inc(sems["prob_exp"], 1)
                    if 2 <= g < groups + 2:
                        for j in range(per):
                            e = (g - 2) * per + j
                            t = plan.tile[(key, "T", g - 2)] + j
                            take(t, probT[:, e % 4, :, :].rearrange("p a b -> p (a b)"))
                    if g >= 3:
                        t = plan.tile[(key, "O", g - 3)]
                        if per == 2:
                            take(t, oT[:, g - 3, :], lambda ps: ps[:, 0:S])
                        else:
                            take(t, oT[:, 2 * (g - 3):2 * (g - 3) + 2, :].rearrange("p a b -> p (a b)"))

            for q in range(4):
                take(plan.tile["x"] + q, pair(xT, q))
            for q in range(4):
                take(plan.tile["mem"] + q, pair(memT, q))
            act.wait_ge(sems["cols_in"], 48)
            for m in range(RING):
                split_w(0, m)
            split_x(0, plan.tile["x"])
            for i in range(DEPTH):
                ffn(2 * i)
                norm(4 * i, ("ln", 4 * i))
                if i == 0:
                    for j in range(6):
                        take(plan.tile["ab_in"] + j, raw[:, :, j * 256:(j + 1) * 256])
                    act.wait_ge(sems["ab_ssq"], 1)
                    A(srt[:, :, :], ssq[:, :, :], ACT.Sqrt).then_inc(sems["ab_sqrt"], 1)
                else:
                    act.wait_ge(sems["x_updated"], 4 * i + 1)
                    for j in range(12):
                        dst = pair(qT, j) if j < 4 else pair(kT, j - 4) if j < 8 else \
                            v_tok[:, :, (j - 8) * 256:(j - 7) * 256]
                        take(plan.tile["c_in"] + j, dst)
                for j in range(8):
                    dst = pair(mkT, j) if j < 4 else mv_tok[:, :, (j - 4) * 256:(j - 3) * 256]
                    take(plan.tile[("kv", i)] + j, dst)
                if i == 0:
                    act.wait_ge(sems["x_updated"], 1)
                    for q in range(6):
                        take(plan.tile["ab_T"] + q, pair(qT, q) if q < 4 else pair(kT, q - 4))
                    attention(0, 8, 2, HD ** -0.5, lambda e: None if e < 8 else "sink", oT)
                else:
                    attention(2, 8, 2, HD ** -0.5, lambda e: "bias", oT)
                norm(4 * i + 1, ("ln", 4 * i + 1))
                act.wait_ge(sems["x_updated"], 4 * i + 2)
                for j in range(4):
                    take(plan.tile[("mq", i)] + j, pair(qT, j))
                attention(2 * i + 1, 4, 1, 256 ** -0.5, lambda e: None, oT)
                for m in range(2):
                    split_w(2 * i + 1, m)
                norm(4 * i + 2, ("ln", 4 * i + 2))
                split_x(2 * i + 1, plan.tile[("ln", 4 * i + 2)])
                split_w(2 * i + 1, 2)
                ffn(2 * i + 1)
                if i + 1 < DEPTH:
                    split_w(2 * i + 2, 0)
                    split_w(2 * i + 2, 1)
                norm(4 * i + 3, ("ln", 4 * i + 3))
                if i + 1 < DEPTH:
                    split_x(2 * i + 2, plan.tile[("ln", 4 * i + 3)])
                    split_w(2 * i + 2, 2)

            act.wait_ge(sems["lb_arg"], 1)
            A(lb[:, :, :], lb[:, :, :], ACT.Exp).then_inc(sems["lb_exp"], 1)

            def rms_scale(r):
                act.wait_ge(sems["ln_var"], 8 + r + 1)
                A(std[:, :], var[:, :], ACT.Sqrt).then_inc(sems["ln_std"], 1)
                if r < 4:
                    for q in (0, 2):
                        take_scaled(plan.tile[("rms", r)] + q, 2 * q, col[:, 128 + r * KT:128 + (r + 1) * KT])

            def take_func(t, dst, func, scale=1.0):
                act.wait_ge(*ready(t))
                A(dst, bank[t % NB][:, :], func, scale=scale).then_inc(tile_taken[t % NB], 1)

            def tok2(v, j):
                return v[:, :, j * 256:(j + 1) * 256]

            def mixer2(l):
                T = plan.tile
                for j in range(2):
                    take_func(T[("hq", l)] + j, pair(hq, j), ACT.Silu)
                for j in range(4):
                    take_func(T[("hf", l)] + j, pair(hk[:, j // 2], j % 2), ACT.Exp, -1.0)
                for j in range(2):
                    take(T[("hi", l)] + j, tok2(hi, j))
                for j in range(2):
                    t = T[("hz", l)] + j
                    act.wait_ge(*ready(t))
                    A(tok2(hz, j), bank[t % NB][:, :].rearrange("p (t c) -> p t c", t=TT),
                      ACT.Silu).then_inc(tile_taken[t % NB], 1)
                for d in range(2):
                    act.wait_ge(sems["hg_num"], 2 * l + d + 1)
                    A(hE[:, d, 1, :], hE[:, d, 1, :], ACT.Ln).then_inc(sems["hg_log"], 1)
                for j in range(6):
                    act.wait_ge(sems["qkv_conv"], 6 * l + j + 1)
                    A(pair(qkvT, j), pair(qkvT, j), ACT.Silu).then_inc(sems["qkv_silu"], 1)
                take(T[("ba", l)], ba32, lambda ps: ps[:, 0:32])
                for j in range(2):
                    t = T[("z", l)] + j
                    act.wait_ge(*ready(t))
                    A(tok2(zs, j), bank[t % NB][:, :].rearrange("p (t c) -> p t c", t=TT),
                      ACT.Silu).then_inc(tile_taken[t % NB], 1)
                ba3 = ba32.rearrange("p (t c) -> p t c", t=TT)
                act.wait_ge(*taken(T[("ba", l)]))
                step.did(A(eb.rearrange("p (t c) -> p t c", t=TT), ba3[:, :, 0:8], ACT.Exp, scale=-1.0))
                step.did(A(arow[:, l, 0, :], arow[:, l, 0, :], ACT.Exp))
                act.wait_ge(sems["ba_y"], l + 1)
                step.link(A(ny, ny, ACT.Exp))
                A(ny, ny, ACT.Ln, bias=1.0).then_inc(sems["ba_sp"], 1)
                for i in range(LEVELS + 2):
                    if i != LEVELS:
                        act.wait_ge(sems["hg_arg"], (LEVELS + 1) * l + (i if i < LEVELS else LEVELS) + 1)
                        A(hE[:, i % 2].rearrange("p a b -> p (a b)"), hE[:, i % 2].rearrange("p a b -> p (a b)"),
                          ACT.Exp).then_inc(sems["hg_exp"], 1)
                    if i < 8:
                        take(T[("gate", l, i)], pair(gates, i))
                act.wait_ge(sems["hg_ssq"], l + 1)
                A(bss[:, 0:8], bss[:, 0:8], ACT.Sqrt).then_inc(sems["hg_std"], 1)
                act.wait_ge(sems["l2_arg"], 4 * l + 4)
                for j in range(4):
                    A(l2r[:, j, :], l2r[:, j, :], ACT.Sqrt).then_inc(sems["l2_sqrt"], 1)
                for j in range(2):
                    take(T[("hg_T", l)] + j, pair(oT_hg, j))
                for j in range(4):
                    take(T[("kv_T", l)] + j, (k_tk if j < 2 else v_tk)[:, j % 2, :])
                act.wait_ge(sems["gc_arg"], l + 1)
                step.did(A(eg, gc, ACT.Exp))
                A(kdf, kdf, ACT.Exp).then_inc(sems["gc_exp"], 1)
                for g in range(4):
                    act.wait_ge(sems["dec_arg"], 4 * l + g + 1)
                    step.link(A(dec[:, g, :], dec[:, g, :], ACT.Abs))
                    A(dec[:, g, :], dec[:, g, :], ACT.Exp, scale=-1.0).then_inc(sems["dec"], 1)
                for v in range(1, LEVELS):
                    for g in range(4):
                        take(T[("Y", l, v)] + g, yinv[:, g, :])
                for name, dst in (("vnA", (0, 3)), ("vnB", (2, 1))):
                    for d in range(2):
                        take(T[(name, l)] + d, vn[:, dst[d], :])
                act.wait_ge(sems["dn_ssq"], l + 1)
                A(bss[:, 0:8], bss[:, 0:8], ACT.Sqrt).then_inc(sems["dn_std"], 1)
                for j in range(2):
                    take(T[("dn_T", l)] + j, pair(oT_dn, j))

            for l in range(DEPTH):
                rms_scale(2 * l)
                mixer2(l)
                for i in range(8):
                    act.wait_ge(*taken(plan.tile[("gate", l, i)]))
                A(gates[:, :, :], gates[:, :, :], ACT.Sigmoid).then_inc(sems["gates_ready"], 1)
                act.wait_ge(sems["merged"], 4 * l + 4)
                for m in range(2):
                    split_w(4 + l, m)
                rms_scale(2 * l + 1)
                split_x(4 + l, plan.tile[("rms", 2 * l + 1)])
                split_w(4 + l, 2)
                ffn(4 + l, conv_first=True)
            rms_scale(4)



        @block.vector
        def _(dve):
            V = nc.vector
            step = Progress(dve, sems["dve_step"])

            def split_x(n):
                for q in range(4):
                    dve.wait_ge(sems["x_hi"], 4 * n + q + 1)
                    V.tensor_tensor(pair(xT_lo, q), pair(xT, q), pair(xT_hi, q).bitcast(F32),
                                    ALU.subtract).then_inc(sems["x_lo"], 1)

            def split_w(n, m, more=0):
                u = plan.unit[("ffn", n)] + m
                dve.wait_ge(sems["w_hi"], more * 6 + FU * n + m + 1)
                V.tensor_tensor(w_lo[u % RING][:, :], ring[:, u % RING, :], w_hi[u % RING][:, :].bitcast(F32),
                                ALU.subtract).then_inc(sems["w_lo"], 1)

            def ffn(n, conv_first=False):
                t0 = plan.tile[("ffn", n)]

                def product(f, more):
                    dve.wait_ge(sems["gate_silu"], more * 4 + FT * n + f + 1)
                    b, h = (t0 + f) % NB, f % 4
                    V.scalar_tensor_tensor(hidden[:, h, :], silu_gate[:, h, :], 1.0 if conv_first else 0.5,
                                           bank[b][:, S:2 * S], ALU.mult, ALU.mult).then_inc(tile_taken[b], 1)
                    dve.wait_ge(tile_taken[b], more + (t0 + f) // NB + 1)
                    V.tensor_copy(hidden_hi[:, h, :], hidden[:, h, :]).then_inc(sems["hidden_high"], 1)
                    dve.wait_ge(sems["hidden_high"], more * 4 + FT * n + f + 1)
                    V.tensor_tensor(hidden_lo[:, h, :], hidden[:, h, :], hidden_hi[:, h, :].bitcast(F32),
                                    ALU.subtract).then_inc(sems["hidden_split"], 1)

                def ffn_step(m, more=0, split=True):
                    f = tile_of_step(m)
                    if f is not None and conv_first:
                        convolve(n, f, more)
                    if split:
                        split_w(n, m + RING, more)
                    if f is not None:
                        product(f, more)
                run_steps(dve, ffn_step)

            def await_acc(n, tt, half, last_unit):
                j = tt * 2 + half
                if j < 3:
                    dve.wait_ge(sems["acc_ready"], 3 * n + j + 1)
                else:
                    dve.wait_ge(sems["unit_used"], last_unit + 1)
                return acc[j][:, :]

            def take_scaled(t0, inst, bias=True):
                for q in (1, 3):
                    t = t0 + q
                    dve.wait_ge(*ready(t))
                    for j in range(2):
                        k = 2 * q + j
                        g = col[:, inst * KT + k:inst * KT + k + 1]
                        src = bank[t % NB][:, j * S:(j + 1) * S]
                        if bias:
                            i = V.tensor_scalar(xT[:, k, :], src, g, col[:, (8 + inst) * KT + k:(8 + inst) * KT + k + 1],
                                                ALU.mult, ALU.add)
                        else:
                            i = V.tensor_scalar(xT[:, k, :], src, g, None, ALU.mult)
                        if j == 0:
                            step.did(i)
                    i.then_inc(tile_taken[t % NB], 1)

            def norm(inst, key, last_unit):
                if inst > 0:
                    dve.wait_ge(sems["x_updated"], inst)
                else:
                    dve.wait_ge(sems["x_in"], 16)
                for tt in range(TT):
                    for h in range(2):
                        a = await_acc(inst, tt, h, last_unit)
                        c = slice(h * 512, (h + 1) * 512)
                        step.link(V.scalar_tensor_tensor(xh[:, tt, c], x[:, tt, c], ALPHA, a, ALU.mult, ALU.add))
                        step.did(V.bn_stats(bn[:, tt * 2 + h, :], xh[:, tt, c]))
                    step.sync()
                    step.did(V.bn_aggr(mv[:, tt, :], bn[:, 2 * tt:2 * tt + 2, :]))
                step.sync()
                V.tensor_scalar(var[:, :], mv[:, :, 1], LN_EPS, None, ALU.add).then_inc(sems["ln_var"], 1)
                dve.wait_ge(sems["ln_std"], inst + 1)
                step.link(V.reciprocal(rstd[:, :], std[:, :]))
                for tt in range(TT):
                    V.tensor_scalar(xh[:, tt, :], xh[:, tt, :], mv[:, tt, 0:1], rstd[:, tt:tt + 1],
                                    ALU.subtract, ALU.mult).then_inc(sems["ln_xh"], 1)
                take_scaled(plan.tile[key], inst)

            def rope():
                for j in range(6):
                    dve.wait_ge(*taken(plan.tile["ab_in"] + j))
                heads = raw[:, :, 0:640]
                step.link(V.tensor_tensor(rtmp[:, 0], heads, heads, ALU.mult))
                step.link(V.reduce_sum(ssq[:, :, :].rearrange("p t h -> p (t h)"),
                                       rtmp[:, 0].rearrange("p t (h d) -> p (t h) d", d=HD), axis=AX_X))
                V.tensor_scalar(ssq[:, :, :], ssq[:, :, :], 1.0 / HD, EPS, ALU.mult, ALU.add).then_inc(sems["ab_ssq"], 1)
                dve.wait_ge(sems["ab_sqrt"], 1)
                step.link(V.reciprocal(srt[:, :, :], srt[:, :, :]))
                h4 = heads.rearrange("p t (h d) -> p t h d", d=HD)
                for tt in range(TT):
                    step.did(V.tensor_tensor(h4[:, tt], h4[:, tt], srt[:, tt, :].unsqueeze(2).to_broadcast([P, 10, HD]), ALU.mult))
                step.sync()
                for a, b, g in ((0, 8, 0), (8, 10, HD)):
                    gb = gain[:, g:g + HD].unsqueeze(1).to_broadcast([P, b - a, HD])
                    for tt in range(TT):
                        step.did(V.tensor_tensor(h4[:, tt, a:b], h4[:, tt, a:b], gb, ALU.mult))
                step.sync()
                rt = table("rope").rearrange("p (t m f) -> p t m f", t=TT, m=2)
                for m in range(2):
                    for tt in range(TT):
                        src = raw[:, tt, m * 768:m * 768 + 640].rearrange("p (h d) -> p h d", d=HD)
                        a = rtmp[:, 2 * m, tt].rearrange("p (h d) -> p h d", d=HD)
                        b = rtmp[:, 2 * m + 1, tt].rearrange("p (h d) -> p h d", d=HD)

                        def row(lo, n):
                            return rt[:, tt, m, lo:lo + n].unsqueeze(1).to_broadcast([P, 10, n])
                        step.did(V.tensor_tensor(a, src, row(0, 64), ALU.mult))
                        step.did(V.tensor_tensor(b[:, :, 0:32], src[:, :, 32:64], row(64, 32), ALU.mult))
                        step.did(V.tensor_tensor(b[:, :, 32:64], src[:, :, 0:32], row(96, 32), ALU.mult))
                step.sync()
                for m in range(2):
                    a, b, c = rtmp[:, 2 * m], rtmp[:, 2 * m + 1], m * 768
                    step.did(V.tensor_tensor(roped[:, :, c:c + 512], a[:, :, 0:512], b[:, :, 0:512], ALU.add))
                    keys = roped[:, :, c + 512:c + 768].rearrange("p t (k u d) -> p t k u d", k=2, u=2)
                    for u in range(2):
                        for tt in range(TT):
                            i = V.tensor_tensor(keys[:, tt, :, u, :],
                                                a[:, tt, 512:640].rearrange("p (k d) -> p k d", k=2),
                                                b[:, tt, 512:640].rearrange("p (k d) -> p k d", k=2), ALU.add)
                            if u + tt < 2:
                                step.did(i)
                    i.then_inc(sems["ab_roped"], 1)

            def attention(a, groups, per, scale, mode, exps):
                key = ("att", a)
                e0 = first_score(a)
                first_masked = min([e for e in range(groups * per) if mode(e)] or [0])
                for g in range(groups + 1):
                    if g < groups:
                        for j in range(per):
                            e = g * per + j
                            t = plan.tile[(key, "S", g)] + j
                            b = bank[t % NB]
                            dve.wait_ge(*ready(t))
                            masked = mode(e)
                            if not masked:
                                step.link(V.reduce_max(mx[:, e, :], b[:, :].rearrange("p (t s) -> p t s", t=TT), axis=AX_X))
                                V.tensor_scalar(nmx[:, e, :], mx[:, e, :], -scale, None, ALU.mult).then_inc(sems["score_max"], 1)
                                continue
                            sc = score[:, e % 4, :, :]
                            if masked == "sink":
                                V.scalar_tensor_tensor(sc.rearrange("p a b -> p (a b)"), b[:, :], scale, table("window"),
                                                       ALU.mult, ALU.add).then_inc(tile_taken[t % NB], 1)
                            else:
                                for tt in range(TT):
                                    bias = grid_bias[:, e, 2 - 2 * tt:6 - 2 * tt, ::-1]

                                    def rows(v):
                                        return v.rearrange("p (r c) -> p r c", c=GRID)
                                    i = V.scalar_tensor_tensor(rows(sc[:, tt, :]), rows(b[:, tt * S:(tt + 1) * S]), scale, bias,
                                                               ALU.mult, ALU.add)
                                    if tt == 0:
                                        step.did(i)
                                i.then_inc(tile_taken[t % NB], 1)
                                step.sync()
                            dve.wait_ge(*taken(t))
                            step.link(V.reduce_max(mx[:, e, :], sc, axis=AX_X))
                            if masked == "sink":
                                step.link(V.tensor_scalar(mx[:, e, :], mx[:, e, :], sink_b[:, e - 8:e - 7], None, ALU.max))
                            V.tensor_scalar(nmx[:, e, :], mx[:, e, :], -1.0, None, ALU.mult).then_inc(sems["score_max"], 1)
                    if g >= 1:
                        for j in range(per):
                            e = (g - 1) * per + j
                            masked = mode(e)
                            if masked:
                                dve.wait_ge(sems["prob_exp"], exps + e - first_masked + 1)
                            else:
                                dve.wait_ge(*taken(plan.tile[(key, "S", g - 1)] + j))
                            if masked == "sink":
                                step.link(V.tensor_tensor(psum_p[:, e, :], psum_p[:, e, :], sink_e[:, e, :], ALU.add))
                            step.link(V.reciprocal(rec[:, e, :], psum_p[:, e, :]))
                            for tt in range(TT):
                                i = V.tensor_scalar(prob[:, e % 6, tt, :], prob[:, e % 6, tt, :], rec[:, e, tt:tt + 1], None,
                                                    ALU.mult)
                                if tt == 0:
                                    step.did(i)
                            i.then_inc(sems["prob_norm"], 1)

            dve.wait_ge(sems["cols_in"], 48)
            for m in range(RING):
                split_w(0, m)
            split_x(0)
            for i in range(DEPTH):
                ffn(2 * i)
                norm(4 * i, ("ln", 4 * i), plan.unit[("ffn", 2 * i)] + 32)
                if i == 0:
                    rope()
                    attention(0, 8, 2, HD ** -0.5, lambda e: None if e < 8 else "sink", 0)
                else:
                    dve.wait_ge(sems["bias_ready"], 1)
                    attention(2, 8, 2, HD ** -0.5, lambda e: "bias", 8)
                norm(4 * i + 1, ("ln", 4 * i + 1), plan.unit[("out", 2 * i)] + 3)
                attention(2 * i + 1, 4, 1, 256 ** -0.5, lambda e: None, 0)
                for m in range(2):
                    split_w(2 * i + 1, m)
                norm(4 * i + 2, ("ln", 4 * i + 2), plan.unit[("out", 2 * i + 1)] + 3)
                split_x(2 * i + 1)
                split_w(2 * i + 1, 2)
                ffn(2 * i + 1)
                if i + 1 < DEPTH:
                    split_w(2 * i + 2, 0)
                    split_w(2 * i + 2, 1)
                norm(4 * i + 3, ("ln", 4 * i + 3), plan.unit[("ffn", 2 * i + 1)] + 32)
                if i + 1 < DEPTH:
                    split_x(2 * i + 2)
                    split_w(2 * i + 2, 2)

            def signal(sem, n):
                step.sync()
                dve.sem_inc(sem, n)

            def rms(r):
                for tt in range(TT):
                    for h in range(2):
                        c = slice(h * 512, (h + 1) * 512)
                        if r > 0:
                            last = plan.unit[("out", 4 + r // 2)] + 3 if r % 2 else plan.unit[("ffn", 3 + r // 2)] + 32
                            a = await_acc(7 + r, tt, h, last)
                            step.link(V.tensor_tensor(x[:, tt, c], x[:, tt, c], a, ALU.add))
                        step.did(V.bn_stats(bn[:, tt * 2 + h, :], x[:, tt, c]))
                    step.sync()
                    step.did(V.bn_aggr(mv[:, tt, :], bn[:, 2 * tt:2 * tt + 2, :]))
                step.sync()
                step.link(V.tensor_tensor(var[:, :], mv[:, :, 0], mv[:, :, 0], ALU.mult))
                V.scalar_tensor_tensor(var[:, :], var[:, :], EPS, mv[:, :, 1], ALU.add, ALU.add).then_inc(sems["ln_var"], 1)
                dve.wait_ge(sems["ln_std"], 8 + r + 1)
                step.link(V.reciprocal(rstd[:, :], std[:, :]))
                for tt in range(TT):
                    V.tensor_scalar(xh[:, tt, :], x[:, tt, :], rstd[:, tt:tt + 1], None, ALU.mult).then_inc(sems["ln_xh"], 1)
                if r < 4:
                    for q in (1, 3):
                        t = plan.tile[("rms", r)] + q
                        dve.wait_ge(*ready(t))
                        for j in range(2):
                            k = 2 * q + j
                            i = V.tensor_scalar(xT[:, k, :], bank[t % NB][:, j * S:(j + 1) * S],
                                                col[:, 128 + r * KT + k:129 + r * KT + k], None, ALU.mult)
                            if j == 0:
                                step.did(i)
                        i.then_inc(tile_taken[t % NB], 1)

            def taps(dst, src, weight, center, bias=None):
                yield lambda: V.tensor_scalar(dst, src, weight(center), bias, ALU.mult,
                                              ALU.add if bias is not None else ALU.bypass)
                for j in range(2 * center + 1):
                    o = j - center
                    if o < 0:
                        yield lambda o=o, j=j: V.scalar_tensor_tensor(dst[:, -o:S], src[:, 0:S + o], weight(j),
                                                                     dst[:, -o:S], ALU.mult, ALU.add)
                    if o > 0:
                        yield lambda o=o, j=j: V.scalar_tensor_tensor(dst[:, 0:S - o], src[:, o:S], weight(j),
                                                                     dst[:, 0:S - o], ALU.mult, ALU.add)

            def lower_bounds():
                c = 160 + 120 + 176
                l0, l1 = col[:, c:c + 8], col[:, c + 8:c + 16]
                m = small[:, 0, 0:8]
                step.link(V.tensor_tensor(m, l0, l1, ALU.max))
                step.did(V.tensor_tensor(lb[:, 0, :], l0, m, ALU.subtract))
                V.tensor_tensor(lb[:, 1, :], l1, m, ALU.subtract).then_inc(sems["lb_arg"], 1)
                dve.wait_ge(sems["lb_exp"], 1)
                step.link(V.tensor_tensor(m, lb[:, 0, :], lb[:, 1, :], ALU.add))
                step.link(V.reciprocal(m, m))
                for i in range(2):
                    step.did(V.tensor_tensor(lb[:, i, :], lb[:, i, :], m, ALU.mult))
                step.sync()
                step.link(V.tensor_tensor(lb[:, 1, :], lb[:, 0, :], lb[:, 1, :], ALU.add))
                step.link(V.tensor_tensor(lb[:, 1, :], lb[:, 1, :], lb[:, 0, :], ALU.subtract))
                step.link(V.tensor_tensor(lb[:, 0, :], lb[:, 0, :], lb[:, 0, :], ALU.subtract))
                step.link(V.tensor_scalar(lb[:, :, :], lb[:, :, :], 0.0, 1.0, ALU.max, ALU.min))
                r = float(P) ** -0.5
                step.link(V.tensor_scalar(omlb[:, :, :], lb[:, :, :], -r, r, ALU.mult, ALU.add))

            def decays(l):
                T = plan.tile
                flat = lambda v: v.rearrange("p a b -> p (a b)")
                for d in range(2):
                    for j in range(2):
                        dve.wait_ge(*taken(T[("hf", l)] + 2 * d + j))
                    e, den, num = hk[:, d], hE[:, d, 0, :], hE[:, d, 1, :]
                    step.link(V.tensor_scalar(den, flat(e), 1.0, None, ALU.add))
                    step.did(V.reciprocal(den, den))
                    for h in range(4):
                        step.did(V.tensor_scalar(num[:, h * S:(h + 1) * S], e[:, h, :], lb[:, l, d * 4 + h:d * 4 + h + 1],
                                                 1.0, ALU.mult, ALU.add))
                    step.sync()
                    V.tensor_tensor(num, num, den, ALU.mult).then_inc(sems["hg_num"], 1)
                    for h in range(4):
                        step.did(V.scalar_tensor_tensor(e[:, h, :], e[:, h, :], omlb[:, l, d * 4 + h:d * 4 + h + 1],
                                                        den[:, h * S:(h + 1) * S], ALU.mult, ALU.mult))
                for d in range(2):
                    dve.wait_ge(sems["hg_log"], 2 * l + d + 1)
                    num = hE[:, d, 1, :]
                    for b in range(8):
                        c = slice(b * P, (b + 1) * P)
                        step.did(V.tensor_tensor_scan(flat(hF[:, d])[:, c], table("ones"), num[:, c], 0.0,
                                                      ALU.mult, ALU.add))
                step.sync()
                step.link(V.tensor_copy(btot, hF[:, 1, :, P - 1]))
                step.link(V.tensor_tensor(flat(hF[:, 1]), flat(hF[:, 1]), hE[:, 1, 1, :], ALU.subtract))

            def conv_qkv(l):
                for j in range(6):
                    t = plan.tile[("qkv", l)] + j
                    dve.wait_ge(*ready(t))
                    steps = []
                    for f in range(2):
                        n = 2 * j + f

                        def weight(tap, n=n):
                            c = 160 + (l * 5 + tap) * 12 + n
                            return col[:, c:c + 1]
                        steps.append(list(taps(qkvT[:, n, :], bank[t % NB][:, f * S:(f + 1) * S], weight, 2)))
                    for k in range(5):
                        for f in range(2):
                            i = steps[f][k]()
                            if k == 4 and f == 1:
                                i.then_inc(tile_taken[t % NB], 1)
                            else:
                                step.did(i)
                        if k < 4:
                            step.sync()
                    step.sync()
                    dve.wait_ge(*taken(t))
                    signal(sems["qkv_conv"], 1)

            def args(l, i):
                K, Q = hE[:, i % 2, 0, :], hE[:, i % 2, 1, :]
                F, B = hF[:, 0].rearrange("p h s -> p (h s)"), hF[:, 1].rearrange("p h s -> p (h s)")
                m = 1 << min(i, LEVELS)
                half = lambda v: v.rearrange("p (n u m) -> p n u m", u=2, m=m)
                nb = 4 * S // (2 * m)
                K4, Q4, F4, B4 = half(K), half(Q), half(F), half(B)
                if i < LEVELS:
                    fref = F4[:, :, 0, m - 1:m].to_broadcast([P, nb, m])
                    bref = B4[:, :, 1, 0:1].to_broadcast([P, nb, m])
                    step.did(V.tensor_tensor(K4[:, :, 0, :], fref, F4[:, :, 0, :], ALU.subtract))
                    step.did(V.tensor_tensor(K4[:, :, 1, :], B4[:, :, 1, :], bref, ALU.subtract))
                    step.did(V.tensor_tensor(Q4[:, :, 1, :], F4[:, :, 1, :], fref, ALU.subtract))
                    V.tensor_tensor(Q4[:, :, 0, :], bref, B4[:, :, 0, :], ALU.subtract).then_inc(sems["hg_arg"], 1)
                else:
                    fref = F4[:, :, 0, m - 1:m].to_broadcast([P, nb, m])
                    step.did(V.tensor_tensor(K4[:, :, 0, :], fref, F4[:, :, 0, :], ALU.subtract))
                    step.did(V.tensor_copy(K4[:, :, 1, :], B4[:, :, 1, :]))
                    step.did(V.tensor_copy(Q4[:, :, 1, :], F4[:, :, 1, :]))
                    V.tensor_tensor(Q4[:, :, 0, :], btot.unsqueeze(2).to_broadcast([P, 4, m]), B4[:, :, 0, :],
                                    ALU.subtract).then_inc(sems["hg_arg"], 1)

            def kmul(l, i):
                K = hKQ[:, i % 2, 0, :]
                kf, kb = hk[:, 0].rearrange("p h s -> p (h s)"), hk[:, 1].rearrange("p h s -> p (h s)")
                if i == LEVELS:
                    V.tensor_tensor(K, kf, kb, ALU.add).then_inc(sems["hg_k"], 1)
                    return
                dve.wait_ge(sems["hg_exp"], (LEVELS + 1) * l + min(i, LEVELS) + 1)
                m = 1 << min(i, LEVELS)
                half = lambda v: v.rearrange("p (n u m) -> p n u m", u=2, m=m)
                E = half(hE[:, i % 2, 0, :])
                step.did(V.tensor_tensor(half(K)[:, :, 0, :], half(kf)[:, :, 0, :], E[:, :, 0, :], ALU.mult))
                V.tensor_tensor(half(K)[:, :, 1, :], half(kb)[:, :, 1, :], E[:, :, 1, :], ALU.mult).then_inc(sems["hg_k"], 1)

            def gather(l, i):
                for c in range(2):
                    t = plan.tile[("level", l, i)] + c
                    dve.wait_ge(*ready(t))
                    src = heads2(bank[t % NB][:, :])
                    q = c if i <= LEVELS else 1 - c
                    dst = hatt[:, c, :, q * P:(q + 1) * P]
                    if 0 < i <= LEVELS:
                        dve.wait_ge(*taken(plan.tile[("level", l, i - 1)] + c))
                    if i == 0 or i > LEVELS:
                        j = V.tensor_copy(dst, src)
                    else:
                        mask = hmask[:, i * P:(i + 1) * P].unsqueeze(1).to_broadcast([P, 4, P])
                        j = V.copy_predicated(dst, mask, src)
                    j.then_inc(tile_taken[t % NB], 1)

            def head_rms(rows, gate, ssq_name, std_name, l):
                v8 = lambda v: v.rearrange("p t (h d) -> p (t h) d", d=P)
                sq = region(10240, 1024)
                step.link(V.tensor_tensor(sq, rows.rearrange("p t c -> p (t c)"), rows.rearrange("p t c -> p (t c)"), ALU.mult))
                step.link(V.reduce_sum(bss[:, 0:8], sq.rearrange("p (a d) -> p a d", d=P), axis=AX_X))
                V.tensor_scalar(bss[:, 0:8], bss[:, 0:8], 1.0 / P, EPS, ALU.mult, ALU.add).then_inc(sems[ssq_name], 1)
                dve.wait_ge(sems[std_name], l + 1)
                step.link(V.reciprocal(brs[:, 0:8], bss[:, 0:8]))
                step.link(V.tensor_tensor(v8(rows), v8(rows), brs[:, 0:8].unsqueeze(2).to_broadcast([P, 8, P]), ALU.mult))

            def mixer2(l):
                T = plan.tile
                decays(l)
                conv_qkv(l)
                dve.wait_ge(*taken(T[("ba", l)]))
                ba3 = ba32.rearrange("p (t c) -> p t c", t=TT)
                t3 = lambda v: v.rearrange("p (t c) -> p t c", t=TT)
                step.link(V.tensor_tensor(t3(yb), ba3[:, :, 8:16], arow[:, l, 1, :].unsqueeze(1).to_broadcast([P, TT, 8]), ALU.add))
                V.scalar_tensor_tensor(ny, yb, -1.0, yb, ALU.mult, ALU.min).then_inc(sems["ba_y"], 1)
                dve.wait_ge(sems["ba_sp"], l + 1)
                step.link(V.tensor_scalar(eb, eb, 1.0, None, ALU.add))
                step.did(V.reciprocal(beta, eb))
                step.link(V.scalar_tensor_tensor(gg, yb, 0.0, ny, ALU.max, ALU.add))
                V.scalar_tensor_tensor(t3(gg), t3(gg), -1.0, arow[:, l, 0, :].unsqueeze(1).to_broadcast([P, TT, 8]),
                                       ALU.mult, ALU.mult).then_inc(sems["g_ready"], 1)
                n = LEVELS + 2
                for i in range(n + 2):
                    if i < n and i != LEVELS:
                        if i >= 2 and i - 2 != LEVELS:
                            dve.wait_ge(sems["hg_q"], n * l + i - 1)
                            dve.wait_ge(sems["hg_k"], n * l + i - 1)
                        args(l, i)
                    if 1 <= i <= n:
                        kmul(l, i - 1)
                    if i >= 2:
                        gather(l, i - 2)
                dve.wait_ge(*ready(T[("hg_o", l)] + 1))
                for tt in range(TT):
                    t = T[("hg_o", l)] + tt
                    V.tensor_copy(hi[:, tt, :], bank[t % NB][:, :]).then_inc(tile_taken[t % NB], 1)
                for tt in range(TT):
                    dve.wait_ge(*taken(T[("hg_o", l)] + tt))
                for j in range(4):
                    dve.wait_ge(sems["qkv_silu"], 6 * l + j + 1)
                    src = qkvT[:, 2 * j:2 * j + 2, :].rearrange("p a b -> p (a b)")
                    V.tensor_tensor(l2s[:, j, :], src, src, ALU.mult).then_inc(sems["l2_sq"], 1)
                for j in range(4):
                    t = T[("l2", l)] + j
                    dve.wait_ge(*ready(t))
                    step.link(V.tensor_scalar(l2r[:, j, :], bank[t % NB][:, :], EPS, None, ALU.add))
                    signal(tile_taken[t % NB], 1)
                head_rms(hi, hz, "hg_ssq", "hg_std", l)
                dve.wait_ge(sems["z_ready"], 2 * l + 1)
                V.tensor_tensor(hz, hi, hz, ALU.mult).then_inc(sems["hg_out"], 1)
                signal(sems["l2_arg"], 4)
                for j in range(4):
                    dve.wait_ge(sems["l2_sqrt"], 4 * l + j + 1)
                    step.link(V.reciprocal(l2r[:, j, :], l2r[:, j, :]))
                    src = qkvT[:, 2 * j:2 * j + 2, :].rearrange("p a b -> p (a b)")
                    i = V.scalar_tensor_tensor(src, src, float(P) ** -0.5 if j < 2 else 1.0, l2r[:, j, :], ALU.mult, ALU.mult)
                    if j < 3:
                        step.did(i)
                i.then_inc(sems["l2_done"], 1)
                t = T[("gcum", l)]
                dve.wait_ge(*ready(t))
                step.did(V.tensor_copy(gc, bank[t % NB][:, 0:16]))
                step.link(V.tensor_copy(kdf, bank[t % NB][:, 16:32]))
                step.link(V.tensor_tensor(kdf, kdf, gc, ALU.subtract))
                signal(tile_taken[t % NB], 1)
                signal(sems["gc_arg"], 1)
                for g in range(4):
                    t = T[("gcB", l)] + g
                    dve.wait_ge(*ready(t))
                    for h in range(4):
                        c = (g // 2) * 8 + (g % 2) * 4 + h
                        step.did(V.tensor_scalar(dec[:, g, h * P:(h + 1) * P], bank[t % NB][:, h * P:(h + 1) * P],
                                                 gc[:, c:c + 1], None, ALU.subtract))
                    step.sync()
                    signal(tile_taken[t % NB], 1)
                    signal(sems["dec_arg"], 1)
                dve.wait_ge(sems["gc_exp"], l + 1)
                V.scalar_tensor_tensor(nbe, beta, -1.0, eg, ALU.mult, ALU.mult).then_inc(sems["nbe"], 1)
                for tt in range(TT):
                    t = T[("G", l)] + tt
                    dve.wait_ge(*ready(t))
                    for d in range(2):
                        g = 2 * tt + d
                        dve.wait_ge(sems["dec"], 4 * l + g + 1)
                        for h in range(4):
                            c = tt * 8 + d * 4 + h
                            i = V.scalar_tensor_tensor(amat[:, g, h * P:(h + 1) * P], bank[t % NB][:, h * P:(h + 1) * P],
                                                       beta[:, c:c + 1], dec[:, g, h * P:(h + 1) * P], ALU.mult, ALU.mult)
                            if h < 3:
                                step.did(i)
                        i.then_inc(sems["a_ready"], 1)
                    dve.wait_ge(sems["a_ready"], 4 * l + 2 * tt + 2)
                    signal(tile_taken[t % NB], 1)
                for tt in range(TT):
                    t = T[("QK", l)] + tt
                    dve.wait_ge(*ready(t))
                    dve.wait_ge(sems["dec_masked"], 4 * l + 2 * tt + 2)
                    step.did(V.tensor_tensor(qkd[:, 2 * tt, :], bank[t % NB][:, :], qkd[:, 2 * tt, :], ALU.mult))
                    V.tensor_tensor(qkd[:, 2 * tt + 1, :], bank[t % NB][:, :], qkd[:, 2 * tt + 1, :],
                                    ALU.mult).then_inc(tile_taken[t % NB], 1)
                eye = ident.unsqueeze(1).to_broadcast([P, 4, P])
                for g in range(4):
                    dve.wait_ge(sems["a_level"], 4 * LEVELS * l + g + 1)
                    V.tensor_tensor(heads2(xinv[:, g, :]), eye, heads2(alev[:, g, :]), ALU.subtract).then_inc(sems["x_first"], 1)
                    t = T[("A0", l)] + g
                    dve.wait_ge(*ready(t))
                    V.tensor_tensor(heads2(winv[:, g, :]), eye, heads2(bank[t % NB][:, :]),
                                    ALU.subtract).then_inc(tile_taken[t % NB], 1)
                for v in range(1, LEVELS):
                    for g in range(4):
                        for j, m in enumerate((winv, xinv) if v < LEVELS - 1 else (winv,)):
                            t = T[("Z", l, v)] + (2 * g if v < LEVELS - 1 else g) + j
                            dve.wait_ge(*ready(t))
                            V.tensor_tensor(m[:, g, :], m[:, g, :], bank[t % NB][:, :], ALU.subtract).then_inc(tile_taken[t % NB], 1)
                for d in range(2):
                    t = T[("S", l)] + d
                    dve.wait_ge(*ready(t))
                    V.tensor_copy(state[:, d, :], bank[t % NB][:, :]).then_inc(tile_taken[t % NB], 1)
                for d in range(2):
                    t, gb, tb = T[("kS", l)] + d, 2 - d, 1 - d
                    dve.wait_ge(*ready(t))
                    dve.wait_ge(sems["vb"], 4 * l + 4)
                    dve.wait_ge(sems["nbe"], l + 1)
                    for h in range(4):
                        c = tb * 8 + d * 4 + h
                        hs = slice(h * P, (h + 1) * P)
                        i = V.scalar_tensor_tensor(vb[:, gb, hs], bank[t % NB][:, hs], nbe[:, c:c + 1], vb[:, gb, hs],
                                                   ALU.mult, ALU.add)
                        if h < 3:
                            step.did(i)
                    i.then_inc(tile_taken[t % NB], 1)
                for d in range(2):
                    t, tb = T[("qS", l)] + d, 1 - d
                    dve.wait_ge(*ready(t))
                    for h in range(4):
                        c = tb * 8 + d * 4 + h
                        hs = slice(h * P, (h + 1) * P)
                        i = V.tensor_scalar(qs[:, tb, hs], bank[t % NB][:, hs], eg[:, c:c + 1], None, ALU.mult)
                        if h < 3:
                            step.did(i)
                    i.then_inc(tile_taken[t % NB], 1)
                for d in range(2):
                    dve.wait_ge(*taken(T[("qS", l)] + d))
                for tt in range(TT):
                    t = T[("dn_o", l)] + tt
                    dve.wait_ge(*ready(t))
                    V.tensor_tensor(dn_o[:, tt, :], bank[t % NB][:, :], qs[:, tt, :], ALU.add).then_inc(tile_taken[t % NB], 1)
                for tt in range(TT):
                    dve.wait_ge(*taken(T[("dn_o", l)] + tt))
                head_rms(dn_o, zs, "dn_ssq", "dn_std", l)
                dve.wait_ge(sems["z_ready"], 2 * l + 2)
                V.tensor_tensor(dn_o, dn_o, zs, ALU.mult).then_inc(sems["dn_out"], 1)
                dve.wait_ge(sems["gates_ready"], l + 1)
                for j in range(4):
                    t = T[("branch_dn", l)] + j
                    dve.wait_ge(*ready(t))
                    V.tensor_tensor(pair2(mtmp, j), pair2(gates, j), bank[t % NB][:, :], ALU.mult).then_inc(tile_taken[t % NB], 1)
                for j in range(4):
                    t = T[("branch_hg", l)] + j
                    dve.wait_ge(*ready(t))
                    V.tensor_tensor(pair2(merged, j), pair2(gates, 4 + j), bank[t % NB][:, :],
                                    ALU.mult).then_inc(tile_taken[t % NB], 1)
                for j in range(4):
                    dve.wait_ge(*taken(T[("branch_dn", l)] + j))
                    dve.wait_ge(*taken(T[("branch_hg", l)] + j))
                    V.tensor_tensor(pair2(merged, j), pair2(merged, j), pair2(mtmp, j), ALU.add).then_inc(sems["merged"], 1)

            def pair2(buf, j):
                return buf[:, 2 * j:2 * j + 2, :].rearrange("p a b -> p (a b)")

            def convolve(n, f, more):
                l, t0 = n - 4, plan.tile[("ffn", n)]
                dve.wait_ge(sems["unit_used"], more * 6 + plan.ready[t0 + f][1])
                c = 280 + l * 66 + f

                def pick(at):
                    return col[:, at:at + 1] if isinstance(more, int) else col[:, bass.ds(more * 4 + at, 1)]
                steps = list(taps(conv[:, f % 4, :], bank[(t0 + f) % NB][:, 0:S], lambda j: pick(c + j * FT), 1,
                                  pick(280 + 132 + l * FT + f)))
                for k in range(2):
                    steps[k]().then_inc(sems["conv_step"], 1)
                    dve.wait_ge(sems["conv_step"], more * 8 + FT * 2 * l + 2 * f + k + 1)
                steps[2]().then_inc(sems["conv_done"], 1)

            lower_bounds()
            dve.wait_ge(sems["x_updated"], 8)
            dve.wait_ge(sems["head_in"], 16 * 2)
            for l in range(DEPTH):
                rms(2 * l)
                mixer2(l)
                for m in range(2):
                    split_w(4 + l, m)
                rms(2 * l + 1)
                split_x(4 + l)
                split_w(4 + l, 2)
                ffn(4 + l, conv_first=True)
            rms(4)
            dve.wait_ge(sems["final_in"], 16)
            dve.wait_ge(sems["ln_xh"], 2 * 13)
            V.tensor_tensor(x[:, :, :], xh, f_rows.unsqueeze(1).to_broadcast([P, TT, D]), ALU.mult).then_inc(sems["final_rows"], 1)


        @block.gpsimd
        def _(pool):
            G = nc.gpsimd
            step = Progress(pool, sems["pool_step"])

            pool.wait_ge(sems["masks_in"], 16)
            pairs = region(18432, (3 * LEVELS + 1) * P)
            step.did(G.tensor_copy(hmask[:, :], pairs[:, 0:(LEVELS + 1) * P]))
            step.link(G.tensor_copy(levels[:, :], pairs[:, (LEVELS + 1) * P:]))
            rows = 0
            for inst in range(4 * DEPTH):
                pool.dma_start(g_rows, ln_g_rows[inst:inst + 1, :].partition_broadcast(P)).then_inc(sems["rows_in"], 16)
                pool.dma_start(b_rows, ln_b_rows[inst:inst + 1, :].partition_broadcast(P)).then_inc(sems["rows_in"], 16)
                rows += 32
                pool.wait_ge(sems["rows_in"], rows)
                pool.wait_ge(sems["ln_xh"], 2 * (inst + 1))
                for tt in range(TT):
                    step.did(G.tensor_tensor(x[:, tt, :], xh[:, tt, :], g_rows, ALU.mult))
                step.sync()
                for tt in range(TT):
                    i = G.tensor_tensor(x[:, tt, :], x[:, tt, :], b_rows, ALU.add)
                    if tt == 0:
                        step.did(i)
                i.then_inc(sems["x_updated"], 1)
                pool.wait_ge(sems["x_updated"], inst + 1)
                if inst == 1:
                    for half in range(2):
                        for h in range(NHEADS):
                            src = bass.AP(rpb.tensor, rpb.offset + h * 465 + (1 - half + 4) * 31 - 48,
                                          [[1, GRID], [31, 6], [1, GRID]])
                            pool.dma_start(grid_bias[half * GRID:(half + 1) * GRID, h], src).then_inc(sems["rpb_in"], 16)
                    pool.wait_ge(sems["rpb_in"], 16 * 2 * NHEADS)
                    gb = table("grid").unsqueeze(1).to_broadcast([P, NHEADS * 6, GRID])
                    flat = grid_bias.rearrange("p h j c -> p (h j) c")
                    G.tensor_tensor(flat, flat, gb, ALU.add).then_inc(sems["bias_ready"], 1)

            pool.dma_start(table("window"), head_rows.partition_broadcast(P)).then_inc(sems["gains_in"], 16)
            pool.wait_ge(sems["gains_in"], 16)
            for l in range(DEPTH):
                T, n = plan.tile, LEVELS + 2
                pool.wait_ge(sems["head_in"], 16 * 2)
                for j in range(2):
                    pool.wait_ge(*taken(T[("hz", l)] + j))
                v8 = lambda v: v.rearrange("p t (h d) -> p (t h) d", d=P)
                G.tensor_tensor(v8(hz), v8(hz), head_norm[:, l, 1, :].unsqueeze(1).to_broadcast([P, 8, P]),
                                ALU.mult).then_inc(sems["z_ready"], 1)
                for j in range(2):
                    pool.wait_ge(*taken(T[("z", l)] + j))
                G.tensor_tensor(v8(zs), v8(zs), head_norm[:, l, 0, :].unsqueeze(1).to_broadcast([P, 8, P]),
                                ALU.mult).then_inc(sems["z_ready"], 1)
                for j in range(2):
                    pool.wait_ge(*taken(T[("hq", l)] + j))
                q = hq.rearrange("p h s -> p (h s)")
                for i in range(n):
                    if i >= 2:
                        pool.wait_ge(*ready(T[("level", l, i - 2)] + 1))
                    if i == LEVELS:
                        G.tensor_copy(hKQ[:, i % 2, 1, :], q).then_inc(sems["hg_q"], 1)
                        continue
                    pool.wait_ge(sems["hg_exp"], (LEVELS + 1) * l + min(i, LEVELS) + 1)
                    G.tensor_tensor(hKQ[:, i % 2, 1, :], q, hE[:, i % 2, 1, :], ALU.mult).then_inc(sems["hg_q"], 1)
                for g in range(4):
                    pool.wait_ge(sems["dec"], 4 * l + g + 1)
                    mask = table("le" if g % 2 == 0 else "ge").unsqueeze(1).to_broadcast([P, 4, P])
                    G.tensor_tensor(heads2(qkd[:, g, :]), heads2(dec[:, g, :]), mask, ALU.mult).then_inc(sems["dec_masked"], 1)
                for v in range(LEVELS):
                    for g in range(4):
                        if v == 0:
                            pool.wait_ge(sems["a_ready"], 4 * l + g + 1)
                        elif v == 1:
                            pool.wait_ge(*ready(T[("A0", l)] + g))
                            pool.wait_ge(sems["x_first"], 4 * l + g + 1)
                        else:
                            pool.wait_ge(*ready(T[("Y", l, v - 1)] + g))
                        mask = levels[:, ((g % 2) * LEVELS + v) * P:((g % 2) * LEVELS + v + 1) * P]
                        G.tensor_tensor(heads2(alev[:, g, :]), heads2(amat[:, g, :]),
                                        mask.unsqueeze(1).to_broadcast([P, 4, P]), ALU.mult).then_inc(sems["a_level"], 1)
                    if v == 1:
                        for j in range(4):
                            pool.wait_ge(*taken(T[("kv_T", l)] + j))
                        pool.wait_ge(sems["gc_exp"], l + 1)
                        pool.wait_ge(sems["dec_masked"], 4 * l + 4)
                        for g in range(4):
                            for h in range(4):
                                c = (g // 2) * 8 + (g % 2) * 4 + h
                                hs = slice(h * P, (h + 1) * P)
                                i = G.tensor_scalar(vb[:, g, hs], v_tk[:, g // 2, hs], beta[:, c:c + 1], None, ALU.mult)
                                if h < 3:
                                    step.did(i)
                            i.then_inc(sems["vb"], 1)
                        for d in range(2):
                            for h in range(4):
                                c = d * 8 + d * 4 + h
                                hs = slice(h * P, (h + 1) * P)
                                i = G.tensor_scalar(kd[:, d, hs], k_tk[:, d, hs], kdf[:, c:c + 1], None, ALU.mult)
                                if h < 3:
                                    step.did(i)
                            i.then_inc(sems["kd"], 1)
            pool.wait_ge(sems["ln_xh"], 2 * 12)
            pool.dma_start(f_rows, final_norm.partition_broadcast(P)).then_inc(sems["final_in"], 16)
            pool.wait_ge(sems["final_in"], 16)
            pool.wait_ge(sems["final_rows"], 1)
            pool.dma_start(out.rearrange("b (t p) d -> p (b t) d", p=P), x[:, :, :]).then_inc(sems["out_stored"], 16)




def kernel(**inputs):
    import concourse.bacc as bacc
    from concourse.bass_utils import run_bass_kernel_spmd

    a = {k: np.asarray(v) for k, v in inputs.items()}
    tables = constants()
    arrays = {
        "weights": weight_stream(a),
        "x_in": a["x"],
        "mem_in": a["mem"],
        "consts": np.concatenate([tables[k] for k in CONSTANTS], axis=1),
        "cols": np.concatenate([columns(a["ln_g"].reshape(8, D)), columns(a["ln_b"].reshape(8, D)),
                                columns(np.stack([a["mix_norm_2"], a["ffn_norm_2"]], axis=1).reshape(4, D)),
                                columns(a["dn_conv_2"].reshape(10, 1536)),
                                columns(a["ffn_conv_2"].reshape(6, FF)), columns(a["ffn_conv_bias_2"]),
                                columns(a["hg_lb_logits_2"].reshape(4, 512))
                                ], axis=1),
        "ln_g_rows": a["ln_g"].reshape(8, D),
        "ln_b_rows": a["ln_b"].reshape(8, D),
        "gains": np.concatenate([a["ab_q_gain"], a["ab_k_gain"]], axis=1),
        "sink": a["ab_sink"],
        "rpb": a["c_rpb"][..., ::-1].reshape(-1),
        "hmask_in": hg_masks(),
        "wba_in": a["w_in_2"][:, :, 2048:2064].reshape(DEPTH, KT, P, 16).transpose(2, 0, 1, 3),
        "head_rows": np.stack([a["dn_norm_2"], a["hg_norm_2"]], axis=1).reshape(1, -1),
        "decay_rows": np.stack([a["dn_a_log_2"], a["dn_dt_bias_2"]], axis=1).reshape(1, -1),
        "final_norm": a["final_norm_2"].reshape(1, D),

    }
    nc = bacc.Bacc("TRN2", target_bir_lowering=False, num_devices=1)
    args = []
    for name in arrays:
        arrays[name] = np.ascontiguousarray(arrays[name])
        args.append(nc.dram_tensor(name, arrays[name].shape, mybir.dt.from_np(arrays[name].dtype),
                                   kind="ExternalInput").ap())
    args.append(nc.dram_tensor("out", (1, S, D), F32, kind="ExternalOutput").ap())
    build(nc, *args)
    result = run_bass_kernel_spmd(nc, [arrays], core_ids=[0])
    return result.results[0]["out"]
```

```python
from contextlib import ExitStack

import numpy as np

import concourse.bass as bass
from concourse import mybir

F32 = mybir.dt.float32
F32R = mybir.dt.float32r
U8 = mybir.dt.uint8
ALU = mybir.AluOpType
ACT = mybir.ActivationFunctionType
AX_X = mybir.AxisListType.X

P = 128
S = 256
D = 1024
KT = D // P
TT = S // P
FF = 2816
FT = FF // P
UW = 2048
HW = UW // 2
RING = 3
NB = 4
HD = 64
DEPTH = 2
ALPHA = (2.0 * DEPTH) ** 0.25
LN_EPS = 1e-5
EPS = 1e-6
NEG = -1.0e30
GRID = 64
NA_KH, NA_KW = 8, 16
WINDOW = 128
NHEADS = 16
FU = 33
DN_H = 4
LEVELS = 7



class Plan:

    def __init__(self):
        self.unit = {}
        self.tile = {}
        self.units = 0
        self.tiles = 0
        self.sets = {}
        self.ready = []
        self.plain = 0
        self.on_pool = set()
        self.stages()
        self.low = {}
        made = {"w_lo": 0, "w_lo_pool": 0}
        for u in range(self.units):
            for h in range(2):
                name = "w_lo_pool" if (u, h) in self.on_pool else "w_lo"
                made[name] += 1
                self.low[u, h] = (name, made[name])

    def from_units(self, name, n, per=1):
        self.unit[name] = self.units
        self.tile[name] = self.tiles
        for i in range(n):
            self.units += 1
            for _ in range(per):
                self.ready.append(("unit_used", self.units))
                self.tiles += 1

    def operand(self, name):
        self.sets[name] = len(self.sets)

    def from_chip(self, name, n):
        self.tile[name] = self.tiles
        for _ in range(n):
            self.plain += 1
            self.ready.append(("tile_ready", self.plain))
            self.tiles += 1

    def to_acc(self, name, n):
        self.unit[name] = self.units
        for _ in range(n):
            self.units += 1

    def ffn(self, name):
        self.unit[name] = self.units
        self.tile[name] = self.tiles
        order = "GG" + "GGD" * (FT // 2 - 1) + "D"
        for c in order:
            self.units += 1
            if c == "G":
                self.ready.append(("unit_used", self.units))
                self.tiles += 1

    def attention(self, name, groups, per):
        for g in range(groups + 3):
            if g < groups:
                self.from_chip((name, "S", g), per)
            if 2 <= g < groups + 2:
                self.from_chip((name, "T", g - 2), per)
            if g >= 3:
                self.from_chip((name, "O", g - 3), 1)

    def stages(self):
        self.from_chip("x", 4)
        self.operand("x")
        for i in range(DEPTH):
            self.ffn(("ffn", 2 * i))
            if i == 0:
                self.from_chip("mem", 4)
            self.from_chip(("ln", 4 * i), 4)
            self.operand(("ln", 4 * i))
            self.operand(("mem", i))
            if i == 0:
                self.from_units("ab_in", 6)
                self.from_units(("kv", 0), 8)
                self.from_chip("ab_T", 6)
                self.attention(("att", 0), 8, 2)
            else:
                self.from_units("c_in", 12)
                self.from_units(("kv", 1), 8)
                self.attention(("att", 2), 8, 2)
            self.operand(("out", 2 * i))
            self.to_acc(("out", 2 * i), 4)
            self.from_chip(("ln", 4 * i + 1), 4)
            self.operand(("ln", 4 * i + 1))
            self.from_units(("mq", i), 4)
            self.attention(("att", 2 * i + 1), 4, 1)
            self.operand(("out", 2 * i + 1))
            self.to_acc(("out", 2 * i + 1), 4)
            self.from_chip(("ln", 4 * i + 2), 4)
            self.operand(("ln", 4 * i + 2))
            self.ffn(("ffn", 2 * i + 1))
            self.from_chip(("ln", 4 * i + 3), 4)
            if i + 1 < DEPTH:
                self.operand(("ln", 4 * i + 3))

        for l in range(DEPTH):
            self.from_chip(("rms", 2 * l), 4)
            self.operand(("rms", 2 * l))
            self.from_units(("hq", l), 2)
            self.from_units(("hf", l), 4)
            self.from_units(("hi", l), 2)
            self.from_units(("hz", l), 2)
            self.from_units(("qkv", l), 6)
            self.from_chip(("ba", l), 1)
            self.from_units(("z", l), 2)
            for i in range(LEVELS + 2):
                if i < 8:
                    self.from_units(("gate", l, i), 1)
                self.from_chip(("level", l, i), 2)
            first, last = self.unit[("hi", l)] + 2, self.unit[("gate", l, 7)] + 2
            for u in range(first, last + 1):
                self.on_pool.add((u, 1))
                if u < first + 4:
                    self.on_pool.add((u, 0))
            self.from_chip(("l2", l), 1)
            self.from_chip(("hg_o", l), 2)
            self.from_chip(("gcum", l), 1)
            self.from_chip(("gcB", l), 4)
            self.from_chip(("l2B", l), 4)
            self.from_chip(("hg_T", l), 2)
            self.from_chip(("kv_T", l), 4)
            self.from_chip(("G", l), 2)
            self.from_chip(("QK", l), 2)
            self.from_chip(("A0", l), 4)
            for v in range(1, LEVELS):
                self.from_chip(("Y", l, v), 4)
                self.from_chip(("Z", l, v), 8 if v < LEVELS - 1 else 4)
            for name in ("vnA", "S", "kS", "vnB", "qS", "dn_o"):
                self.from_chip((name, l), 2)
            self.operand(("branch", l))
            self.from_units(("branch_hg", l), 2, per=2)
            self.from_chip(("dn_T", l), 2)
            self.from_units(("branch_dn", l), 2, per=2)
            self.operand(("out", 4 + l))
            self.to_acc(("out", 4 + l), 4)
            self.from_chip(("rms", 2 * l + 1), 4)
            self.operand(("rms", 2 * l + 1))
            self.ffn(("ffn", 4 + l))



def scores_per_attention(a):
    return 16 if a % 2 == 0 else 4


def first_score(a):
    return sum(scores_per_attention(b) for b in range(a))



def pack_features(w):
    c = w.shape[1] // 256
    return w.reshape(KT, P, c, 2, P).transpose(2, 1, 3, 0, 4).reshape(c, P, UW)


def pack_tokens(w):
    c = w.shape[1] // 256
    return w.reshape(KT, P, c, 256).transpose(2, 1, 0, 3).reshape(c, P, UW)


def pack_rows(w):
    n = w.shape[0] // 256
    return w.reshape(n, 2, P, D).transpose(0, 2, 1, 3).reshape(n, P, UW)


def pack_ffn(gate, up, down):
    gu = np.stack([gate.reshape(D, FT, P), up.reshape(D, FT, P)], axis=2).reshape(D, 2 * FF)
    gu = pack_features(gu)
    d = pack_rows(down)
    out = [gu[0:2]]
    for j in range(FT // 2 - 1):
        out += [gu[2 * j + 2:2 * j + 4], d[j:j + 1]]
    out.append(d[FT // 2 - 1:])
    return out


def pack_branch(w):
    return w.reshape(4, P, 2, 2, 256).transpose(2, 1, 3, 0, 4).reshape(2, P, UW)


def weight_stream(a):
    out = []
    for i in range(DEPTH):
        out += pack_ffn(a["ffn_w_gate"][i, 0], a["ffn_w_up"][i, 0], a["ffn_w_down"][i, 0])
        if i == 0:
            out.append(pack_tokens(a["ab_w_in"][0]))
        else:
            out.append(pack_features(a["c_w_in"][0][:, :2 * D]))
            out.append(pack_tokens(a["c_w_in"][0][:, 2 * D:]))
        out.append(pack_features(a["mem_w_kv"][i][:, :D]))
        out.append(pack_tokens(a["mem_w_kv"][i][:, D:]))
        out.append(pack_rows((a["ab_w_out"] if i == 0 else a["c_w_out"])[0]))
        out.append(pack_features(a["mem_w_q"][i]))
        out.append(pack_rows(a["mem_w_o"][i]))
        out += pack_ffn(a["ffn_w_gate"][i, 1], a["ffn_w_up"][i, 1], a["ffn_w_down"][i, 1])

    for l in range(DEPTH):
        w = a["w_in_2"][l]
        out.append(pack_features(w[:, 2064:3600]))
        out.append(pack_tokens(w[:, 3600:4624]))
        out.append(pack_features(w[:, 0:1536]))
        out.append(pack_tokens(w[:, 1536:2048]))
        out.append(pack_features(w[:, 4624:6672]))
        out.append(pack_branch(a["w_branch_hg_2"][l]))
        out.append(pack_branch(a["w_branch_dn_2"][l]))
        out.append(pack_rows(a["w_out_2"][l]))
        up = a["w_up_2"][l]
        out += pack_ffn(up[:, :FF], up[:, FF:], a["w_down_2"][l])

    return np.concatenate(out, axis=0)


def columns(v):
    n, w = v.shape
    return v.reshape(n, w // P, P).transpose(2, 0, 1).reshape(P, -1)


def level_mask(l):
    t = np.arange(P)[:, None]
    s = np.arange(P)[None, :]
    return ((t >> (l + 1)) == (s >> (l + 1))) & ((t >> l) % 2 == 1) & ((s >> l) % 2 == 0)


def constants():
    i = np.arange(P)
    out = {"ident": np.eye(P), "ones": np.ones((P, P)),
           "le": (i[:, None] <= i[None, :]) * 1.0, "ge": (i[:, None] >= i[None, :]) * 1.0}
    q = np.arange(S).reshape(TT, P).transpose(1, 0)[:, :, None]
    s = np.arange(S)[None, None, :]
    out["window"] = np.where(np.abs(s - q) <= WINDOW, 0.0, NEG).reshape(P, -1)
    c = (i % GRID)[:, None]
    start = np.clip(c - NA_KW // 2, 0, GRID - NA_KW)
    cc = np.arange(GRID)[None, ::-1]
    out["grid"] = np.where((cc >= start) & (cc < start + NA_KW), 0.0, NEG)
    t = np.arange(S)
    inv2 = 10000.0 ** (-np.arange(0, 32, 2, dtype=np.float32) / 32)
    inv1 = 10000.0 ** (-np.arange(0, 64, 2, dtype=np.float32) / 64)
    f = np.float32
    ang2 = np.concatenate([(t // GRID).astype(f)[:, None] * inv2.astype(f),
                           (t % GRID).astype(f)[:, None] * inv2.astype(f)], axis=1)
    ang1 = t.astype(f)[:, None] * inv1.astype(f)
    rope = np.stack([np.stack([np.cos(x), np.cos(x), -np.sin(x), np.sin(x)], 1) for x in (ang2, ang1)], 1)
    out["rope"] = rope.reshape(TT, P, 2 * 4 * 32).transpose(1, 0, 2).reshape(P, -1)
    return {k: np.ascontiguousarray(v, dtype=np.float32) for k, v in out.items()}


def offsets(parts):
    at, out = 0, {}
    for name, v in parts.items():
        out[name] = (at, v.shape[1])
        at += v.shape[1]
    return out, at


def hg_masks():
    m = [level_mask(l) | level_mask(l).T for l in range(LEVELS)] + [np.eye(P, dtype=bool)]
    m += [level_mask(l) for l in range(LEVELS)] + [level_mask(l).T for l in range(LEVELS)]
    return np.concatenate(m, axis=1).astype(np.float32)


CONSTANTS, CONSTANTS_W = offsets(constants())



class Progress:

    def __init__(self, eng, sem):
        self.eng, self.sem, self.n = eng, sem, 0

    def did(self, ins):
        ins.then_inc(self.sem, 1)
        self.n += 1

    def sync(self):
        self.eng.wait_ge(self.sem, self.n)

    def link(self, ins):
        self.did(ins)
        self.sync()


def build(nc, weights, x_in, mem_in, consts, cols, ln_g_rows, ln_b_rows, gains, sink, rpb, hmask_in, wba_in, head_rows, decay_rows, final_norm,
          out):
    plan = Plan()
    with ExitStack() as ctx:
        def sb(name, shape, dt=F32):
            return ctx.enter_context(nc.sbuf_tensor(name, shape, dt))

        def with_low(name, shape):
            at = -(-nc.sbuf_base // 32) * 32
            return sb(name, shape), nc.alloc_sbuf_tensor_at(name + "_lo", shape, F32R, offset=at)

        ring, ring_lo = with_low("ring", [P, RING, UW])
        x = sb("x", [P, TT, D])
        w_hi = sb("w_hi", [P, 4, HW], F32R)
        xT, xT_lo = with_low("xT", [P, KT, S])
        xT_hi = sb("xT_hi", [P, KT, S], F32R)
        hidden, hidden_lo = with_low("hidden", [P, 4, S])
        hidden_hi = sb("hidden_hi", [P, 4, S], F32R)
        const = sb("const", [P, CONSTANTS_W])
        WORK = 29696
        work = sb("work", [P, WORK])
        col = sb("col", [P, cols.shape[1]])
        bn = sb("bn", [P, 4, 6])
        mv = sb("mv", [P, TT, 2])
        var = sb("var", [P, TT])
        std = sb("std", [P, TT])
        rstd = sb("rstd", [P, TT])
        gain = sb("gain", [P, 2 * HD])
        sink_b = sb("sink_b", [P, 8])
        ssq = sb("ssq", [P, TT, 10])
        srt = sb("srt", [P, TT, 10])
        mx = sb("mx", [P, 16, TT])
        nmx = sb("nmx", [P, 16, TT])
        psum_p = sb("psum_p", [P, 16, TT])
        sink_e = sb("sink_e", [P, 16, TT])
        rec = sb("rec", [P, 16, TT])

        hmask = sb("hmask", [P, (LEVELS + 1) * P], U8)
        levels = sb("levels", [P, 2 * LEVELS * P], mybir.dt.bfloat16)
        wba, wba_lo = with_low("wba", [P, DEPTH, KT, 16])
        wba_hi = sb("wba_hi", [P, DEPTH, KT, 16], F32R)
        arow = sb("arow", [P, DEPTH, 2, 8])
        lb = sb("lb", [P, 2, 8])
        omlb = sb("omlb", [P, 2, 8])
        small = sb("small", [P, 17, 16])
        btot_t = sb("btot_t", [P, 4])


        def region(at, *shape):
            n = int(np.prod(shape))
            v = work[:, at:at + n]
            if len(shape) == 2:
                v = v.rearrange("p (a b) -> p a b", a=shape[0])
            if len(shape) == 3:
                v = v.rearrange("p (a b c) -> p a b c", a=shape[0], b=shape[1])
            return v

        def table(name):
            a, n = CONSTANTS[name]
            return const[:, a:a + n]

        ident = table("ident")
        xh = region(0, TT, D)
        qT = region(0, 8, S)
        kT = region(2048, 8, S)
        v_tok = region(4096, TT, D)
        memT = region(6144, KT, S)
        mkT = region(8192, KT, S)
        mv_tok = region(10240, TT, D)
        prob = region(12288, 6, TT, S)
        probT = region(15360, 4, TT, S)
        score = region(17408, 4, TT, S)
        oT = region(19456, KT, S)
        g_rows = region(21504, D)
        b_rows = region(22528, D)
        raw = region(23552, TT, 1536)
        mem_rows = region(23552, TT, D)
        roped = region(26624, TT, 2 * 768)
        rtmp = region(12288, 4, 2, 640)
        grid_bias = region(23552, NHEADS, 6, GRID)

        acc = [ctx.enter_context(nc.psum_tensor(f"acc{b}", [P, 512], F32)) for b in range(4)]
        bank = [ctx.enter_context(nc.psum_tensor(f"tile{b}", [P, 512], F32)) for b in range(NB)]

        names = ["const_in", "x_in", "mem_in", "unit_used", "tile_ready", "acc_ready",
                 "act_step", "dve_step", "pool_step", "out_stored",
                 "gate_silu", "bias_ready", "half_used", "w_hi", "w_lo", "w_lo_pool", "x_hi", "x_lo", "hidden_high", "hidden_split",
                 "ln_var", "ln_std", "ln_xh", "x_updated", "rows_in", "cols_in", "rpb_in",
                 "ab_raw", "ab_sqrt", "ab_ssq", "ab_roped",
                 "score_max", "prob_exp", "prob_norm"]

        names += ["head_in", "ba_hi", "ba_lo", "gains_in", "masks_in", "lb_arg", "lb_exp", "qkv_conv", "qkv_silu", "conv_done", "conv_step", "final_rows", "final_in",
                  "hg_num", "hg_log", "hg_arg", "hg_exp", "hg_k", "hg_q", "hg_ssq", "hg_std", "hg_out",
                  "l2_sq", "l2_inv", "l2_arg", "l2_sqrt", "l2_done",
                  "ba_y", "ba_sp", "g_ready", "gc_arg", "gc_exp", "dec", "dec_masked",
                  "a_ready", "a_level", "x_first", "vb", "kd", "nbe",
                  "z_ready", "dn_ssq", "dn_std", "dn_out", "gates_ready", "merged_dn", "merged"]
        hq = region(2048, 4, S)
        hk = region(3072, 2, 4, S)
        hF = region(5120, 2, 4, S)
        hE = region(7168, 2, 2, 4 * S)
        hKQ = region(11264, 2, 2, 4 * S)
        hatt = region(15360, TT, 4, S)
        hi = region(17408, TT, 512)
        dec = region(2048, 4, 512)
        amat = region(4096, 4, 512)
        qkd = region(6144, 4, 512)
        xinv = region(8192, 4, 512)
        winv = region(10240, 4, 512)
        yinv = region(12288, 4, 512)
        alev = region(14336, 4, 512)
        kd = region(16384, 2, 512)
        state = region(17408, 2, 512)
        vb, vn, qs, dn_o = dec, yinv, region(8192, 2, 512), region(4096, TT, 512)
        l2s = region(8192, 8, S)
        merged = region(18432, KT, S)
        mtmp = region(12288, KT, S)
        qkvT = region(18432, 12, S)
        v_tk = region(21504, TT, 512)
        k_tk = region(22528, TT, 512)
        gates = region(23552, 16, S)
        zs = region(27648, TT, 512)
        hz = region(28672, TT, 512)
        oT_hg = region(0, 4, S)
        oT_dn = region(1024, 4, S)
        conv = region(18432, 4, S)
        f_rows = region(21504, D)
        (eb, yb, ny, beta, gg, gc, eg, kdf, nbe, bss) = [small[:, i, :] for i in range(2, 12)]
        brs = small[:, 12, :]
        note = small[:, 13, :]
        l2n, l2i, ngc = [small[:, i, :] for i in range(14, 17)]
        ba32 = small[:, 0:2, :].rearrange("p a b -> p (a b)")
        btot = btot_t[:, :]

        head_norm = table("window").rearrange("p (l b d) -> p l b d", l=DEPTH, b=2)

        def before_rms(r):
            return plan.unit[("out", 4 + r // 2)] + 3 if r % 2 else plan.unit[("ffn", 3 + r // 2)] + 32

        def side(v, level, second):
            return v.rearrange("p (n u m) -> p n u m", u=2, m=1 << level)[:, :, int(second), :]

        def heads2(v):
            return v.rearrange("p (h s) -> p h s", s=P)

        sems = {n: ctx.enter_context(nc.semaphore(n)) for n in names}
        slot_full = [ctx.enter_context(nc.semaphore(f"slot_full{s}")) for s in range(RING)]
        tile_taken = [ctx.enter_context(nc.semaphore(f"tile_taken{b}")) for b in range(NB)]

        def ready(t):
            name, value = plan.ready[t]
            return sems[name], value

        def taken(t):
            return tile_taken[t % NB], t // NB + 1

        def pair(buf, j):
            return buf[:, 2 * j:2 * j + 2, :].rearrange("p a b -> p (a b)")

        def tile_of_step(m):
            if m < 2:
                return m
            if m == FU - 1 or (m - 2) % 3 == 2:
                return None
            return 2 + 2 * ((m - 2) // 3) + (m - 2) % 3

        def whole(v):
            return v.rearrange("p a b -> p (a b)")

        def half_of(buf, u, h):
            return buf[:, u % RING, h * HW:(h + 1) * HW]

        def high_of(u, h):
            return w_hi[:, 2 * (u % 2) + h, :]

        def run_steps(eng, do):
            for m in range(2):
                do(m)
            with eng.Fori(0, 4) as lap:
                for m in range(2, 8):
                    do(m, lap)
            for m in range(26, FU):
                do(m)

        block = ctx.enter_context(nc.Block())

        @block.sync
        def _(sp):
            sp.dma_start(x[:, :, :], x_in.rearrange("b (t p) d -> p (b t) d", p=P)).then_inc(sems["x_in"], 16)
            for s in range(RING):
                sp.dma_start(ring[:, s, :], weights[s]).then_inc(slot_full[s], 16)
            laps = plan.units // RING
            with sp.Fori(0, laps - 1) as lap:
                for s in range(RING):
                    sp.wait_ge(sems["unit_used"], lap * RING + s + 1)
                    src = weights[bass.ds(lap * RING + (RING + s), 1)].rearrange("u p n -> p (u n)")
                    sp.dma_start(ring[:, s, :], src).then_inc(slot_full[s], 16)
            for u in range(laps * RING, plan.units):
                sp.wait_ge(sems["unit_used"], u - RING + 1)
                sp.dma_start(ring[:, u % RING, :], weights[u]).then_inc(slot_full[u % RING], 16)
            sp.wait_ge(sems["out_stored"], 16)

        @block.tensor
        def _(pe):
            mm = nc.tensor.matmul

            def open_tile(t, more=0):
                if t >= NB:
                    pe.wait_ge(tile_taken[t % NB], more + t // NB)
                return bank[t % NB]

            def keep_warm(ps, n):
                for _ in range(n):
                    mm(ps[:, :], ident, const[:, 0:512], start=True, stop=True)

            THREE = ((0, 0), (0, 1), (1, 0))
            x2 = (xT_hi, xT_lo)
            h2 = (hidden_hi, hidden_lo)

            def open_half(u, h, k, more=0):
                name, value = plan.low[u, h]
                pe.wait_ge(sems[name], more * 12 + value)
                return [v.rearrange("p (k c) -> p k c", k=k) for v in (high_of(u, h), half_of(ring_lo, u, h))]

            def await_x(name, q):
                pe.wait_ge(sems["x_lo"], 4 * plan.sets[name] + q + 1)

            def features(u, t, x_set=None, more=0):
                for f in range(2):
                    w = open_half(u, f, KT, more)
                    if f == 0:
                        ps = open_tile(t, more)
                    for k in range(KT):
                        if x_set is not None and f == 0 and k % 2 == 0:
                            await_x(x_set, k // 2)
                        for i, (a, b) in enumerate(THREE):
                            j = mm(ps[:, f * S:(f + 1) * S], w[a][:, k, :], x2[b][:, k, :],
                                   start=(k == 0 and i == 0), stop=(k == KT - 1 and i == 2))
                    j.then_inc(sems["unit_used" if f else "half_used"], 1)

            def tokens(u, t, x_set=None):
                w = [open_half(u, h, KT // 2) for h in range(2)]
                ps = open_tile(t)
                for tt in range(TT):
                    for k in range(KT):
                        if x_set is not None and tt == 0 and k % 2 == 0:
                            await_x(x_set, k // 2)
                        for i, (a, b) in enumerate(THREE):
                            j = mm(ps[:, tt * 256:(tt + 1) * 256], x2[b][:, k, tt * P:(tt + 1) * P],
                                   w[k // 4][a][:, k % 4, :], start=(k == 0 and i == 0),
                                   stop=(k == KT - 1 and i == 2))
                        if tt == 1 and k == 3:
                            j.then_inc(sems["half_used"], 1)
                j.then_inc(sems["unit_used"], 1)

            def to_acc(u, src, at, first, last, more=0):
                if last:
                    w = [open_half(u, k, 1) for k in range(2)]
                    order = [(b, k) for b in range(4) for k in range(2)]
                else:
                    w = [None, None]
                    order = [(b, k) for k in range(2) for b in range(4)]
                for b, k in order:
                    if w[k] is None:
                        w[k] = open_half(u, k, 1, more)
                    for i, (c, d) in enumerate(THREE):
                        j = mm(acc[b][:, :], src[d][:, at + k, (b // 2) * P:(b // 2 + 1) * P],
                               w[k][c][:, 0, (b % 2) * 512:(b % 2 + 1) * 512],
                               start=(first and k == 0 and i == 0), stop=(last and k == 1 and i == 2))
                    if last and k == 1 and b < 3:
                        j.then_inc(sems["acc_ready"], 1)
                    if b == 3:
                        j.then_inc(sems["unit_used" if k else "half_used"], 1)

            def transposes(t0, src):
                for q in range(4):
                    ps = open_tile(t0 + q)
                    for k in range(2):
                        for tt in range(TT):
                            c = (2 * q + k) * P
                            i = nc.tensor.transpose(ps[:, k * S + tt * P:k * S + (tt + 1) * P],
                                                    src[:, tt, c:c + P], ident)
                    i.then_inc(sems["tile_ready"], 1)

            def await_features(t0):
                for q in range(4):
                    pe.wait_ge(*taken(t0 + q))

            def ffn(n, x_set):
                u0, t0 = plan.unit[("ffn", n)], plan.tile[("ffn", n)]

                def down(j, u, first, last, more=0):
                    pe.wait_ge(sems["hidden_split"], more * 4 + FT * n + 2 * j + 2)
                    to_acc(u, h2, 2 * j % 4, first, last, more)

                features(u0, t0, x_set)
                features(u0 + 1, t0 + 1)

                def lap(it):
                    for half in range(2):
                        u, t = u0 + 2 + 3 * half, t0 + 2 + 2 * half
                        features(u, t, more=it)
                        features(u + 1, t + 1, more=it)
                        down(half, u + 2, isinstance(it, int) and half == 0, False, it)
                lap(0)
                with pe.Fori(1, (FT // 2 - 1) // 2) as it:
                    lap(it)
                down(FT // 2 - 1, u0 + FU - 1, False, True)

            def norm_transposes(key, inst, warm=5):
                keep_warm(open_tile(plan.tile[key]), warm)
                pe.wait_ge(sems["ln_xh"], 2 * (inst + 1))
                transposes(plan.tile[key], xh)
                await_features(plan.tile[key])

            def out_proj(n):
                u0 = plan.unit[("out", n)]
                keep_warm(acc[0], 2)
                for j in range(4):
                    await_x(("out", n), j)
                    to_acc(u0 + j, x2, 2 * j, j == 0, j == 3)

            def attention(a, groups, per, q_of, k_of, v_of):
                key = ("att", a)
                e0 = first_score(a)
                for g in range(groups + 3):
                    if g < groups:
                        for j in range(per):
                            e = g * per + j
                            ps = open_tile(plan.tile[(key, "S", g)] + j)
                            qs, ks = q_of(e), k_of(e)
                            for tt in range(TT):
                                for m in range(len(qs)):
                                    i = mm(ps[:, tt * S:(tt + 1) * S], qs[m][:, tt * P:(tt + 1) * P],
                                           ks[m], start=(m == 0), stop=(m == len(qs) - 1))
                            i.then_inc(sems["tile_ready"], 1)
                    if a == 2 and g == 2:
                        keep_warm(acc[0], 4)
                    if 2 <= g < groups + 2:
                        for j in range(per):
                            e = (g - 2) * per + j
                            ps = open_tile(plan.tile[(key, "T", g - 2)] + j)
                            pe.wait_ge(sems["prob_norm"], e0 + e + 1)
                            for st in range(TT):
                                for tt in range(TT):
                                    i = nc.tensor.transpose(
                                        ps[:, st * S + tt * P:st * S + (tt + 1) * P],
                                        prob[:, e % 6, tt, st * P:(st + 1) * P], ident)
                            i.then_inc(sems["tile_ready"], 1)
                    if g >= 3:
                        t = plan.tile[(key, "O", g - 3)]
                        ps = open_tile(t)
                        for j in range(2):
                            e = (g - 3) * per + (j if per == 2 else 0)
                            pe.wait_ge(*taken(plan.tile[(key, "T", g - 3)] + e % per))
                            for st in range(TT):
                                dst = ps[HD * j:HD * (j + 1), 0:S] if per == 2 else ps[:, j * S:(j + 1) * S]
                                i = mm(dst, v_of(e, j)[:, st, :], probT[:, e % 4, st, :],
                                       start=(st == 0), stop=(st == TT - 1))
                        i.then_inc(sems["tile_ready"], 1)
                for g in range(groups):
                    pe.wait_ge(*taken(plan.tile[(key, "O", g)]))

            pe.wait_ge(sems["const_in"], 16)
            pe.wait_ge(sems["x_in"], 16)
            transposes(plan.tile["x"], x)
            for i in range(DEPTH):
                ffn(2 * i, "x" if i == 0 else ("ln", 4 * i - 1))
                if i == 0:
                    pe.wait_ge(sems["mem_in"], 16)
                    transposes(plan.tile["mem"], mem_rows)
                norm_transposes(("ln", 4 * i), 4 * i, 3 if i == 0 else 5)
                if i == 0:
                    for j in range(6):
                        tokens(plan.unit["ab_in"] + j, plan.tile["ab_in"] + j, ("ln", 0) if j == 0 else None)
                else:
                    for j in range(8):
                        features(plan.unit["c_in"] + j, plan.tile["c_in"] + j, ("ln", 4) if j == 0 else None)
                    for j in range(8, 12):
                        tokens(plan.unit["c_in"] + j, plan.tile["c_in"] + j)
                keep_warm(acc[0], 2 + i)
                for j in range(4):
                    features(plan.unit[("kv", i)] + j, plan.tile[("kv", i)] + j, ("mem", i) if j == 0 else None)
                for j in range(4, 8):
                    tokens(plan.unit[("kv", i)] + j, plan.tile[("kv", i)] + j)
                if i == 0:
                    t0 = plan.tile["ab_T"]
                    pe.wait_ge(sems["ab_roped"], 2)
                    for q in range(6):
                        ps = open_tile(t0 + q)
                        for b in range(2):
                            for tt in range(TT):
                                if q < 4:
                                    c = (q // 2) * 768 + ((q % 2) * 2 + b) * P
                                else:
                                    c = (q - 4) * 768 + 512 + b * P
                                i2 = nc.tensor.transpose(ps[:, b * S + tt * P:b * S + (tt + 1) * P],
                                                         roped[:, tt, c:c + P], ident)
                        i2.then_inc(sems["tile_ready"], 1)
                    for q in range(6):
                        pe.wait_ge(*taken(t0 + q))
                    attention(0, 8, 2,
                              lambda e: [qT[HD * (e % 2):HD * (e % 2) + HD, e // 2, :]],
                              lambda e: [kT[HD * (e % 2):HD * (e % 2) + HD, e // 4, :]],
                              lambda e, j: raw[:, :, (e // 8) * 768 + 640 + (e // 4 % 2) * HD:
                                               (e // 8) * 768 + 640 + (e // 4 % 2) * HD + HD])
                else:
                    for j in range(12):
                        pe.wait_ge(*taken(plan.tile["c_in"] + j))
                    attention(2, 8, 2,
                              lambda e: [qT[HD * (e % 2):HD * (e % 2) + HD, e // 2, :]],
                              lambda e: [kT[HD * (e % 2):HD * (e % 2) + HD, e // 2, :]],
                              lambda e, j: v_tok[:, :, e * HD:(e + 1) * HD])
                out_proj(2 * i)
                norm_transposes(("ln", 4 * i + 1), 4 * i + 1)
                for j in range(4):
                    features(plan.unit[("mq", i)] + j, plan.tile[("mq", i)] + j,
                             ("ln", 4 * i + 1) if j == 0 else None)
                keep_warm(acc[0], 4)
                for j in range(4):
                    pe.wait_ge(*taken(plan.tile[("mq", i)] + j))
                for j in range(8):
                    pe.wait_ge(*taken(plan.tile[("kv", i)] + j))
                attention(2 * i + 1, 4, 1,
                          lambda e: [qT[:, 2 * e + m, :] for m in range(2)],
                          lambda e: [mkT[:, 2 * e + m, :] for m in range(2)],
                          lambda e, j: mv_tok[:, :, (2 * e + j) * P:(2 * e + j + 1) * P])
                out_proj(2 * i + 1)
                norm_transposes(("ln", 4 * i + 2), 4 * i + 2)
                ffn(2 * i + 1, ("ln", 4 * i + 2))
                norm_transposes(("ln", 4 * i + 3), 4 * i + 3)

            def small_tokens(l):
                pe.wait_ge(sems["ba_lo"], 1)
                ps = open_tile(plan.tile[("ba", l)])
                for tt in range(TT):
                    for k in range(KT):
                        for part, (c, d) in enumerate(THREE):
                            i = mm(ps[:, tt * 16:(tt + 1) * 16], x2[d][:, k, tt * P:(tt + 1) * P],
                                   (wba_hi, wba_lo)[c][:, l, k, :], start=(k + part == 0),
                                   stop=(k == KT - 1 and part == 2))
                i.then_inc(sems["tile_ready"], 1)

            def per_head(t, lhsT, rhs, part=lambda out: out):
                ps = open_tile(t)
                for h in range(4):
                    i = mm(part(ps[:, h * P:(h + 1) * P]), lhsT(h), rhs(h), start=True, stop=True)
                i.then_inc(sems["tile_ready"], 1)

            def hd(h):
                return slice(h * P, (h + 1) * P)

            def turn4(t, src):
                ps = open_tile(t)
                for b in range(4):
                    i = nc.tensor.transpose(ps[:, b * P:(b + 1) * P], src(b), ident)
                i.then_inc(sems["tile_ready"], 1)

            def mixer2(l):
                U, T = plan.unit, plan.tile
                for j in range(2):
                    features(U[("hq", l)] + j, T[("hq", l)] + j, ("rms", 2 * l) if j == 0 else None)
                for j in range(4):
                    features(U[("hf", l)] + j, T[("hf", l)] + j)
                for j in range(2):
                    tokens(U[("hi", l)] + j, T[("hi", l)] + j)
                for j in range(2):
                    tokens(U[("hz", l)] + j, T[("hz", l)] + j)
                for j in range(6):
                    features(U[("qkv", l)] + j, T[("qkv", l)] + j)
                small_tokens(l)
                for j in range(2):
                    tokens(U[("z", l)] + j, T[("z", l)] + j)
                for i in range(LEVELS + 2):
                    if i < 8:
                        features(U[("gate", l, i)], T[("gate", l, i)])
                    if i in (0, LEVELS + 1):
                        keep_warm(open_tile(T[("level", l, i)]), 5 if i == 0 else 4)
                    pe.wait_ge(sems["hg_k"], (LEVELS + 2) * l + i + 1)
                    pe.wait_ge(sems["hg_q"], (LEVELS + 2) * l + i + 1)
                    K, Q = hKQ[:, i % 2, 0], hKQ[:, i % 2, 1]
                    for c in range(2):
                        s, t = (c, c) if i <= LEVELS else (c, 1 - c)
                        per_head(T[("level", l, i)] + c,
                                 lambda h: K[:, h * S + s * P:h * S + (s + 1) * P],
                                 lambda h: Q[:, h * S + t * P:h * S + (t + 1) * P])
                pe.wait_ge(sems["l2_sq"], 4 * l + 4)
                ps = open_tile(T[("l2", l)])
                for c in range(16):
                    i = mm(ps[:, c:c + 1], l2s[:, c // 2, (c % 2) * P:(c % 2 + 1) * P], table("ones")[:, 0:1],
                           start=True, stop=True)
                i.then_inc(sems["tile_ready"], 1)
                for i in range(LEVELS + 2):
                    for c in range(2):
                        pe.wait_ge(*taken(T[("level", l, i)] + c))
                for tt in range(TT):
                    ps = open_tile(T[("hg_o", l)] + tt)
                    for h in range(4):
                        for st in range(TT):
                            i = mm(ps[:, hd(h)], hatt[:, st, h, tt * P:(tt + 1) * P], hi[:, st, hd(h)],
                                   start=(st == 0), stop=(st == TT - 1))
                    i.then_inc(sems["tile_ready"], 1)
                pe.wait_ge(sems["g_ready"], l + 1)
                ps = open_tile(T[("gcum", l)])
                sums = [table("le"), table("ge")]
                for tt in range(TT):
                    for d in range(2):
                        c = tt * 8 + d * 4
                        mm(ps[:, c:c + 4], sums[d], gg[:, c:c + 4], start=True, stop=True)
                i = mm(ps[:, 16:32], table("ones"), gg[:, :], start=True, stop=True)
                i.then_inc(sems["tile_ready"], 1)
                for g in range(4):
                    tt, d = g // 2, g % 2
                    per_head(T[("gcB", l)] + g,
                             lambda h: gg[:, tt * 8 + d * 4 + h:tt * 8 + d * 4 + h + 1].to_broadcast([P, P]),
                             lambda h: sums[d])
                keep_warm(acc[0], 3)
                pe.wait_ge(sems["l2_inv"], l + 1)
                for j in range(4):
                    per_head(T[("l2B", l)] + j, lambda c: l2i[:, 4 * j + c:4 * j + c + 1].to_broadcast([P, P]),
                             lambda c: ident)
                pe.wait_ge(sems["hg_out"], l + 1)
                for j in range(2):
                    turn4(T[("hg_T", l)] + j, lambda b: hz[:, b % 2, hd(2 * j + b // 2)])
                pe.wait_ge(sems["l2_done"], l + 1)
                for j in range(4):
                    turn4(T[("kv_T", l)] + j, lambda b: qkvT[:, 4 + 4 * (j // 2) + b, (j % 2) * P:(j % 2 + 1) * P])
                for tt in range(TT):
                    per_head(T[("G", l)] + tt, lambda h: qkvT[:, 4 + h, tt * P:(tt + 1) * P],
                             lambda h: qkvT[:, 4 + h, tt * P:(tt + 1) * P])
                for tt in range(TT):
                    per_head(T[("QK", l)] + tt, lambda h: qkvT[:, 4 + h, tt * P:(tt + 1) * P],
                             lambda h: qkvT[:, h, tt * P:(tt + 1) * P])
                for g in range(4):
                    pe.wait_ge(sems["a_level"], 4 * LEVELS * l + g + 1)
                    turn4(T[("A0", l)] + g, lambda h: alev[:, g, hd(h)])
                for v in range(1, LEVELS):
                    for g in range(4):
                        before = T[("A0", l)] + g if v == 1 else T[("Z", l, v - 1)] + 2 * g
                        pe.wait_ge(*taken(before))
                        pe.wait_ge(sems["a_level"], 4 * LEVELS * l + 4 * v + g + 1)
                        per_head(T[("Y", l, v)] + g, lambda h: alev[:, g, hd(h)], lambda h: winv[:, g, hd(h)])
                    for g in range(4):
                        if v == 1:
                            pe.wait_ge(sems["x_first"], 4 * l + g + 1)
                        else:
                            pe.wait_ge(*taken(T[("Z", l, v - 1)] + 2 * g + 1))
                        pe.wait_ge(*taken(T[("Y", l, v)] + g))
                        z = T[("Z", l, v)] + (2 * g if v < LEVELS - 1 else g)
                        forward = g % 2 == 0
                        per_head(z, lambda h: xinv[:, g, hd(h)], lambda h: side(yinv[:, g, hd(h)], v, forward),
                                 lambda out: side(out, v, forward))
                        if v < LEVELS - 1:
                            per_head(z + 1, lambda h: yinv[:, g, hd(h)], lambda h: side(xinv[:, g, hd(h)], v, not forward),
                                     lambda out: side(out, v, not forward))
                for d in range(2):
                    ga = 3 * d
                    pe.wait_ge(sems["vb"], 4 * l + ga + 1)
                    pe.wait_ge(*taken(T[("Z", l, LEVELS - 1)] + ga))
                    per_head(T[("vnA", l)] + d, lambda h: winv[:, ga, hd(h)], lambda h: vb[:, ga, hd(h)])
                for d in range(2):
                    pe.wait_ge(sems["kd"], 2 * l + d + 1)
                    pe.wait_ge(*taken(T[("vnA", l)] + d))
                    per_head(T[("S", l)] + d, lambda h: kd[:, d, hd(h)], lambda h: vn[:, 3 * d, hd(h)])
                for d in range(2):
                    tb = 1 - d
                    pe.wait_ge(*taken(T[("S", l)] + d))
                    per_head(T[("kS", l)] + d, lambda h: qkvT[:, 4 + h, tb * P:(tb + 1) * P],
                             lambda h: state[:, d, hd(h)])
                for d in range(2):
                    gb = 2 - d
                    pe.wait_ge(*taken(T[("kS", l)] + d))
                    pe.wait_ge(*taken(T[("Z", l, LEVELS - 1)] + gb))
                    per_head(T[("vnB", l)] + d, lambda h: winv[:, gb, hd(h)], lambda h: vb[:, gb, hd(h)])
                for d in range(2):
                    tb = 1 - d
                    per_head(T[("qS", l)] + d, lambda h: qkvT[:, h, tb * P:(tb + 1) * P],
                             lambda h: state[:, d, hd(h)])
                for d in range(2):
                    pe.wait_ge(*taken(T[("vnB", l)] + d))
                for tt in range(TT):
                    pe.wait_ge(*taken(T[("QK", l)] + tt))
                    ps = open_tile(T[("dn_o", l)] + tt)
                    for h in range(4):
                        for d in range(2):
                            i = mm(ps[:, hd(h)], qkd[:, 2 * tt + d, hd(h)], vn[:, 2 * tt + d, hd(h)],
                                   start=(d == 0), stop=(d == 1))
                    i.then_inc(sems["tile_ready"], 1)
                def branch(name, q0):
                    for j in range(2):
                        for half in range(2):
                            w = open_half(U[(name, l)] + j, half, 4)
                            ps = open_tile(T[(name, l)] + 2 * j + half)
                            for f in range(2):
                                for k in range(4):
                                    if j + half + f == 0 and k % 2 == 0:
                                        await_x(("branch", l), q0 + k // 2)
                                    for p, (c, d) in enumerate(THREE):
                                        i = mm(ps[:, f * S:(f + 1) * S], w[c][:, k, f * P:(f + 1) * P],
                                               x2[d][:, 2 * q0 + k, :], start=(k + p == 0), stop=(k == 3 and p == 2))
                            i.then_inc(sems["unit_used" if half else "half_used"], 1)

                branch("branch_hg", 0)
                pe.wait_ge(sems["dn_out"], l + 1)
                for j in range(2):
                    turn4(T[("dn_T", l)] + j, lambda b: dn_o[:, b % 2, hd(2 * j + b // 2)])
                keep_warm(acc[0], 2)
                branch("branch_dn", 2)
                out_proj(4 + l)

            pe.wait_ge(sems["head_in"], 16 * 2)
            for l in range(DEPTH):
                norm_transposes(("rms", 2 * l), 8 + 2 * l)
                mixer2(l)
                norm_transposes(("rms", 2 * l + 1), 9 + 2 * l)
                ffn(4 + l, ("rms", 2 * l + 1))


        @block.scalar
        def _(act):
            A = nc.scalar.activation
            step = Progress(act, sems["act_step"])

            act.dma_start(const[:, :], consts).then_inc(sems["const_in"], 16)
            act.dma_start(col[:, :], cols).then_inc(sems["cols_in"], 16)
            act.dma_start(gain[:, :], gains.partition_broadcast(P)).then_inc(sems["cols_in"], 16)
            act.dma_start(sink_b[:, :], sink.partition_broadcast(P)).then_inc(sems["cols_in"], 16)

            def take(t, dst, src=None):
                act.wait_ge(*ready(t))
                ps = bank[t % NB]
                A(dst, ps[:, :] if src is None else src(ps), ACT.Copy).then_inc(tile_taken[t % NB], 1)

            def take_scaled(t, k, scale, bias=None):
                act.wait_ge(*ready(t))
                for j in range(2):
                    i = A(xT[:, k + j, :], bank[t % NB][:, j * S:(j + 1) * S], ACT.Identity,
                          scale=scale[:, k + j:k + j + 1], bias=bias[:, k + j:k + j + 1] if bias is not None else 0.0)
                    if j == 0:
                        step.did(i)
                i.then_inc(tile_taken[t % NB], 1)

            def split_pair(name, q, src):
                A(pair(xT_hi, q), src, ACT.Copy).then_inc(sems["x_hi"], 1)

            def split_norm(name, t0):
                for q in range(4):
                    act.wait_ge(*taken(t0 + q))
                    split_pair(name, q, pair(xT, q))

            def split_out(a, per):
                for q in range(4):
                    act.wait_ge(*taken(plan.tile[(("att", a), "O", per * q + per - 1)]))
                    split_pair(("out", a), q, pair(oT, q))

            def split_half(u, h, more=0):
                if h == 0:
                    act.wait_ge(slot_full[u % RING], more * 32 + 16 * (u // RING + 1))
                if u >= 2:
                    act.wait_ge(sems["unit_used" if h else "half_used"], more * 6 + u - 1)
                A(high_of(u, h), half_of(ring, u, h), ACT.Copy).then_inc(sems["w_hi"], 1)

            def feed(u, more=0):
                if u + 2 < plan.units:
                    split_half(u + 2, 0, more)
                    split_half(u + 2, 1, more)

            def ffn(n, conv_first=False):
                t0, u0 = plan.tile[("ffn", n)], plan.unit[("ffn", n)]

                def gate(f, more):
                    if conv_first:
                        act.wait_ge(sems["conv_done"], more * 4 + FT * (n - 4) + f + 1)
                        src = conv[:, f % 4, :]
                    else:
                        act.wait_ge(sems["unit_used"], more * 6 + plan.ready[t0 + f][1])
                        src = bank[(t0 + f) % NB][:, 0:S]
                    A(hidden[:, f % 4, :], src, ACT.Silu).then_inc(sems["gate_silu"], 1)

                def ffn_step(m, more=0):
                    f = tile_of_step(m)
                    if m + 1 < FU:
                        feed(u0 + m, more)
                    if f is not None:
                        gate(f, more)
                run_steps(act, ffn_step)

            def norm(inst, key, last_unit):
                act.wait_ge(sems["ln_var"], inst + 1)
                A(std[:, :], var[:, :], ACT.Sqrt).then_inc(sems["ln_std"], 1)
                t0 = plan.tile[key]
                gcol = col[:, inst * KT:(inst + 1) * KT]
                bcol = col[:, (8 + inst) * KT:(9 + inst) * KT]
                for q in (0, 2):
                    take_scaled(t0 + q, 2 * q, gcol, bcol)
                if key in plan.sets:
                    split_norm(key, t0)
                feed(last_unit)

            def attention(a, groups, per, scale, mode, dst):
                key = ("att", a)
                e0 = first_score(a)
                for g in range(groups + 3):
                    if g < groups:
                        for j in range(per):
                            e = g * per + j
                            t = plan.tile[(key, "S", g)] + j
                            act.wait_ge(sems["score_max"], e0 + e + 1)
                            masked = mode(e)
                            src = score[:, e % 4, :, :] if masked else bank[t % NB][:, :].rearrange("p (t s) -> p t s", t=TT)
                            for tt in range(TT):
                                i = A(prob[:, e % 6, tt, :], src[:, tt, :], ACT.Exp,
                                      bias=nmx[:, e, tt:tt + 1], scale=1.0 if masked else scale,
                                      accum_out=psum_p[:, e, tt:tt + 1])
                                if tt == 0:
                                    step.did(i)
                            if not masked:
                                i.then_inc(tile_taken[t % NB], 1)
                            elif masked == "bias":
                                i.then_inc(sems["prob_exp"], 1)
                            else:
                                step.did(i)
                                for tt in range(TT):
                                    i = A(sink_e[:, e, tt:tt + 1], sink_b[:, e - 8:e - 7], ACT.Exp,
                                          bias=nmx[:, e, tt:tt + 1])
                                    if tt == 0:
                                        step.did(i)
                                i.then_inc(sems["prob_exp"], 1)
                    if 2 <= g < groups + 2:
                        for j in range(per):
                            e = (g - 2) * per + j
                            t = plan.tile[(key, "T", g - 2)] + j
                            take(t, probT[:, e % 4, :, :].rearrange("p a b -> p (a b)"))
                    if g >= 3:
                        t = plan.tile[(key, "O", g - 3)]
                        if per == 2:
                            take(t, oT[:, g - 3, :], lambda ps: ps[:, 0:S])
                        else:
                            take(t, oT[:, 2 * (g - 3):2 * (g - 3) + 2, :].rearrange("p a b -> p (a b)"))

            def feed_stage(name, n):
                for j in range(n):
                    feed(plan.unit[name] + j)

            for q in range(4):
                take(plan.tile["x"] + q, pair(xT, q))
            for h in range(2):
                split_half(0, h)
            split_norm("x", plan.tile["x"])
            for h in range(2):
                split_half(1, h)
            act.dma_start(mem_rows, mem_in.rearrange("b (t p) d -> p (b t) d", p=P)).then_inc(sems["mem_in"], 16)
            act.dma_start(region(18432, (3 * LEVELS + 1) * P), hmask_in).then_inc(sems["masks_in"], 16)
            act.dma_start(wba[:, :, :, :], wba_in).then_inc(sems["head_in"], 16)
            act.dma_start(arow[:, :, :, :].rearrange("p a b c -> p (a b c)"),
                          decay_rows.partition_broadcast(P)).then_inc(sems["head_in"], 16)
            act.wait_ge(sems["cols_in"], 48)
            for i in range(DEPTH):
                ffn(2 * i)
                if i == 0:
                    for q in range(4):
                        take(plan.tile["mem"] + q, pair(memT, q))
                norm(4 * i, ("ln", 4 * i), plan.unit[("ffn", 2 * i)] + 32)
                name, n = ("ab_in", 6) if i == 0 else ("c_in", 12)
                for j in range(n):
                    feed(plan.unit[name] + j)
                    if i == 0:
                        take(plan.tile["ab_in"] + j, raw[:, :, j * 256:(j + 1) * 256])
                        continue
                    if j == 3:
                        act.wait_ge(sems["x_updated"], 4 * i + 1)
                    for m in range(0 if j == 3 else j, j + 1 if j >= 3 else j):
                        dst = pair(qT, m) if m < 4 else pair(kT, m - 4) if m < 8 else \
                            v_tok[:, :, (m - 8) * 256:(m - 7) * 256]
                        take(plan.tile["c_in"] + m, dst)
                act.wait_ge(sems["unit_used"], plan.unit[name] + n)
                for q in range(4):
                    act.wait_ge(*taken(plan.tile["mem"] + q))
                    split_pair(("mem", i), q, pair(memT, q))
                for j in range(8):
                    feed(plan.unit[("kv", i)] + j)
                    dst = pair(mkT, j) if j < 4 else mv_tok[:, :, (j - 4) * 256:(j - 3) * 256]
                    take(plan.tile[("kv", i)] + j, dst)
                    if i == 0 and j == 1:
                        act.wait_ge(sems["ab_ssq"], 1)
                        A(srt[:, :, :], ssq[:, :, :], ACT.Sqrt).then_inc(sems["ab_sqrt"], 1)
                if i == 0:
                    act.wait_ge(sems["x_updated"], 1)
                    for q in range(6):
                        take(plan.tile["ab_T"] + q, pair(qT, q) if q < 4 else pair(kT, q - 4))
                    attention(0, 8, 2, HD ** -0.5, lambda e: None if e < 8 else "sink", oT)
                else:
                    attention(2, 8, 2, HD ** -0.5, lambda e: "bias", oT)
                split_out(2 * i, 2)
                feed_stage(("out", 2 * i), 3)
                norm(4 * i + 1, ("ln", 4 * i + 1), plan.unit[("out", 2 * i)] + 3)
                feed_stage(("mq", i), 4)
                act.wait_ge(sems["x_updated"], 4 * i + 2)
                for j in range(4):
                    take(plan.tile[("mq", i)] + j, pair(qT, j))
                attention(2 * i + 1, 4, 1, 256 ** -0.5, lambda e: None, oT)
                split_out(2 * i + 1, 1)
                feed_stage(("out", 2 * i + 1), 3)
                norm(4 * i + 2, ("ln", 4 * i + 2), plan.unit[("out", 2 * i + 1)] + 3)
                ffn(2 * i + 1)
                norm(4 * i + 3, ("ln", 4 * i + 3), plan.unit[("ffn", 2 * i + 1)] + 32)

            act.wait_ge(sems["head_in"], 32)
            A(wba_hi[:, :, :, :], wba[:, :, :, :], ACT.Copy).then_inc(sems["ba_hi"], 1)
            act.wait_ge(sems["lb_arg"], 1)
            A(lb[:, :, :], lb[:, :, :], ACT.Exp).then_inc(sems["lb_exp"], 1)

            def rms_scale(r):
                act.wait_ge(sems["ln_var"], 8 + r + 1)
                A(std[:, :], var[:, :], ACT.Sqrt).then_inc(sems["ln_std"], 1)
                if r < 4:
                    for q in (0, 2):
                        take_scaled(plan.tile[("rms", r)] + q, 2 * q, col[:, 128 + r * KT:128 + (r + 1) * KT])
                    split_norm(("rms", r), plan.tile[("rms", r)])
                if r > 0:
                    feed(before_rms(r))

            def take_func(t, dst, func, scale=1.0):
                act.wait_ge(*ready(t))
                A(dst, bank[t % NB][:, :], func, scale=scale).then_inc(tile_taken[t % NB], 1)

            def tok2(v, j):
                return v[:, :, j * 256:(j + 1) * 256]

            def mixer2(l):
                T, U = plan.tile, plan.unit

                def feed_of(name, j):
                    feed(U[(name, l)] + j)
                for j in range(2):
                    feed_of("hq", j)
                    take_func(T[("hq", l)] + j, pair(hq, j), ACT.Silu)
                for j in range(4):
                    feed_of("hf", j)
                    take_func(T[("hf", l)] + j, pair(hk[:, j // 2], j % 2), ACT.Exp, -1.0)
                for j in range(2):
                    feed_of("hi", j)
                    take(T[("hi", l)] + j, tok2(hi, j))
                for j in range(2):
                    feed_of("hz", j)
                    t = T[("hz", l)] + j
                    act.wait_ge(*ready(t))
                    A(tok2(hz, j), bank[t % NB][:, :].rearrange("p (t c) -> p t c", t=TT),
                      ACT.Silu).then_inc(tile_taken[t % NB], 1)
                for d in range(2):
                    act.wait_ge(sems["hg_num"], 2 * l + d + 1)
                    A(hE[:, d, 1, :], hE[:, d, 1, :], ACT.Ln).then_inc(sems["hg_log"], 1)
                for j in range(8):
                    feed_of("qkv", j) if j < 6 else feed_of("z", j - 6)
                    if j >= 2:
                        act.wait_ge(sems["qkv_conv"], 6 * l + j - 1)
                        A(pair(qkvT, j - 2), pair(qkvT, j - 2), ACT.Silu).then_inc(sems["qkv_silu"], 1)
                take(T[("ba", l)], ba32, lambda ps: ps[:, 0:32])
                for j in range(2):
                    t = T[("z", l)] + j
                    act.wait_ge(*ready(t))
                    A(tok2(zs, j), bank[t % NB][:, :].rearrange("p (t c) -> p t c", t=TT),
                      ACT.Silu).then_inc(tile_taken[t % NB], 1)
                ba3 = ba32.rearrange("p (t c) -> p t c", t=TT)
                act.wait_ge(*taken(T[("ba", l)]))
                step.did(A(eb.rearrange("p (t c) -> p t c", t=TT), ba3[:, :, 0:8], ACT.Exp, scale=-1.0))
                step.did(A(arow[:, l, 0, :], arow[:, l, 0, :], ACT.Exp))
                act.wait_ge(sems["ba_y"], l + 1)
                step.link(A(ny, ny, ACT.Exp))
                A(ny, ny, ACT.Ln, bias=1.0).then_inc(sems["ba_sp"], 1)
                for i in range(LEVELS + 2):
                    if i != LEVELS:
                        act.wait_ge(sems["hg_arg"], (LEVELS + 1) * l + (i if i < LEVELS else LEVELS) + 1)
                        A(hE[:, i % 2].rearrange("p a b -> p (a b)"), hE[:, i % 2].rearrange("p a b -> p (a b)"),
                          ACT.Exp).then_inc(sems["hg_exp"], 1)
                    if 1 <= i:
                        feed(U[("gate", l, i - 1)])
                    if i < 8:
                        take(T[("gate", l, i)], pair(gates, i))
                act.wait_ge(sems["hg_k"], (LEVELS + 2) * (l + 1))
                act.wait_ge(sems["hg_q"], (LEVELS + 2) * (l + 1))
                act.wait_ge(sems["qkv_silu"], 6 * l + 4)
                for j in range(4):
                    A(pair(l2s, j), pair(qkvT, j), ACT.Square).then_inc(sems["l2_sq"], 1)
                act.wait_ge(sems["l2_arg"], l + 1)
                A(l2n, l2n, ACT.Sqrt).then_inc(sems["l2_sqrt"], 1)
                act.wait_ge(sems["hg_ssq"], l + 1)
                A(bss[:, 0:8], bss[:, 0:8], ACT.Sqrt).then_inc(sems["hg_std"], 1)
                act.wait_ge(sems["gc_arg"], l + 1)
                step.did(A(eg, gc, ACT.Exp))
                A(kdf, kdf, ACT.Exp).then_inc(sems["gc_exp"], 1)
                for g in range(4):
                    t = T[("gcB", l)] + g
                    act.wait_ge(*ready(t))
                    for h in range(4):
                        c = (g // 2) * 8 + (g % 2) * 4 + h
                        i = A(dec[:, g, h * P:(h + 1) * P], bank[t % NB][:, h * P:(h + 1) * P], ACT.Abs,
                              bias=ngc[:, c:c + 1])
                        if h < 3:
                            step.did(i)
                    i.then_inc(tile_taken[t % NB], 1)
                    step.sync()
                    act.wait_ge(*taken(t))
                    A(dec[:, g, :], dec[:, g, :], ACT.Exp, scale=-1.0).then_inc(sems["dec"], 1)
                for j in range(2):
                    take(T[("hg_T", l)] + j, pair(oT_hg, j))
                for j in range(2):
                    act.wait_ge(*taken(T[("hg_T", l)] + j))
                    split_pair(("branch", l), j, pair(oT_hg, j))
                for j in range(4):
                    take(T[("kv_T", l)] + j, (k_tk if j < 2 else v_tk)[:, j % 2, :])
                for i in range(8):
                    act.wait_ge(*taken(T[("gate", l, i)]))
                A(gates[:, :, :], gates[:, :, :], ACT.Sigmoid).then_inc(sems["gates_ready"], 1)
                for v in range(1, LEVELS):
                    for g in range(4):
                        take(T[("Y", l, v)] + g, yinv[:, g, :])
                for name, dst in (("vnA", (0, 3)), ("vnB", (2, 1))):
                    for d in range(2):
                        take(T[(name, l)] + d, vn[:, dst[d], :])
                act.wait_ge(sems["dn_ssq"], l + 1)
                A(bss[:, 0:8], bss[:, 0:8], ACT.Sqrt).then_inc(sems["dn_std"], 1)
                feed_of("branch_hg", 0)
                split_half(U[("branch_hg", l)] + 3, 0)
                for j in range(2):
                    take(T[("dn_T", l)] + j, pair(oT_dn, j))
                for j in range(2):
                    act.wait_ge(*taken(T[("dn_T", l)] + j))
                    split_pair(("branch", l), 2 + j, pair(oT_dn, j))
                split_half(U[("branch_hg", l)] + 3, 1)
                feed_of("branch_dn", 0)
                act.wait_ge(sems["unit_used"], U[("branch_dn", l)] + 2)
                for j in range(4):
                    act.wait_ge(sems["merged"], 4 * l + j + 1)
                    split_pair(("out", 4 + l), j, pair(merged, j))
                feed_of("branch_dn", 1)
                feed_stage(("out", 4 + l), 3)

            for l in range(DEPTH):
                rms_scale(2 * l)
                mixer2(l)
                rms_scale(2 * l + 1)
                ffn(4 + l, conv_first=True)
            rms_scale(4)



        @block.vector
        def _(dve):
            V = nc.vector
            step = Progress(dve, sems["dve_step"])

            def split_pair(name, q, src):
                dve.wait_ge(sems["x_hi"], 4 * plan.sets[name] + q + 1)
                V.tensor_tensor(pair(xT_lo, q), src, pair(xT_hi, q).bitcast(F32), ALU.subtract).then_inc(sems["x_lo"], 1)

            def split_operand(name, src):
                for q in range(4):
                    split_pair(name, q, pair(src, q))

            def split_half(u, h, more=0):
                if (u, h) in plan.on_pool:
                    return
                dve.wait_ge(sems["w_hi"], more * 12 + 2 * u + h + 1)
                V.tensor_tensor(half_of(ring_lo, u, h), half_of(ring, u, h), high_of(u, h).bitcast(F32),
                                ALU.subtract).then_inc(sems["w_lo"], 1)

            def feed(u, more=0, halves=(0, 1)):
                for h in halves:
                    if u + 2 < plan.units:
                        split_half(u + 2, h, more)

            def feed_stage(name, n):
                for j in range(n):
                    feed(plan.unit[name] + j)

            def feed_out(n):
                feed_stage(("out", n), 2)
                feed(plan.unit[("out", n)] + 2, halves=(0,))

            def ffn(n, conv_first=False):
                t0, u0 = plan.tile[("ffn", n)], plan.unit[("ffn", n)]

                def product(f, more):
                    dve.wait_ge(sems["gate_silu"], more * 4 + FT * n + f + 1)
                    b, h = (t0 + f) % NB, f % 4
                    V.scalar_tensor_tensor(hidden[:, h, :], hidden[:, h, :], 1.0 if conv_first else 0.5,
                                           bank[b][:, S:2 * S], ALU.mult, ALU.mult).then_inc(tile_taken[b], 1)
                    dve.wait_ge(tile_taken[b], more + (t0 + f) // NB + 1)
                    V.tensor_copy(hidden_hi[:, h, :], hidden[:, h, :]).then_inc(sems["hidden_high"], 1)
                    dve.wait_ge(sems["hidden_high"], more * 4 + FT * n + f + 1)
                    V.tensor_tensor(hidden_lo[:, h, :], hidden[:, h, :], hidden_hi[:, h, :].bitcast(F32),
                                    ALU.subtract).then_inc(sems["hidden_split"], 1)

                def ffn_step(m, more=0):
                    f = tile_of_step(m)
                    if m + 1 < FU:
                        feed(u0 + m, more, halves=(0,))
                    if f is not None and conv_first:
                        convolve(n, f, more)
                    if m + 2 < FU:
                        feed(u0 + m, more, halves=(1,))
                    if f is not None:
                        product(f, more)
                run_steps(dve, ffn_step)

            def await_acc(n, tt, half, last_unit):
                j = tt * 2 + half
                if j < 3:
                    dve.wait_ge(sems["acc_ready"], 3 * n + j + 1)
                else:
                    dve.wait_ge(sems["unit_used"], last_unit + 1)
                return acc[j][:, :]

            def take_scaled(t0, inst, bias=True):
                for q in (1, 3):
                    t = t0 + q
                    dve.wait_ge(*ready(t))
                    for j in range(2):
                        k = 2 * q + j
                        g = col[:, inst * KT + k:inst * KT + k + 1]
                        src = bank[t % NB][:, j * S:(j + 1) * S]
                        if bias:
                            i = V.tensor_scalar(xT[:, k, :], src, g, col[:, (8 + inst) * KT + k:(8 + inst) * KT + k + 1],
                                                ALU.mult, ALU.add)
                        else:
                            i = V.tensor_scalar(xT[:, k, :], src, g, None, ALU.mult)
                        if j == 0:
                            step.did(i)
                    i.then_inc(tile_taken[t % NB], 1)

            def norm(inst, key, last_unit):
                if inst > 0:
                    dve.wait_ge(sems["x_updated"], inst)
                else:
                    dve.wait_ge(sems["x_in"], 16)
                for tt in range(TT):
                    for h in range(2):
                        a = await_acc(inst, tt, h, last_unit)
                        c = slice(h * 512, (h + 1) * 512)
                        step.link(V.scalar_tensor_tensor(xh[:, tt, c], x[:, tt, c], ALPHA, a, ALU.mult, ALU.add))
                        step.did(V.bn_stats(bn[:, tt * 2 + h, :], xh[:, tt, c]))
                    step.sync()
                    step.did(V.bn_aggr(mv[:, tt, :], bn[:, 2 * tt:2 * tt + 2, :]))
                step.sync()
                V.tensor_scalar(var[:, :], mv[:, :, 1], LN_EPS, None, ALU.add).then_inc(sems["ln_var"], 1)
                dve.wait_ge(sems["ln_std"], inst + 1)
                step.link(V.reciprocal(rstd[:, :], std[:, :]))
                for tt in range(TT):
                    V.tensor_scalar(xh[:, tt, :], xh[:, tt, :], mv[:, tt, 0:1], rstd[:, tt:tt + 1],
                                    ALU.subtract, ALU.mult).then_inc(sems["ln_xh"], 1)
                feed(last_unit - 1, halves=(1,))
                take_scaled(plan.tile[key], inst)
                if key in plan.sets:
                    split_operand(key, xT)
                feed(last_unit)

            def rope():
                for j in range(6):
                    dve.wait_ge(*taken(plan.tile["ab_in"] + j))
                heads = raw[:, :, 0:640]
                step.link(V.tensor_tensor(rtmp[:, 0], heads, heads, ALU.mult))
                step.link(V.reduce_sum(ssq[:, :, :].rearrange("p t h -> p (t h)"),
                                       rtmp[:, 0].rearrange("p t (h d) -> p (t h) d", d=HD), axis=AX_X))
                V.tensor_scalar(ssq[:, :, :], ssq[:, :, :], 1.0 / HD, EPS, ALU.mult, ALU.add).then_inc(sems["ab_ssq"], 1)
                yield
                yield
                dve.wait_ge(sems["ab_sqrt"], 1)
                step.link(V.reciprocal(srt[:, :, :], srt[:, :, :]))
                h4 = heads.rearrange("p t (h d) -> p t h d", d=HD)
                for tt in range(TT):
                    step.did(V.tensor_tensor(h4[:, tt], h4[:, tt], srt[:, tt, :].unsqueeze(2).to_broadcast([P, 10, HD]), ALU.mult))
                step.sync()
                for a, b, g in ((0, 8, 0), (8, 10, HD)):
                    gb = gain[:, g:g + HD].unsqueeze(1).to_broadcast([P, b - a, HD])
                    for tt in range(TT):
                        step.did(V.tensor_tensor(h4[:, tt, a:b], h4[:, tt, a:b], gb, ALU.mult))
                step.sync()
                yield
                rt = table("rope").rearrange("p (t m f) -> p t m f", t=TT, m=2)
                for m in range(2):
                    for tt in range(TT):
                        src = raw[:, tt, m * 768:m * 768 + 640].rearrange("p (h d) -> p h d", d=HD)
                        a = rtmp[:, 2 * m, tt].rearrange("p (h d) -> p h d", d=HD)
                        b = rtmp[:, 2 * m + 1, tt].rearrange("p (h d) -> p h d", d=HD)

                        def row(lo, n):
                            return rt[:, tt, m, lo:lo + n].unsqueeze(1).to_broadcast([P, 10, n])
                        step.did(V.tensor_tensor(a, src, row(0, 64), ALU.mult))
                        step.did(V.tensor_tensor(b[:, :, 0:32], src[:, :, 32:64], row(64, 32), ALU.mult))
                        step.did(V.tensor_tensor(b[:, :, 32:64], src[:, :, 0:32], row(96, 32), ALU.mult))
                    yield
                step.sync()
                for m in range(2):
                    a, b, c = rtmp[:, 2 * m], rtmp[:, 2 * m + 1], m * 768
                    step.did(V.tensor_tensor(roped[:, :, c:c + 512], a[:, :, 0:512], b[:, :, 0:512], ALU.add))
                    keys = roped[:, :, c + 512:c + 768].rearrange("p t (k u d) -> p t k u d", k=2, u=2)
                    for u in range(2):
                        for tt in range(TT):
                            i = V.tensor_tensor(keys[:, tt, :, u, :],
                                                a[:, tt, 512:640].rearrange("p (k d) -> p k d", k=2),
                                                b[:, tt, 512:640].rearrange("p (k d) -> p k d", k=2), ALU.add)
                            if u + tt < 2:
                                step.did(i)
                    i.then_inc(sems["ab_roped"], 1)

            def attention(a, groups, per, scale, mode, exps):
                key = ("att", a)
                e0 = first_score(a)
                first_masked = min([e for e in range(groups * per) if mode(e)] or [0])
                for g in range(groups + 1):
                    if g < groups:
                        for j in range(per):
                            e = g * per + j
                            t = plan.tile[(key, "S", g)] + j
                            b = bank[t % NB]
                            dve.wait_ge(*ready(t))
                            masked = mode(e)
                            if not masked:
                                step.link(V.reduce_max(mx[:, e, :], b[:, :].rearrange("p (t s) -> p t s", t=TT), axis=AX_X))
                                V.tensor_scalar(nmx[:, e, :], mx[:, e, :], -scale, None, ALU.mult).then_inc(sems["score_max"], 1)
                                continue
                            sc = score[:, e % 4, :, :]
                            if masked == "sink":
                                V.scalar_tensor_tensor(sc.rearrange("p a b -> p (a b)"), b[:, :], scale, table("window"),
                                                       ALU.mult, ALU.add).then_inc(tile_taken[t % NB], 1)
                            else:
                                for tt in range(TT):
                                    bias = grid_bias[:, e, 2 - 2 * tt:6 - 2 * tt, ::-1]

                                    def rows(v):
                                        return v.rearrange("p (r c) -> p r c", c=GRID)
                                    i = V.scalar_tensor_tensor(rows(sc[:, tt, :]), rows(b[:, tt * S:(tt + 1) * S]), scale, bias,
                                                               ALU.mult, ALU.add)
                                    if tt == 0:
                                        step.did(i)
                                i.then_inc(tile_taken[t % NB], 1)
                                step.sync()
                            dve.wait_ge(*taken(t))
                            step.link(V.reduce_max(mx[:, e, :], sc, axis=AX_X))
                            if masked == "sink":
                                step.link(V.tensor_scalar(mx[:, e, :], mx[:, e, :], sink_b[:, e - 8:e - 7], None, ALU.max))
                            V.tensor_scalar(nmx[:, e, :], mx[:, e, :], -1.0, None, ALU.mult).then_inc(sems["score_max"], 1)
                    if g >= 1:
                        for j in range(per):
                            e = (g - 1) * per + j
                            masked = mode(e)
                            if masked:
                                dve.wait_ge(sems["prob_exp"], exps + e - first_masked + 1)
                            else:
                                dve.wait_ge(*taken(plan.tile[(key, "S", g - 1)] + j))
                            if masked == "sink":
                                step.link(V.tensor_tensor(psum_p[:, e, :], psum_p[:, e, :], sink_e[:, e, :], ALU.add))
                            step.link(V.reciprocal(rec[:, e, :], psum_p[:, e, :]))
                            for tt in range(TT):
                                i = V.tensor_scalar(prob[:, e % 6, tt, :], prob[:, e % 6, tt, :], rec[:, e, tt:tt + 1], None,
                                                    ALU.mult)
                                if tt == 0:
                                    step.did(i)
                            i.then_inc(sems["prob_norm"], 1)

            for h in range(2):
                split_half(0, h)
            split_operand("x", xT)
            for h in range(2):
                split_half(1, h)
            dve.wait_ge(sems["cols_in"], 48)
            for i in range(DEPTH):
                ffn(2 * i)
                norm(4 * i, ("ln", 4 * i), plan.unit[("ffn", 2 * i)] + 32)
                feed_stage("ab_in" if i == 0 else "c_in", 6 if i == 0 else 12)
                split_operand(("mem", i), memT)
                parts = rope() if i == 0 else iter(())
                for j in range(8):
                    feed(plan.unit[("kv", i)] + j)
                    next(parts, None)
                for _ in parts:
                    pass
                if i == 0:
                    attention(0, 8, 2, HD ** -0.5, lambda e: None if e < 8 else "sink", 0)
                else:
                    dve.wait_ge(sems["bias_ready"], 1)
                    attention(2, 8, 2, HD ** -0.5, lambda e: "bias", 8)
                split_operand(("out", 2 * i), oT)
                feed_out(2 * i)
                norm(4 * i + 1, ("ln", 4 * i + 1), plan.unit[("out", 2 * i)] + 3)
                feed_stage(("mq", i), 4)
                attention(2 * i + 1, 4, 1, 256 ** -0.5, lambda e: None, 0)
                split_operand(("out", 2 * i + 1), oT)
                feed_out(2 * i + 1)
                norm(4 * i + 2, ("ln", 4 * i + 2), plan.unit[("out", 2 * i + 1)] + 3)
                ffn(2 * i + 1)
                norm(4 * i + 3, ("ln", 4 * i + 3), plan.unit[("ffn", 2 * i + 1)] + 32)

            def signal(sem, n):
                step.sync()
                dve.sem_inc(sem, n)

            def rms(r):
                for tt in range(TT):
                    for h in range(2):
                        c = slice(h * 512, (h + 1) * 512)
                        if r > 0:
                            a = await_acc(7 + r, tt, h, before_rms(r))
                            step.link(V.tensor_tensor(x[:, tt, c], x[:, tt, c], a, ALU.add))
                        step.did(V.bn_stats(bn[:, tt * 2 + h, :], x[:, tt, c]))
                    step.sync()
                    step.did(V.bn_aggr(mv[:, tt, :], bn[:, 2 * tt:2 * tt + 2, :]))
                step.sync()
                step.link(V.tensor_tensor(var[:, :], mv[:, :, 0], mv[:, :, 0], ALU.mult))
                V.scalar_tensor_tensor(var[:, :], var[:, :], EPS, mv[:, :, 1], ALU.add, ALU.add).then_inc(sems["ln_var"], 1)
                dve.wait_ge(sems["ln_std"], 8 + r + 1)
                step.link(V.reciprocal(rstd[:, :], std[:, :]))
                for tt in range(TT):
                    V.tensor_scalar(xh[:, tt, :], x[:, tt, :], rstd[:, tt:tt + 1], None, ALU.mult).then_inc(sems["ln_xh"], 1)
                if r > 0:
                    feed(before_rms(r) - 1, halves=(1,))
                if r < 4:
                    for q in (1, 3):
                        t = plan.tile[("rms", r)] + q
                        dve.wait_ge(*ready(t))
                        for j in range(2):
                            k = 2 * q + j
                            i = V.tensor_scalar(xT[:, k, :], bank[t % NB][:, j * S:(j + 1) * S],
                                                col[:, 128 + r * KT + k:129 + r * KT + k], None, ALU.mult)
                            if j == 0:
                                step.did(i)
                        i.then_inc(tile_taken[t % NB], 1)
                    split_operand(("rms", r), xT)
                if r > 0:
                    feed(before_rms(r))

            def taps(dst, src, weight, center, bias=None):
                yield lambda: V.tensor_scalar(dst, src, weight(center), bias, ALU.mult,
                                              ALU.add if bias is not None else ALU.bypass)
                for j in range(2 * center + 1):
                    o = j - center
                    if o < 0:
                        yield lambda o=o, j=j: V.scalar_tensor_tensor(dst[:, -o:S], src[:, 0:S + o], weight(j),
                                                                     dst[:, -o:S], ALU.mult, ALU.add)
                    if o > 0:
                        yield lambda o=o, j=j: V.scalar_tensor_tensor(dst[:, 0:S - o], src[:, o:S], weight(j),
                                                                     dst[:, 0:S - o], ALU.mult, ALU.add)

            def lower_bounds():
                c = 160 + 120 + 176
                l0, l1 = col[:, c:c + 8], col[:, c + 8:c + 16]
                m = small[:, 0, 0:8]
                step.link(V.tensor_tensor(m, l0, l1, ALU.max))
                step.did(V.tensor_tensor(lb[:, 0, :], l0, m, ALU.subtract))
                V.tensor_tensor(lb[:, 1, :], l1, m, ALU.subtract).then_inc(sems["lb_arg"], 1)
                dve.wait_ge(sems["lb_exp"], 1)
                step.link(V.tensor_tensor(m, lb[:, 0, :], lb[:, 1, :], ALU.add))
                step.link(V.reciprocal(m, m))
                for i in range(2):
                    step.did(V.tensor_tensor(lb[:, i, :], lb[:, i, :], m, ALU.mult))
                step.sync()
                step.link(V.tensor_tensor(lb[:, 1, :], lb[:, 0, :], lb[:, 1, :], ALU.add))
                step.link(V.tensor_tensor(lb[:, 1, :], lb[:, 1, :], lb[:, 0, :], ALU.subtract))
                step.link(V.tensor_tensor(lb[:, 0, :], lb[:, 0, :], lb[:, 0, :], ALU.subtract))
                step.link(V.tensor_scalar(lb[:, :, :], lb[:, :, :], 0.0, 1.0, ALU.max, ALU.min))
                r = float(P) ** -0.5
                step.link(V.tensor_scalar(omlb[:, :, :], lb[:, :, :], -r, r, ALU.mult, ALU.add))

            def decays(l):
                T = plan.tile
                flat = lambda v: v.rearrange("p a b -> p (a b)")
                for d in range(2):
                    for j in range(2):
                        dve.wait_ge(*taken(T[("hf", l)] + 2 * d + j))
                    e, den, num = hk[:, d], hE[:, d, 0, :], hE[:, d, 1, :]
                    step.link(V.tensor_scalar(den, flat(e), 1.0, None, ALU.add))
                    step.did(V.reciprocal(den, den))
                    for h in range(4):
                        step.did(V.tensor_scalar(num[:, h * S:(h + 1) * S], e[:, h, :], lb[:, l, d * 4 + h:d * 4 + h + 1],
                                                 1.0, ALU.mult, ALU.add))
                    step.sync()
                    V.tensor_tensor(num, num, den, ALU.mult).then_inc(sems["hg_num"], 1)
                    for h in range(4):
                        step.did(V.scalar_tensor_tensor(e[:, h, :], e[:, h, :], omlb[:, l, d * 4 + h:d * 4 + h + 1],
                                                        den[:, h * S:(h + 1) * S], ALU.mult, ALU.mult))
                    yield
                yield
                for d in range(2):
                    dve.wait_ge(sems["hg_log"], 2 * l + d + 1)
                    num = hE[:, d, 1, :]
                    for b in range(8):
                        c = slice(b * P, (b + 1) * P)
                        step.did(V.tensor_tensor_scan(flat(hF[:, d])[:, c], table("ones"), num[:, c], 0.0,
                                                      ALU.mult, ALU.add))
                    yield
                step.sync()
                step.link(V.tensor_copy(btot, hF[:, 1, :, P - 1]))
                step.link(V.tensor_tensor(flat(hF[:, 1]), flat(hF[:, 1]), hE[:, 1, 1, :], ALU.subtract))

            def conv_qkv(l):
                for j in range(6):
                    if j > 0:
                        feed(plan.unit[("qkv", l)] + j + 1) if j < 5 else feed(plan.unit[("z", l)])
                    t = plan.tile[("qkv", l)] + j
                    dve.wait_ge(*ready(t))
                    steps = []
                    for f in range(2):
                        n = 2 * j + f

                        def weight(tap, n=n):
                            c = 160 + (l * 5 + tap) * 12 + n
                            return col[:, c:c + 1]
                        steps.append(list(taps(qkvT[:, n, :], bank[t % NB][:, f * S:(f + 1) * S], weight, 2)))
                    for k in range(5):
                        for f in range(2):
                            i = steps[f][k]()
                            if k == 4 and f == 1:
                                i.then_inc(tile_taken[t % NB], 1)
                            else:
                                step.did(i)
                        if k < 4:
                            step.sync()
                    step.sync()
                    dve.wait_ge(*taken(t))
                    signal(sems["qkv_conv"], 1)

            def args(l, i):
                K, Q = hE[:, i % 2, 0, :], hE[:, i % 2, 1, :]
                F, B = hF[:, 0].rearrange("p h s -> p (h s)"), hF[:, 1].rearrange("p h s -> p (h s)")
                m = 1 << min(i, LEVELS)
                half = lambda v: v.rearrange("p (n u m) -> p n u m", u=2, m=m)
                nb = 4 * S // (2 * m)
                K4, Q4, F4, B4 = half(K), half(Q), half(F), half(B)
                if i < LEVELS:
                    fref = F4[:, :, 0, m - 1:m].to_broadcast([P, nb, m])
                    bref = B4[:, :, 1, 0:1].to_broadcast([P, nb, m])
                    step.did(V.tensor_tensor(K4[:, :, 0, :], fref, F4[:, :, 0, :], ALU.subtract))
                    step.did(V.tensor_tensor(K4[:, :, 1, :], B4[:, :, 1, :], bref, ALU.subtract))
                    step.did(V.tensor_tensor(Q4[:, :, 1, :], F4[:, :, 1, :], fref, ALU.subtract))
                    V.tensor_tensor(Q4[:, :, 0, :], bref, B4[:, :, 0, :], ALU.subtract).then_inc(sems["hg_arg"], 1)
                else:
                    fref = F4[:, :, 0, m - 1:m].to_broadcast([P, nb, m])
                    step.did(V.tensor_tensor(K4[:, :, 0, :], fref, F4[:, :, 0, :], ALU.subtract))
                    step.did(V.tensor_copy(K4[:, :, 1, :], B4[:, :, 1, :]))
                    step.did(V.tensor_copy(Q4[:, :, 1, :], F4[:, :, 1, :]))
                    V.tensor_tensor(Q4[:, :, 0, :], btot.unsqueeze(2).to_broadcast([P, 4, m]), B4[:, :, 0, :],
                                    ALU.subtract).then_inc(sems["hg_arg"], 1)

            def kmul(l, i):
                K = hKQ[:, i % 2, 0, :]
                kf, kb = hk[:, 0].rearrange("p h s -> p (h s)"), hk[:, 1].rearrange("p h s -> p (h s)")
                if i == LEVELS:
                    V.tensor_tensor(K, kf, kb, ALU.add).then_inc(sems["hg_k"], 1)
                    return
                dve.wait_ge(sems["hg_exp"], (LEVELS + 1) * l + min(i, LEVELS) + 1)
                m = 1 << min(i, LEVELS)
                half = lambda v: v.rearrange("p (n u m) -> p n u m", u=2, m=m)
                E = half(hE[:, i % 2, 0, :])
                step.did(V.tensor_tensor(half(K)[:, :, 0, :], half(kf)[:, :, 0, :], E[:, :, 0, :], ALU.mult))
                V.tensor_tensor(half(K)[:, :, 1, :], half(kb)[:, :, 1, :], E[:, :, 1, :], ALU.mult).then_inc(sems["hg_k"], 1)

            def gather(l, i):
                for c in range(2):
                    t = plan.tile[("level", l, i)] + c
                    dve.wait_ge(*ready(t))
                    src = heads2(bank[t % NB][:, :])
                    q = c if i <= LEVELS else 1 - c
                    dst = hatt[:, c, :, q * P:(q + 1) * P]
                    if 0 < i <= LEVELS:
                        dve.wait_ge(*taken(plan.tile[("level", l, i - 1)] + c))
                    if i == 0 or i > LEVELS:
                        j = V.tensor_copy(dst, src)
                    else:
                        mask = hmask[:, i * P:(i + 1) * P].unsqueeze(1).to_broadcast([P, 4, P])
                        j = V.copy_predicated(dst, mask, src)
                    j.then_inc(tile_taken[t % NB], 1)

            def head_rms(rows, gate, ssq_name, std_name, l):
                v8 = lambda v: v.rearrange("p t (h d) -> p (t h) d", d=P)
                sq = region(10240, 1024)
                step.link(V.tensor_tensor(sq, rows.rearrange("p t c -> p (t c)"), rows.rearrange("p t c -> p (t c)"), ALU.mult))
                step.link(V.reduce_sum(bss[:, 0:8], sq.rearrange("p (a d) -> p a d", d=P), axis=AX_X))
                V.tensor_scalar(bss[:, 0:8], bss[:, 0:8], 1.0 / P, EPS, ALU.mult, ALU.add).then_inc(sems[ssq_name], 1)
                dve.wait_ge(sems[std_name], l + 1)
                step.link(V.reciprocal(brs[:, 0:8], bss[:, 0:8]))
                step.link(V.tensor_tensor(v8(rows), v8(rows), brs[:, 0:8].unsqueeze(2).to_broadcast([P, 8, P]), ALU.mult))

            def mixer2(l):
                T = plan.tile
                U = plan.unit
                for j in range(2):
                    feed(U[("hq", l)] + j)
                for j in range(4):
                    feed(U[("hf", l)] + j)
                parts = decays(l)
                feed(U[("hi", l)])
                next(parts)
                feed(U[("hi", l)] + 1)
                next(parts)
                feed(U[("hz", l)])
                feed(U[("hz", l)] + 1)
                next(parts)
                feed(U[("qkv", l)])
                next(parts)
                feed(U[("qkv", l)] + 1)
                next(parts)
                next(parts, None)
                conv_qkv(l)
                feed(U[("z", l)] + 1)
                dve.wait_ge(*taken(T[("ba", l)]))
                ba3 = ba32.rearrange("p (t c) -> p t c", t=TT)
                t3 = lambda v: v.rearrange("p (t c) -> p t c", t=TT)
                step.link(V.tensor_tensor(t3(yb), ba3[:, :, 8:16], arow[:, l, 1, :].unsqueeze(1).to_broadcast([P, TT, 8]), ALU.add))
                V.scalar_tensor_tensor(ny, yb, -1.0, yb, ALU.mult, ALU.min).then_inc(sems["ba_y"], 1)
                args(l, 0)
                args(l, 1)
                dve.wait_ge(sems["ba_sp"], l + 1)
                step.link(V.tensor_scalar(eb, eb, 1.0, None, ALU.add))
                step.did(V.reciprocal(beta, eb))
                step.link(V.scalar_tensor_tensor(gg, yb, 0.0, ny, ALU.max, ALU.add))
                V.scalar_tensor_tensor(t3(gg), t3(gg), -1.0, arow[:, l, 0, :].unsqueeze(1).to_broadcast([P, TT, 8]),
                                       ALU.mult, ALU.mult).then_inc(sems["g_ready"], 1)
                n = LEVELS + 2
                for i in range(n + 2):
                    if 2 <= i < n and i != LEVELS:
                        if i - 2 != LEVELS:
                            dve.wait_ge(sems["hg_q"], n * l + i - 1)
                            dve.wait_ge(sems["hg_k"], n * l + i - 1)
                        args(l, i)
                    if 1 <= i <= n:
                        kmul(l, i - 1)
                    if i >= 2:
                        gather(l, i - 2)
                    if 1 <= i <= 8:
                        feed(U[("gate", l, i - 1)])
                t = T[("l2", l)]
                dve.wait_ge(*ready(t))
                V.tensor_scalar(l2n, bank[t % NB][:, 0:16], EPS, None, ALU.add).then_inc(tile_taken[t % NB], 1)
                dve.wait_ge(*taken(t))
                dve.sem_inc(sems["l2_arg"], 1)
                dve.wait_ge(*ready(T[("hg_o", l)] + 1))
                for tt in range(TT):
                    t = T[("hg_o", l)] + tt
                    V.tensor_copy(hi[:, tt, :], bank[t % NB][:, :]).then_inc(tile_taken[t % NB], 1)
                dve.wait_ge(sems["l2_sqrt"], l + 1)
                step.link(V.reciprocal(l2i, l2n))
                V.tensor_scalar(l2i[:, 0:8], l2i[:, 0:8], float(P) ** -0.5, None, ALU.mult).then_inc(sems["l2_inv"], 1)
                t = T[("gcum", l)]
                dve.wait_ge(*ready(t))
                step.did(V.tensor_copy(gc, bank[t % NB][:, 0:16]))
                step.did(V.tensor_scalar(ngc, bank[t % NB][:, 0:16], -1.0, None, ALU.mult))
                step.link(V.tensor_copy(kdf, bank[t % NB][:, 16:32]))
                step.link(V.tensor_tensor(kdf, kdf, gc, ALU.subtract))
                signal(tile_taken[t % NB], 1)
                signal(sems["gc_arg"], 1)
                for tt in range(TT):
                    dve.wait_ge(*taken(T[("hg_o", l)] + tt))
                head_rms(hi, hz, "hg_ssq", "hg_std", l)
                dve.wait_ge(sems["z_ready"], 2 * l + 1)
                V.tensor_tensor(hz, hi, hz, ALU.mult).then_inc(sems["hg_out"], 1)
                for j in range(4):
                    t = T[("l2B", l)] + j
                    dve.wait_ge(*ready(t))
                    V.tensor_tensor(pair(qkvT, j), pair(qkvT, j), bank[t % NB][:, :], ALU.mult).then_inc(tile_taken[t % NB], 1)
                for j in range(4):
                    dve.wait_ge(*taken(T[("l2B", l)] + j))
                dve.sem_inc(sems["l2_done"], 1)
                for q in range(2):
                    split_pair(("branch", l), q, pair(oT_hg, q))
                dve.wait_ge(sems["gc_exp"], l + 1)
                V.scalar_tensor_tensor(nbe, beta, -1.0, eg, ALU.mult, ALU.mult).then_inc(sems["nbe"], 1)
                for tt in range(TT):
                    t = T[("G", l)] + tt
                    dve.wait_ge(*ready(t))
                    for d in range(2):
                        g = 2 * tt + d
                        dve.wait_ge(sems["dec"], 4 * l + g + 1)
                        for h in range(4):
                            c = tt * 8 + d * 4 + h
                            i = V.scalar_tensor_tensor(amat[:, g, h * P:(h + 1) * P], bank[t % NB][:, h * P:(h + 1) * P],
                                                       beta[:, c:c + 1], dec[:, g, h * P:(h + 1) * P], ALU.mult, ALU.mult)
                            if h < 3:
                                step.did(i)
                        i.then_inc(sems["a_ready"], 1)
                    dve.wait_ge(sems["a_ready"], 4 * l + 2 * tt + 2)
                    signal(tile_taken[t % NB], 1)
                for tt in range(TT):
                    t = T[("QK", l)] + tt
                    dve.wait_ge(*ready(t))
                    dve.wait_ge(sems["dec_masked"], 4 * l + 2 * tt + 2)
                    step.did(V.tensor_tensor(qkd[:, 2 * tt, :], bank[t % NB][:, :], qkd[:, 2 * tt, :], ALU.mult))
                    V.tensor_tensor(qkd[:, 2 * tt + 1, :], bank[t % NB][:, :], qkd[:, 2 * tt + 1, :],
                                    ALU.mult).then_inc(tile_taken[t % NB], 1)
                eye = ident.unsqueeze(1).to_broadcast([P, 4, P])
                for g in range(4):
                    dve.wait_ge(sems["a_level"], 4 * LEVELS * l + g + 1)
                    V.tensor_tensor(heads2(xinv[:, g, :]), eye, heads2(alev[:, g, :]), ALU.subtract).then_inc(sems["x_first"], 1)
                    t = T[("A0", l)] + g
                    dve.wait_ge(*ready(t))
                    V.tensor_tensor(heads2(winv[:, g, :]), eye, heads2(bank[t % NB][:, :]),
                                    ALU.subtract).then_inc(tile_taken[t % NB], 1)
                for v in range(1, LEVELS):
                    for g in range(4):
                        for j, m in enumerate((winv, xinv) if v < LEVELS - 1 else (winv,)):
                            t = T[("Z", l, v)] + (2 * g if v < LEVELS - 1 else g) + j
                            dve.wait_ge(*ready(t))
                            second = (g % 2 == 0) == (j == 0)
                            V.tensor_tensor(side(m[:, g, :], v, second), side(m[:, g, :], v, second),
                                            side(bank[t % NB][:, :], v, second), ALU.subtract).then_inc(tile_taken[t % NB], 1)
                    if v == 1:
                        for j in range(4):
                            dve.wait_ge(*taken(T[("kv_T", l)] + j))
                        dve.wait_ge(sems["dec_masked"], 4 * l + 4)
                    g, d = v - 1, v - 5
                    for h in range(4):
                        hs = slice(h * P, (h + 1) * P)
                        if v <= 4:
                            c = (g // 2) * 8 + (g % 2) * 4 + h
                            i = V.tensor_scalar(vb[:, g, hs], v_tk[:, g // 2, hs], beta[:, c:c + 1], None, ALU.mult)
                        else:
                            c = d * 8 + d * 4 + h
                            i = V.tensor_scalar(kd[:, d, hs], k_tk[:, d, hs], kdf[:, c:c + 1], None, ALU.mult)
                        if h < 3:
                            step.did(i)
                    i.then_inc(sems["vb" if v <= 4 else "kd"], 1)
                for d in range(2):
                    t = T[("S", l)] + d
                    dve.wait_ge(*ready(t))
                    V.tensor_copy(state[:, d, :], bank[t % NB][:, :]).then_inc(tile_taken[t % NB], 1)
                for d in range(2):
                    t, gb, tb = T[("kS", l)] + d, 2 - d, 1 - d
                    dve.wait_ge(*ready(t))
                    dve.wait_ge(sems["vb"], 4 * l + 4)
                    dve.wait_ge(sems["nbe"], l + 1)
                    for h in range(4):
                        c = tb * 8 + d * 4 + h
                        hs = slice(h * P, (h + 1) * P)
                        i = V.scalar_tensor_tensor(vb[:, gb, hs], bank[t % NB][:, hs], nbe[:, c:c + 1], vb[:, gb, hs],
                                                   ALU.mult, ALU.add)
                        if h < 3:
                            step.did(i)
                    i.then_inc(tile_taken[t % NB], 1)
                for d in range(2):
                    t, tb = T[("qS", l)] + d, 1 - d
                    dve.wait_ge(*ready(t))
                    for h in range(4):
                        c = tb * 8 + d * 4 + h
                        hs = slice(h * P, (h + 1) * P)
                        i = V.tensor_scalar(qs[:, tb, hs], bank[t % NB][:, hs], eg[:, c:c + 1], None, ALU.mult)
                        if h < 3:
                            step.did(i)
                    i.then_inc(tile_taken[t % NB], 1)
                for d in range(2):
                    dve.wait_ge(*taken(T[("qS", l)] + d))
                for tt in range(TT):
                    t = T[("dn_o", l)] + tt
                    dve.wait_ge(*ready(t))
                    V.tensor_tensor(dn_o[:, tt, :], bank[t % NB][:, :], qs[:, tt, :], ALU.add).then_inc(tile_taken[t % NB], 1)
                for tt in range(TT):
                    dve.wait_ge(*taken(T[("dn_o", l)] + tt))
                head_rms(dn_o, zs, "dn_ssq", "dn_std", l)
                dve.wait_ge(sems["z_ready"], 2 * l + 2)
                V.tensor_tensor(dn_o, dn_o, zs, ALU.mult).then_inc(sems["dn_out"], 1)
                dve.wait_ge(sems["gates_ready"], l + 1)
                for j in range(4):
                    t = T[("branch_hg", l)] + j
                    dve.wait_ge(*ready(t))
                    V.tensor_tensor(pair(merged, j), pair(gates, 4 + j), bank[t % NB][:, :],
                                    ALU.mult).then_inc(tile_taken[t % NB], 1)
                    if j == 1:
                        feed(U[("branch_hg", l)])
                feed(U[("branch_hg", l)] + 1, halves=(0,))
                for q in range(2, 4):
                    split_pair(("branch", l), q, pair(oT_dn, q - 2))
                feed(U[("branch_hg", l)] + 1, halves=(1,))
                for j in range(4):
                    t = T[("branch_dn", l)] + j
                    dve.wait_ge(*ready(t))
                    V.tensor_tensor(pair(mtmp, j), pair(gates, j), bank[t % NB][:, :], ALU.mult).then_inc(tile_taken[t % NB], 1)
                    dve.wait_ge(*taken(T[("branch_hg", l)] + j))
                    dve.wait_ge(*taken(T[("branch_dn", l)] + j))
                    V.tensor_tensor(pair(merged, j), pair(merged, j), pair(mtmp, j), ALU.add).then_inc(sems["merged"], 1)
                    if j == 1:
                        feed(U[("branch_dn", l)])
                split_operand(("out", 4 + l), merged)
                feed(U[("branch_dn", l)] + 1)
                feed_out(4 + l)

            def convolve(n, f, more):
                l, t0 = n - 4, plan.tile[("ffn", n)]
                dve.wait_ge(sems["unit_used"], more * 6 + plan.ready[t0 + f][1])
                c = 280 + l * 66 + f

                def pick(at):
                    return col[:, at:at + 1] if isinstance(more, int) else col[:, bass.ds(more * 4 + at, 1)]
                steps = list(taps(conv[:, f % 4, :], bank[(t0 + f) % NB][:, 0:S], lambda j: pick(c + j * FT), 1,
                                  pick(280 + 132 + l * FT + f)))
                for k in range(2):
                    steps[k]().then_inc(sems["conv_step"], 1)
                    dve.wait_ge(sems["conv_step"], more * 8 + FT * 2 * l + 2 * f + k + 1)
                steps[2]().then_inc(sems["conv_done"], 1)

            dve.wait_ge(sems["ba_hi"], 1)
            V.tensor_tensor(wba_lo[:, :, :, :], wba[:, :, :, :], wba_hi[:, :, :, :].bitcast(F32),
                            ALU.subtract).then_inc(sems["ba_lo"], 1)
            lower_bounds()
            dve.wait_ge(sems["x_updated"], 8)
            dve.wait_ge(sems["head_in"], 16 * 2)
            for l in range(DEPTH):
                rms(2 * l)
                mixer2(l)
                rms(2 * l + 1)
                ffn(4 + l, conv_first=True)
            rms(4)
            dve.wait_ge(sems["final_in"], 16)
            dve.wait_ge(sems["ln_xh"], 2 * 13)
            V.tensor_tensor(x[:, :, :], xh, f_rows.unsqueeze(1).to_broadcast([P, TT, D]), ALU.mult).then_inc(sems["final_rows"], 1)


        @block.gpsimd
        def _(pool):
            G = nc.gpsimd
            step = Progress(pool, sems["pool_step"])

            pool.wait_ge(sems["masks_in"], 16)
            pairs = region(18432, (3 * LEVELS + 1) * P)
            step.did(G.tensor_copy(hmask[:, :], pairs[:, 0:(LEVELS + 1) * P]))
            step.link(G.tensor_copy(levels[:, :], pairs[:, (LEVELS + 1) * P:]))
            rows = 0
            for inst in range(4 * DEPTH):
                pool.dma_start(g_rows, ln_g_rows[inst:inst + 1, :].partition_broadcast(P)).then_inc(sems["rows_in"], 16)
                pool.dma_start(b_rows, ln_b_rows[inst:inst + 1, :].partition_broadcast(P)).then_inc(sems["rows_in"], 16)
                rows += 32
                pool.wait_ge(sems["rows_in"], rows)
                pool.wait_ge(sems["ln_xh"], 2 * (inst + 1))
                for tt in range(TT):
                    step.did(G.tensor_tensor(x[:, tt, :], xh[:, tt, :], g_rows, ALU.mult))
                step.sync()
                for tt in range(TT):
                    i = G.tensor_tensor(x[:, tt, :], x[:, tt, :], b_rows, ALU.add)
                    if tt == 0:
                        step.did(i)
                i.then_inc(sems["x_updated"], 1)
                pool.wait_ge(sems["x_updated"], inst + 1)
                if inst == 1:
                    for half in range(2):
                        for h in range(NHEADS):
                            src = bass.AP(rpb.tensor, rpb.offset + h * 465 + (1 - half + 4) * 31 - 48,
                                          [[1, GRID], [31, 6], [1, GRID]])
                            pool.dma_start(grid_bias[half * GRID:(half + 1) * GRID, h], src).then_inc(sems["rpb_in"], 16)
                    pool.wait_ge(sems["rpb_in"], 16 * 2 * NHEADS)
                    gb = table("grid").unsqueeze(1).to_broadcast([P, NHEADS * 6, GRID])
                    flat = grid_bias.rearrange("p h j c -> p (h j) c")
                    G.tensor_tensor(flat, flat, gb, ALU.add).then_inc(sems["bias_ready"], 1)

            def feed(u):
                for h in range(2):
                    if (u + 2, h) in plan.on_pool:
                        pool.wait_ge(sems["w_hi"], 2 * (u + 2) + h + 1)
                        G.tensor_tensor(half_of(ring_lo, u + 2, h), half_of(ring, u + 2, h),
                                        high_of(u + 2, h).bitcast(F32), ALU.subtract).then_inc(sems["w_lo_pool"], 1)

            pool.dma_start(table("window"), head_rows.partition_broadcast(P)).then_inc(sems["gains_in"], 16)
            pool.wait_ge(sems["gains_in"], 16)
            for l in range(DEPTH):
                T, U, n = plan.tile, plan.unit, LEVELS + 2
                pool.wait_ge(sems["head_in"], 16 * 2)
                for name, units in (("hi", 2), ("hz", 2)):
                    for j in range(units):
                        feed(U[(name, l)] + j)
                for j in range(2):
                    pool.wait_ge(*taken(T[("hz", l)] + j))
                v8 = lambda v: v.rearrange("p t (h d) -> p (t h) d", d=P)
                G.tensor_tensor(v8(hz), v8(hz), head_norm[:, l, 1, :].unsqueeze(1).to_broadcast([P, 8, P]),
                                ALU.mult).then_inc(sems["z_ready"], 1)
                for name, units in (("qkv", 6), ("z", 2)):
                    for j in range(units):
                        feed(U[(name, l)] + j)
                for j in range(2):
                    pool.wait_ge(*taken(T[("hq", l)] + j))
                q = hq.rearrange("p h s -> p (h s)")
                for i in range(n):
                    if i >= 2:
                        pool.wait_ge(*ready(T[("level", l, i - 2)] + 1))
                    if i == LEVELS:
                        G.tensor_copy(hKQ[:, i % 2, 1, :], q).then_inc(sems["hg_q"], 1)
                    else:
                        pool.wait_ge(sems["hg_exp"], (LEVELS + 1) * l + min(i, LEVELS) + 1)
                        G.tensor_tensor(hKQ[:, i % 2, 1, :], q, hE[:, i % 2, 1, :], ALU.mult).then_inc(sems["hg_q"], 1)
                    if i >= 1:
                        feed(U[("gate", l, i - 1)])
                for j in range(2):
                    pool.wait_ge(*taken(T[("z", l)] + j))
                G.tensor_tensor(v8(zs), v8(zs), head_norm[:, l, 0, :].unsqueeze(1).to_broadcast([P, 8, P]),
                                ALU.mult).then_inc(sems["z_ready"], 1)
                for g in range(4):
                    pool.wait_ge(sems["dec"], 4 * l + g + 1)
                    mask = table("le" if g % 2 == 0 else "ge").unsqueeze(1).to_broadcast([P, 4, P])
                    G.tensor_tensor(heads2(qkd[:, g, :]), heads2(dec[:, g, :]), mask, ALU.mult).then_inc(sems["dec_masked"], 1)
                for v in range(LEVELS):
                    for g in range(4):
                        if v == 0:
                            pool.wait_ge(sems["a_ready"], 4 * l + g + 1)
                        elif v == 1:
                            pool.wait_ge(*ready(T[("A0", l)] + g))
                            pool.wait_ge(sems["x_first"], 4 * l + g + 1)
                        else:
                            pool.wait_ge(*ready(T[("Y", l, v - 1)] + g))
                        mask = levels[:, ((g % 2) * LEVELS + v) * P:((g % 2) * LEVELS + v + 1) * P]
                        G.tensor_tensor(heads2(alev[:, g, :]), heads2(amat[:, g, :]),
                                        mask.unsqueeze(1).to_broadcast([P, 4, P]), ALU.mult).then_inc(sems["a_level"], 1)
            pool.wait_ge(sems["ln_xh"], 2 * 12)
            pool.dma_start(f_rows, final_norm.partition_broadcast(P)).then_inc(sems["final_in"], 16)
            pool.wait_ge(sems["final_in"], 16)
            pool.wait_ge(sems["final_rows"], 1)
            pool.dma_start(out.rearrange("b (t p) d -> p (b t) d", p=P), x[:, :, :]).then_inc(sems["out_stored"], 16)




def kernel(**inputs):
    import concourse.bacc as bacc
    from concourse.bass_utils import run_bass_kernel_spmd

    a = {k: np.asarray(v) for k, v in inputs.items()}
    tables = constants()
    arrays = {
        "weights": weight_stream(a),
        "x_in": a["x"],
        "mem_in": a["mem"],
        "consts": np.concatenate([tables[k] for k in CONSTANTS], axis=1),
        "cols": np.concatenate([columns(a["ln_g"].reshape(8, D)), columns(a["ln_b"].reshape(8, D)),
                                columns(np.stack([a["mix_norm_2"], a["ffn_norm_2"]], axis=1).reshape(4, D)),
                                columns(a["dn_conv_2"].reshape(10, 1536)),
                                columns(a["ffn_conv_2"].reshape(6, FF)), columns(a["ffn_conv_bias_2"]),
                                columns(a["hg_lb_logits_2"].reshape(4, 512))
                                ], axis=1),
        "ln_g_rows": a["ln_g"].reshape(8, D),
        "ln_b_rows": a["ln_b"].reshape(8, D),
        "gains": np.concatenate([a["ab_q_gain"], a["ab_k_gain"]], axis=1),
        "sink": a["ab_sink"],
        "rpb": a["c_rpb"][..., ::-1].reshape(-1),
        "hmask_in": hg_masks(),
        "wba_in": a["w_in_2"][:, :, 2048:2064].reshape(DEPTH, KT, P, 16).transpose(2, 0, 1, 3),
        "head_rows": np.stack([a["dn_norm_2"], a["hg_norm_2"]], axis=1).reshape(1, -1),
        "decay_rows": np.stack([a["dn_a_log_2"], a["dn_dt_bias_2"]], axis=1).reshape(1, -1),
        "final_norm": a["final_norm_2"].reshape(1, D),

    }
    nc = bacc.Bacc("TRN2", target_bir_lowering=False, num_devices=1)
    args = []
    for name in arrays:
        arrays[name] = np.ascontiguousarray(arrays[name])
        args.append(nc.dram_tensor(name, arrays[name].shape, mybir.dt.from_np(arrays[name].dtype),
                                   kind="ExternalInput").ap())
    args.append(nc.dram_tensor("out", (1, S, D), F32, kind="ExternalOutput").ap())
    build(nc, *args)
    result = run_bass_kernel_spmd(nc, [arrays], core_ids=[0])
    return result.results[0]["out"]
```
